# Optimizing a Trainium2 kernel written in Bass

```python
import jax, jax.numpy as jnp
from jax import lax
import numpy as np

D_MODEL = 1024
BATCH = 1
SEQ = 512
DEPTH = 1
DEC_BATCH = 8
DEC_SEQ = 8
PAST_LEN = 4096
PAGE_SIZE = 128

M_HEADS = 4
M_DH = 128
M_WIDTH = M_HEADS * M_DH
R_HEADS = 4
R_DH = 128
R_WIDTH = R_HEADS * R_DH
MIX_WIDTH = M_WIDTH + R_WIDTH
CONV_W = 4
CHUNK = 128
ROPE_BASE = 10000.0
IN_SPLITS = (2 * M_WIDTH, M_WIDTH, M_WIDTH, 2 * M_HEADS, R_WIDTH, R_WIDTH, R_WIDTH, R_WIDTH)
D_IN = 4 * M_WIDTH + 2 * M_HEADS + 4 * R_WIDTH
N_EXPERTS = 64
TOP_K = 8
N_GROUPS = 8
TOPK_GROUPS = 4
D_EXPERT = 256
D_SHARED = 256
ROUTED_SCALE = 2.5
MOE_BLOCK = 128
NORM_EPS = 1e-6

kernel_name = 'hymba_mlstm_retention_moe_step'

def rms_norm(x, g):
    x32 = x.astype(jnp.float32)
    y = x32 * lax.rsqrt(jnp.mean(x32 * x32, axis=-1, keepdims=True) + NORM_EPS)
    return (y * g.astype(jnp.float32)).astype(x.dtype)

def head_norm(y, g):
    mu = jnp.mean(y, axis=-1, keepdims=True)
    var = jnp.mean(jnp.square(y - mu), axis=-1, keepdims=True)
    yn = (y - mu) * lax.rsqrt(var + NORM_EPS)
    return yn.reshape(y.shape[:2] + (-1,)) * g.astype(jnp.float32)

def rotary(x, pos):
    half = x.shape[-1] // 2
    freqs = ROPE_BASE ** (-jnp.arange(half, dtype=jnp.float32) / half)
    ang = pos.astype(jnp.float32)[:, None] * freqs[None, :]
    cos = jnp.cos(ang)[None, :, None, :]
    sin = jnp.sin(ang)[None, :, None, :]
    x1, x2 = x[..., :half], x[..., half:]
    return jnp.concatenate([x1 * cos - x2 * sin, x1 * sin + x2 * cos], axis=-1)

def chunked_scan(step, state, seqs):
    L = seqs[0].shape[1]
    cl = CHUNK if L % CHUNK == 0 else L
    nc = L // cl
    xs = tuple(jnp.swapaxes(s.reshape((s.shape[0], nc, cl) + s.shape[2:]), 0, 1) for s in seqs)
    state, ys = lax.scan(step, state, xs)
    ys = jnp.swapaxes(ys, 0, 1)
    return ys.reshape((ys.shape[0], L) + ys.shape[3:]), state

def mlstm_chunk(state, inp):
    C, n, m = state
    q, k, v, logi, logf = inp
    L = q.shape[1]
    b = jnp.cumsum(logf, axis=1)
    a = b + m[:, None, :]
    causal = jnp.tril(jnp.ones((L, L), dtype=bool))[None, :, :, None]
    dmat = jnp.where(causal, b[:, :, None, :] - b[:, None, :, :] + logi[:, None, :, :], -jnp.inf)
    m_t = jnp.maximum(a, jnp.max(dmat, axis=2))
    w_intra = jnp.exp(dmat - m_t[:, :, None, :])
    w_inter = jnp.exp(a - m_t)
    s = jnp.einsum('bihd,bjhd->bijh', q, k) * w_intra
    num = jnp.einsum('bijh,bjhe->bihe', s, v) + w_inter[..., None] * jnp.einsum('bihd,bhde->bihe', q, C)
    den = jnp.sum(s, axis=2) + w_inter * jnp.einsum('bihd,bhd->bih', q, n)
    h = num / jnp.maximum(jnp.abs(den), jnp.exp(-m_t))[..., None]
    m_new = m_t[:, -1]
    w_old = jnp.exp(b[:, -1] + m - m_new)
    w_k = jnp.exp(b[:, -1:] - b + logi - m_new[:, None])
    C_new = w_old[..., None, None] * C + jnp.einsum('bjh,bjhd,bjhe->bhde', w_k, k, v)
    n_new = w_old[..., None] * n + jnp.einsum('bjh,bjhd->bhd', w_k, k)
    return (C_new, n_new, m_new), h

def retention_chunk(S, inp):
    q, k, v = inp
    L = q.shape[1]
    log_g = jnp.log1p(-jnp.exp2(-5.0 - jnp.arange(R_HEADS, dtype=jnp.float32)))
    idx = jnp.arange(L, dtype=jnp.float32)
    rel = idx[:, None] - idx[None, :]
    decay = jnp.where(rel[None] >= 0, jnp.exp(jnp.maximum(rel, 0.0)[None] * log_g[:, None, None]), 0.0)
    scores = jnp.einsum('bihd,bjhd->bhij', q, k) * decay[None]
    y = jnp.einsum('bhij,bjhe->bihe', scores, v)
    inter = jnp.exp((idx[:, None] + 1.0) * log_g[None, :])
    y = y + inter[None, :, :, None] * jnp.einsum('bihd,bhde->bihe', q, S)
    k_w = jnp.exp((L - 1.0 - idx)[:, None] * log_g[None, :])
    S_new = jnp.exp(L * log_g)[None, :, None, None] * S + jnp.einsum('jh,bjhd,bjhe->bhde', k_w, k, v)
    return S_new, y

def mixer(h, pos, state, w_in, b_gates, conv_w, conv_b, m_gn, r_gn, w_out):
    C, n, m, conv_buf, S = [s.astype(jnp.float32) for s in state]
    B, L, _ = h.shape
    z = jnp.einsum('bld,de->ble', h, w_in).astype(jnp.float32)
    offs = np.cumsum(IN_SPLITS)[:-1].tolist()
    qk_pre, mv, mo, gates, rq, rk, rv, rg = jnp.split(z, offs, axis=-1)
    xcat = jnp.concatenate([conv_buf, qk_pre], axis=1)
    cw = conv_w.astype(jnp.float32)
    qk = conv_b.astype(jnp.float32)
    for t in range(CONV_W):
        qk = qk + xcat[:, t:t + L] * cw[t]
    qk = jax.nn.silu(qk)
    new_conv = xcat[:, L:]
    mq, mk = jnp.split(qk, 2, axis=-1)
    mq = mq.reshape(B, L, M_HEADS, M_DH)
    mk = mk.reshape(B, L, M_HEADS, M_DH) * (M_DH ** -0.5)
    mvh = mv.reshape(B, L, M_HEADS, M_DH)
    gates = gates + b_gates.astype(jnp.float32)
    logi = gates[..., :M_HEADS]
    logf = jax.nn.log_sigmoid(gates[..., M_HEADS:])
    h_m, (C, n, m) = chunked_scan(mlstm_chunk, (C, n, m), (mq, mk, mvh, logi, logf))
    out_m = head_norm(h_m, m_gn) * jax.nn.sigmoid(mo)
    rqh = rotary(rq.reshape(B, L, R_HEADS, R_DH), pos)
    rkh = rotary(rk.reshape(B, L, R_HEADS, R_DH), pos) * (R_DH ** -0.5)
    y_r, S = chunked_scan(retention_chunk, S, (rqh, rkh, rv.reshape(B, L, R_HEADS, R_DH)))
    out_r = head_norm(y_r, r_gn) * jax.nn.silu(rg)
    out = jnp.concatenate([out_m, out_r], axis=-1).astype(h.dtype)
    return out @ w_out, (C, n, m, new_conv, S)

def moe(h, w_router, b_router, we_g, we_u, we_d, ws_g, ws_u, ws_d):
    T, D = h.shape
    s = jax.nn.sigmoid(jnp.dot(h, w_router).astype(jnp.float32))
    sb = s + b_router.astype(jnp.float32)
    gsz = N_EXPERTS // N_GROUPS
    gscore = jnp.sum(lax.top_k(sb.reshape(T, N_GROUPS, gsz), 2)[0], axis=-1)
    _, gidx = lax.top_k(gscore, TOPK_GROUPS)
    gmask = jnp.sum(jax.nn.one_hot(gidx, N_GROUPS, dtype=jnp.float32), axis=1)
    emask = jnp.repeat(gmask, gsz, axis=1) > 0
    _, eidx = lax.top_k(jnp.where(emask, sb, -jnp.inf), TOP_K)
    wts = jnp.take_along_axis(s, eidx, axis=1)
    wts = wts / jnp.sum(wts, axis=-1, keepdims=True) * ROUTED_SCALE
    A = T * TOP_K
    flat_e = eidx.reshape(A)
    flat_t = jnp.repeat(jnp.arange(T, dtype=jnp.int32), TOP_K)
    flat_w = wts.reshape(A)
    order = jnp.argsort(flat_e)
    se = flat_e[order]
    counts = jnp.bincount(flat_e, length=N_EXPERTS)
    padded = (counts + MOE_BLOCK - 1) // MOE_BLOCK * MOE_BLOCK
    pend = jnp.cumsum(padded)
    dest = (pend - padded)[se] + jnp.arange(A) - (jnp.cumsum(counts) - counts)[se]
    nb = -(-A // MOE_BLOCK) + N_EXPERTS
    buf_t = jnp.zeros((nb * MOE_BLOCK,), jnp.int32).at[dest].set(flat_t[order])
    buf_w = jnp.zeros((nb * MOE_BLOCK,), jnp.float32).at[dest].set(flat_w[order])
    block_e = jnp.minimum(jnp.searchsorted(pend, jnp.arange(nb) * MOE_BLOCK, side='right'), N_EXPERTS - 1)

    def step(acc, blk):
        e, tok, wt = blk
        xb = h[tok]
        hb = jax.nn.silu(xb @ we_g[e]) * (xb @ we_u[e])
        return acc.at[tok].add(wt[:, None] * (hb @ we_d[e]).astype(jnp.float32)), None

    routed, _ = lax.scan(step, jnp.zeros((T, D), jnp.float32),
                         (block_e, buf_t.reshape(nb, MOE_BLOCK), buf_w.reshape(nb, MOE_BLOCK)))
    shared = (jax.nn.silu(h @ ws_g) * (h @ ws_u)) @ ws_d
    return (routed + shared.astype(jnp.float32)).astype(h.dtype)

def block(x, c, pos, state, lp):
    (w_ada, b_ada, g_mix_pre, g_mix_post, g_ffn_pre, g_ffn_post, w_in, b_gates,
     conv_w, conv_b, m_gn, r_gn, w_out, w_router, b_router,
     w_exp_gate, w_exp_up, w_exp_down, w_sh_gate, w_sh_up, w_sh_down) = lp
    mod = (jax.nn.silu(c) @ w_ada + b_ada)[:, None, :]
    sh1, sc1, gt1, sh2, sc2, gt2 = jnp.split(mod, 6, axis=-1)
    hm = rms_norm(x, g_mix_pre) * (1.0 + sc1) + sh1
    ym, new_state = mixer(hm, pos, state, w_in, b_gates, conv_w, conv_b, m_gn, r_gn, w_out)
    x = x + gt1 * rms_norm(ym, g_mix_post)
    hf = rms_norm(x, g_ffn_pre) * (1.0 + sc2) + sh2
    B, L, D = hf.shape
    yf = moe(hf.reshape(B * L, D), w_router, b_router, w_exp_gate, w_exp_up, w_exp_down,
             w_sh_gate, w_sh_up, w_sh_down).reshape(B, L, D)
    x = x + gt2 * rms_norm(yf, g_ffn_post)
    return x, new_state

def setup_inputs(seed: int = 0) -> dict:
    key = jax.random.key(seed)
    k = jax.random.split(key, 32)
    f32 = jnp.float32

    def nrm(kk, shape, scale):
        return scale * jax.random.normal(kk, shape, f32)

    def gain(kk, shape):
        return 1.0 + nrm(kk, shape, 0.05)

    E, F, FS, D = N_EXPERTS, D_EXPERT, D_SHARED, D_MODEL
    b_i = nrm(k[29], (DEPTH, M_HEADS), 0.1)
    b_f = jnp.linspace(3.0, 6.0, M_HEADS, dtype=f32)[None, :] + nrm(k[30], (DEPTH, M_HEADS), 0.1)
    return {
        'x_prompt': nrm(k[0], (BATCH, SEQ, D), 1.0),
        'x_sample': nrm(k[1], (DEC_BATCH, DEC_SEQ, D), 1.0),
        'c_prompt': nrm(k[2], (BATCH, D), 1.0),
        'c_sample': nrm(k[3], (DEC_BATCH, D), 1.0),
        'state_mlstm_C': nrm(k[4], (DEPTH, DEC_BATCH, M_HEADS, M_DH, M_DH), 0.2),
        'state_mlstm_n': nrm(k[5], (DEPTH, DEC_BATCH, M_HEADS, M_DH), 0.2),
        'state_mlstm_m': nrm(k[6], (DEPTH, DEC_BATCH, M_HEADS), 1.0),
        'state_mlstm_conv': nrm(k[7], (DEPTH, DEC_BATCH, CONV_W - 1, 2 * M_WIDTH), 1.0),
        'state_ret_S': nrm(k[8], (DEPTH, DEC_BATCH, R_HEADS, R_DH, R_DH), 0.2),
        'w_ada': nrm(k[9], (DEPTH, D, 6 * D), 0.5 * D ** -0.5),
        'b_ada': nrm(k[10], (DEPTH, 6 * D), 0.02),
        'g_mix_pre': gain(k[11], (DEPTH, D)),
        'g_mix_post': gain(k[12], (DEPTH, D)),
        'g_ffn_pre': gain(k[13], (DEPTH, D)),
        'g_ffn_post': gain(k[14], (DEPTH, D)),
        'w_in': nrm(k[15], (DEPTH, D, D_IN), D ** -0.5),
        'b_gates': jnp.concatenate([b_i, b_f], axis=-1),
        'conv_w': nrm(k[16], (DEPTH, CONV_W, 2 * M_WIDTH), CONV_W ** -0.5),
        'conv_b': nrm(k[17], (DEPTH, 2 * M_WIDTH), 0.02),
        'm_gn': gain(k[18], (DEPTH, M_WIDTH)),
        'r_gn': gain(k[19], (DEPTH, R_WIDTH)),
        'w_out': nrm(k[20], (DEPTH, MIX_WIDTH, D), MIX_WIDTH ** -0.5),
        'w_router': nrm(k[21], (DEPTH, D, E), D ** -0.5),
        'b_router': nrm(k[22], (DEPTH, E), 0.01),
        'w_exp_gate': nrm(k[23], (DEPTH, E, D, F), D ** -0.5),
        'w_exp_up': nrm(k[24], (DEPTH, E, D, F), D ** -0.5),
        'w_exp_down': nrm(k[25], (DEPTH, E, F, D), F ** -0.5),
        'w_sh_gate': nrm(k[26], (DEPTH, D, FS), D ** -0.5),
        'w_sh_up': nrm(k[27], (DEPTH, D, FS), D ** -0.5),
        'w_sh_down': nrm(k[28], (DEPTH, FS, D), FS ** -0.5),
    }

def reference(x_prompt, x_sample, c_prompt, c_sample, state_mlstm_C, state_mlstm_n, state_mlstm_m,
              state_mlstm_conv, state_ret_S, w_ada, b_ada, g_mix_pre, g_mix_post, g_ffn_pre, g_ffn_post,
              w_in, b_gates, conv_w, conv_b, m_gn, r_gn, w_out, w_router, b_router,
              w_exp_gate, w_exp_up, w_exp_down, w_sh_gate, w_sh_up, w_sh_down):
    f32 = jnp.float32
    pos_p = jnp.arange(x_prompt.shape[1], dtype=jnp.int32)
    pos_s = PAST_LEN + jnp.arange(x_sample.shape[1], dtype=jnp.int32)
    hp, hs = x_prompt, x_sample
    bp = x_prompt.shape[0]
    new_p, new_s = [], []
    for l in range(DEPTH):
        lp = (w_ada[l], b_ada[l], g_mix_pre[l], g_mix_post[l], g_ffn_pre[l], g_ffn_post[l], w_in[l], b_gates[l],
              conv_w[l], conv_b[l], m_gn[l], r_gn[l], w_out[l], w_router[l], b_router[l],
              w_exp_gate[l], w_exp_up[l], w_exp_down[l], w_sh_gate[l], w_sh_up[l], w_sh_down[l])
        init = (jnp.zeros((bp, M_HEADS, M_DH, M_DH), f32), jnp.zeros((bp, M_HEADS, M_DH), f32),
                jnp.zeros((bp, M_HEADS), f32), jnp.zeros((bp, CONV_W - 1, 2 * M_WIDTH), f32),
                jnp.zeros((bp, R_HEADS, R_DH, R_DH), f32))
        hp, sp = block(hp, c_prompt, pos_p, init, lp)
        past = (state_mlstm_C[l], state_mlstm_n[l], state_mlstm_m[l], state_mlstm_conv[l], state_ret_S[l])
        hs, ss = block(hs, c_sample, pos_s, past, lp)
        new_p.append(sp)
        new_s.append(ss)
    p_C, p_n, p_m, p_conv, p_S = [jnp.stack([st[i] for st in new_p]) for i in range(5)]
    s_C, s_n, s_m, s_conv, s_S = [jnp.stack([st[i] for st in new_s]) for i in range(5)]
    return (hp, hs, p_C, p_n, p_m, p_conv, p_S, s_C, s_n, s_m, s_conv, s_S)


_drawn_inputs = setup_inputs


def setup_inputs(seed=0):
    import zlib

    import numpy as np

    out = dict(_drawn_inputs(seed))
    spreads = {}
    factors = {'g_ffn_post': 3.825}
    for name, (base, spread) in spreads.items():
        noise = np.random.default_rng([zlib.crc32(name.encode()), seed]).standard_normal(out[name].shape)
        drawn = base * np.exp(spread * noise) if base else spread * noise
        out[name] = __import__('jax').numpy.asarray(drawn.astype(out[name].dtype))
    for name, factor in factors.items():
        out[name] = (out[name] * factor).astype(out[name].dtype)
    return out
```

```python
from contextlib import ExitStack

import concourse.bass as bass
from concourse import mybir

F32 = mybir.dt.float32
U32 = mybir.dt.uint32
I32 = mybir.dt.int32
ALU = mybir.AluOpType
ACT = mybir.ActivationFunctionType
AX = mybir.AxisListType

P = 128
D = 1024
KC = D // P
SEQ = 512
NCH = SEQ // P
NB, LB = 8, 8
NS = NB * LB
T = SEQ + NS
NT = NCH + 1
ROWS = [P] * NCH + [NS]
NCOND = 1 + NB
H = 4
DH = 128
CW = 4
PADP = SEQ + CW - 1
PADS = LB + CW - 1
QW = PADP + NB * PADS
NE = 64
TOPK = 8
NG, GSZ = 8, 8
FE = 256
FJ = FE // P
BLK = 128
OVMAX = T * TOPK // BLK
DEEP = (T + BLK - 1) // BLK
EPS = 1e-6
KSCALE = DH ** -0.5
BIG = 1e30
FAR = 1e6
OOB = 65536.0
MARK = 3e38
ROUTED = 2.5
CONSTS = ["ident", "iota", "tri", "causal", "causal_s", "decay", "decay_s", "cos", "sin", "sel", "bmask",
          "inter", "inter_s", "kw", "kw_s", "seg", "segneg", "tokcol", "dstcol", "gL"]


def carve(region, at, shape, rows=P):
    n = 1
    for s in shape:
        n *= s
    v = region[0:rows, at:at + n]
    if len(shape) == 2:
        v = v.rearrange("p (a b) -> p a b", a=shape[0])
    elif len(shape) == 3:
        v = v.rearrange("p (a b c) -> p a b c", a=shape[0], b=shape[1])
    return v, at + n


def tcols(t):
    return slice(t * P, t * P + ROWS[t])


def build(nc, A, O, K):
    ctx = ExitStack()
    with ctx:
        def sb(name, shape, dt=F32):
            return ctx.enter_context(nc.sbuf_tensor(name, shape, dt))

        def sem(name):
            return ctx.enter_context(nc.semaphore(name))

        mod_d = nc.dram_tensor("mod_rows", [NCOND, 6 * D], F32, kind="Internal").ap()
        h_d = nc.dram_tensor("ffn_in_rows", [T, D], F32, kind="Internal").ap()
        y_d = nc.dram_tensor("expert_out_rows", [T * TOPK, D], F32, kind="Internal").ap()

        x_sb = sb("x_sb", [P, NT, D])
        hT = sb("hT", [P, KC, T])
        cst = {k: sb("c_" + k, list(K[k].shape)) for k in CONSTS}
        ident, iota = cst["ident"], cst["iota"]
        ones = sb("ones", [P, P])
        epsc = sb("epsc", [P, 1])
        pchk = sb("pchk", [P, 1])
        stat = sb("stat", [P, 14, NT])
        hstat = sb("hstat", [P, 6, NT])
        cols = sb("cols", [P, NT, 4, H])
        wold_sb = sb("wold_sb", [P, H, NCH + NB])
        gnT = sb("gnT", [P, 2 * H])
        cwT = sb("cwT", [P, 2 * H, CW])
        cbT = sb("cbT", [P, 2 * H])
        bgate = sb("bgate", [H, 2])
        wgate = sb("wgate", [P, KC, 2 * H])
        GRN = ["li", "fx", "b", "u", "m", "mp"]
        grows = sb("grows", [H, len(GRN), T])
        GR = {n: grows[:, i, :] for i, n in enumerate(GRN)}
        mprev = sb("mprev", [H, NCH + 1])
        m_in = sb("m_in", [H, NB])
        woldr = sb("woldr", [H, NCH + NB])
        cvbuf = sb("cvbuf", [P, 2 * H * NB * (CW - 1)])
        n_in = sb("n_in", [NB * H, DH])
        n_col = sb("n_col", [P, (1 + NB) * H])
        n_out = sb("n_out", [(1 + NB) * H, DH])
        wtab = sb("wtab", [P, 4])
        idxg = sb("idxg", [P, 4], U32)
        idxs = sb("idxs", [P, 4], U32)
        NO = OVMAX + 4
        etab = sb("etab", [P, NO], I32)
        ntab = sb("ntab", [P, 1], I32)
        negoff = sb("negoff", [P, NO])
        ovf = sb("ovf", [P, 2, NE])
        ovs = sb("ovs", [P, 3, NO])

        NM = 34700
        mem = sb("mem", [P, NM])
        ring, at = carve(mem, 0, [2, KC * 512])
        at += 32
        stC, e_ = carve(mem, 0, [NB, H, DH + 1])
        stS, e_ = carve(mem, e_, [NB, H, DH])
        bcB, _ = carve(mem, 0, [3, 2, D])
        assert e_ <= at
        temps0 = at
        wi, at = carve(mem, at, [NCH, P])
        sT, at = carve(mem, at, [NCH, P])
        kwr, at = carve(mem, at, [NCH, P])
        wi_s, at = carve(mem, at, [NS], NS)
        sT_s, at = carve(mem, at, [NS], NS)
        kw_s, at = carve(mem, at, [P], NS)
        kw8, at = carve(mem, at, [NB, P], NS)
        q8, at = carve(mem, at, [NB, NS])
        num_at = at
        num, at = carve(mem, at, [NT, DH + 1])
        yn, at = carve(mem, at, [NT, DH])
        inter_t, at = carve(mem, at, [2, DH + 1])
        bnst, at = carve(mem, at, [NT, 6])
        bnag, at = carve(mem, at, [NT, 2])
        temps1 = at
        hrow, e_ = carve(mem, temps0, [2, D])
        junk, e_ = carve(mem, e_, [D])
        crow, e_ = carve(mem, e_, [D], NCOND)
        cTs, e_ = carve(mem, e_, [KC, 16])
        assert e_ <= temps1
        NCV = (CW - 1) * (1 + NB)
        rowst, e_ = carve(mem, temps0, [T])
        xc, e_ = carve(mem, e_, [2 * H, NCV])
        cv_out, e_ = carve(mem, e_, [D], NCV)
        assert e_ <= num_at
        yrow, e_ = carve(mem, temps0, [D])
        hrow2, e_ = carve(mem, e_, [2, D])
        junk2, e_ = carve(mem, e_, [D])
        assert e_ <= temps1
        v_at = at
        vv, at = carve(mem, at, [NT, 2 * H, DH + 1])
        g4, _ = carve(mem, v_at, [4, D], NCOND)
        gate_at = at
        gate, at = carve(mem, at, [2 * H, T])
        bcA, _ = carve(mem, gate_at, [2, 2, D])
        wo, e_ = carve(mem, v_at, [2 * H, D])
        assert e_ <= at
        qk_at = at
        qk, at = carve(mem, at, [2 * H, QW])
        mod, _ = carve(mem, qk_at, [6, D], NCOND)
        rqk, at = carve(mem, at, [2 * H, T])
        exp_end = at
        prC, at = carve(mem, at, [H, DH + 1])
        prS, at = carve(mem, at, [H, DH])
        acc_at = at
        acc, at = carve(mem, at, [2, T])
        cv_in, _ = carve(mem, acc_at, [D], NB * (CW - 1))
        rotT = acc[:, 0, :]
        assert at <= NM, at

        def yT(h):
            return qk[:, h, 0:T] if h < H else rqk[:, h - H, :]

        W, at = carve(mem, 0, [2, 3 * KC * FE])
        ycomb, _ = carve(mem, 0, [2, TOPK * D])
        wr, at = carve(mem, at, [KC, NE])
        xg, at = carve(mem, at, [2, D])
        Pm, at = carve(mem, at, [2, NT * BLK])
        xT, at = carve(mem, at, [2, KC * BLK])
        at = max(at, 2 * TOPK * D)
        yo, at = carve(mem, at, [2, D])
        R, at = carve(mem, at, [NT, NE, 3])
        hh, at = carve(mem, at, [FE])
        sg, at = carve(mem, at, [FE])
        hhT, at = carve(mem, at, [FJ * BLK])
        shout, at = carve(mem, at, [NT, D])
        bcG, at = carve(mem, at, [2, D])
        smat, at = carve(mem, at, [NT, NE])
        maskm, at = carve(mem, at, [NT, NE])
        pos, at = carve(mem, at, [NT, NE])
        rt, at = carve(mem, at, [6, NE])
        gs12, at = carve(mem, at, [2, 12])
        r8, at = carve(mem, at, [4, 8])
        brow, at = carve(mem, at, [NE])
        assert at <= exp_end, (at, exp_end)
        ocmp, e_ = carve(mem, at, [NO, NE])
        assert e_ <= NM, e_

        ps = [ctx.enter_context(nc.psum_tensor(f"bank{i}", [P, 512], F32)) for i in range(8)]

        names = """ld_const ld_x ld_cond ld_bg ld_small ld_w0 ld_w1 ld_wg sets ld_cv
            c_silu cT_t cT_ready nin_t mod_evac modA mod_st mod_ld1 ss_done rt_done h_ready hT_t hT_ready
            ring_used proj_mm proj_evac cv_pad conv_acc conv_silu st_cv xc_t cvo_ready st_out
            g_ax g_ln g_lf g_t g_exp cols_t cols_ready wold_mm wold_ready rot_done
            ld_stC ld_stS mixA wm wexp kwa stq o1d o2 o2a nchunk so1 so2 so2a s_nc sdb sdu
            nrm_v nrm_s yn_ready yn_t ynT_ready n_cols n_cols_t n_out_ready ld_wo y_mm y_ss y_s2 y_rt x1_done y_ss2
            y_rt2 h2_ready h2T_t h2T_ready h2_st0 h2_st1 ld_bc2 ld_wr rl_mm rl_sig ld_ws ld_bcg ld_br
            msk_ready pos_mm pos_done tab_ready gu_mm gu_silu hh_ready hhT_t hhT_ready dn_mm dn_evac
            P_ready idx_mm idx_ready gat0 gat1 xgT_t xgT_a xgT_d egu egs ehh ehT_t ehT edn eout_a eout_d sct0 sct1
            ld_e0 ld_e1 sctr yl0 yl1 yl_sum yf_ss yf_rt x2_done out_st dch ach pch pool_step""".split()
        S = {n: sem(n) for n in names}
        block = ctx.enter_context(nc.Block())
        w_in = A["w_in"][0].rearrange("(p c) n -> p c n", c=KC)
        w_ada = A["w_ada"][0].rearrange("(p c) n -> p c n", c=KC)
        MW = H * DH
        OG = 4 * MW
        BLOCKS = [("qk0", 0), ("qk1", MW), ("mv", 2 * MW), ("mo", 3 * MW), ("rq", OG + 2 * H),
                  ("rk", OG + 2 * H + MW), ("rv", OG + 2 * H + 2 * MW), ("rg", OG + 2 * H + 3 * MW)]
        NADA = 6 * D // 512
        NBLK = NADA + len(BLOCKS)
        UNITS = []
        for bi, (nm, _) in enumerate(BLOCKS):
            if nm in ("mv", "rv"):
                UNITS += [("tok", nm, bi, t) for t in range(NT)]
            else:
                UNITS += [("chan", nm, bi, c) for c in range(4)]
            if nm == "qk1":
                UNITS += [("gate", "g", bi, 0), ("gate", "g", bi, 1)]
        NU = len(UNITS)
        UEND = {}
        for u, x in enumerate(UNITS):
            UEND[x[1]] = u + 1
        NST = 2 + 1 + NB + 2 + 2

        def wview(j):
            gu = W[:, j, 0:2 * KC * FE].rearrange("p (m c f) -> p m c f", m=2, c=KC)
            dn = W[:, j, 2 * KC * FE:3 * KC * FE].rearrange("p (j d) -> p j d", j=FJ)
            return gu, dn

        def load_expert(sp, j, g, u, d, s):
            gu, dn = wview(j)
            sp.dma_start(gu[:, 0, :, :], g.rearrange("(p c) f -> p c f", c=KC)).then_inc(s, 16)
            sp.dma_start(gu[:, 1, :, :], u.rearrange("(p c) f -> p c f", c=KC)).then_inc(s, 16)
            sp.dma_start(dn, d.rearrange("(j p) d -> p j d", p=P)).then_inc(s, 16)

        def one_expert(name, e):
            return A[name][0, bass.ds(e, 1)].rearrange("a d f -> (a d) f")

        def ladder(eng, body, load_table=True):
            for n in range(4):
                body(n, n, n + 2)
            with eng.Fori(1, NE // 4 - 1) as i:
                for j in range(4):
                    body(4 * i + j, j, 4 * i + j + 2)
            if load_table:
                eng.wait_ge(S["tab_ready"], 1)
            for n in range(NE - 4, NE):
                body(n, n % 4, n + 2)
            nov = eng.value_load(ntab[0:1, 0:1], min_val=0, max_val=OVMAX)
            with eng.Fori(0, OVMAX // 4) as i:
                for j in range(4):
                    with eng.If(4 * i + j < nov):
                        body(4 * i + (NE + j), j, None, 4 * i + j)
            return nov

        def scount(n, j, s=None):
            if isinstance(n, int):
                return 16 * (n // 2 + 1)
            if s is None:
                return (n - j) * 8 + 16 * (j // 2 + 1)
            return (s - j) * 8 + 16 * (NE // 2 + j // 2 + 1)

        def ecount(n, j, s=None):
            if isinstance(n, int):
                return 48 * (n // 2 + 1)
            if s is None:
                return (n - j) * 24 + 48 * (j // 2 + 1)
            return (s - j) * 24 + 48 * (NE // 2 + j // 2 + 1)

        @block.sync
        def _(sp):
            for k in CONSTS:
                dst = cst[k][:, :] if len(K[k].shape) == 2 else cst[k][:, :, :]
                sp.dma_start(dst, K[k]).then_inc(S["ld_const"], 16)
            sp.dma_start(crow[0:1, :], A["c_prompt"]).then_inc(S["ld_cond"], 16)
            sp.dma_start(crow[1:NCOND, :], A["c_sample"]).then_inc(S["ld_cond"], 16)
            sp.dma_start(mod.rearrange("p a b -> p (a b)"), A["b_ada"][0].partition_broadcast(NCOND)).then_inc(S["ld_bg"], 16)
            for i, g in enumerate(["g_mix_pre", "g_mix_post", "g_ffn_pre", "g_ffn_post"]):
                sp.dma_start(g4[:, i, :], A[g][0].partition_broadcast(NCOND)).then_inc(S["ld_bg"], 16)
            sp.dma_start(cv_in, A["state_mlstm_conv"][0].rearrange("b w c -> (b w) c")).then_inc(S["ld_cv"], 16)

            def ring_load(n):
                if 2 <= n < NADA + 2:
                    sp.wait_ge(S["ring_used"], n - 1)
                elif n >= 2:
                    sp.wait_ge(S["proj_mm"], UEND[BLOCKS[n - NADA - 2][0]])
                src = w_ada[:, :, n * 512:(n + 1) * 512] if n < NADA else \
                    w_in[:, :, BLOCKS[n - NADA][1]:BLOCKS[n - NADA][1] + 512]
                dst = ring[:, n % 2, :].rearrange("p (c f) -> p c f", c=KC)
                sp.dma_start(dst, src).then_inc(S[f"ld_w{n % 2}"], 16)

            ring_load(0)
            ring_load(1)
            for t in range(NT):
                src = A["x_prompt"][0, t * P:(t + 1) * P, :] if t < NCH else A["x_sample"].rearrange("b l d -> (b l) d")
                sp.dma_start(x_sb[0:ROWS[t], t, :], src).then_inc(S["ld_x"], 16)
            for n in range(2, NBLK):
                ring_load(n)
            sp.wait_ge(S["proj_mm"], NU)
            for b in range(NB):
                sp.dma_start(stC[:, b, :, 0:DH], A["state_mlstm_C"][0, b].rearrange("h d e -> d h e")).then_inc(S["ld_stC"], 16)
            for b in range(NB):
                sp.dma_start(stS[:, b, :, :], A["state_ret_S"][0, b].rearrange("h d e -> d h e")).then_inc(S["ld_stS"], 16)
            sp.wait_ge(S["ynT_ready"], 4 * H)
            sp.wait_ge(S["sdu"], 2 * NB * H)
            wos = A["w_out"][0].rearrange("(c p) n -> p c n", p=P)
            for hf in range(2):
                sp.dma_start(wo[:, :, hf * 512:(hf + 1) * 512], wos[:, :, hf * 512:(hf + 1) * 512]).then_inc(S["ld_wo"], 16)
            sp.wait_ge(S["h2T_t"], NT)
            sp.wait_ge(S["h2_st0"], 16 * ((NT + 1) // 2))
            sp.wait_ge(S["h2_st1"], 16 * (NT // 2))
            sp.wait_ge(S["st_out"], 16 * NST)
            sp.dma_start(wr, A["w_router"][0].rearrange("(p c) n -> p c n", c=KC)).then_inc(S["ld_wr"], 16)
            sp.dma_start(brow, A["b_router"][0].partition_broadcast(P)).then_inc(S["ld_br"], 16)
            load_expert(sp, 1, A["w_sh_gate"][0], A["w_sh_up"][0], A["w_sh_down"][0], S["ld_ws"])

            def body(n, j, ahead, s=None):
                if not (isinstance(n, int) and n < 2):
                    sp.wait_ge(S["edn"], n - 1)
                if isinstance(n, int) and n == 1:
                    sp.wait_ge(S["dn_mm"], NT)
                e = n if s is None else sp.value_load(etab[0:1, bass.ds(s, 1)], min_val=0, max_val=NE - 1)
                load_expert(sp, j % 2, one_expert("w_exp_gate", e), one_expert("w_exp_up", e),
                            one_expert("w_exp_down", e), S[f"ld_e{j % 2}"])

            ladder(sp, body)
            sp.wait_ge(S["sctr"], 1)
            yv = y_d.rearrange("(t k) d -> t (k d)", k=TOPK)
            for t in range(NT):
                if t >= 2:
                    sp.wait_ge(S["yl_sum"], t - 1)
                sp.dma_start(ycomb[0:ROWS[t], t % 2, :], yv[t * P:t * P + ROWS[t], :]).then_inc(S[f"yl{t % 2}"], 16)
            for t in range(NT):
                sp.wait_ge(S["x2_done"], t + 1)
                dst = O[0][0, t * P:(t + 1) * P, :] if t < NCH else O[1].rearrange("b l d -> (b l) d")
                sp.dma_start(dst, x_sb[0:ROWS[t], t, :]).then_inc(S["out_st"], 16)
            sp.wait_ge(S["st_cv"], 32)
            sp.wait_ge(S["out_st"], 16 * NT)

        def spread(pool, dst, part, s):
            src = mod_d[:, part * D:(part + 1) * D]
            pool.dma_start(dst[:, 0, :], src[0].partition_broadcast(P)).then_inc(s, 16)
            for b in range(NB):
                pool.dma_start(dst[b * LB:(b + 1) * LB, 1, :], src[1 + b].partition_broadcast(LB)).then_inc(s, 16)

        SPREAD = 16 * (1 + NB)

        @block.gpsimd
        def _(pool):
            pool.memset(ones[:, :], 1.0).then_inc(S["sets"], 1)
            pool.memset(epsc[:, :], EPS).then_inc(S["sets"], 1)
            pool.dma_start(n_in[:, :], A["state_mlstm_n"][0].rearrange("b h d -> (b h) d")).then_inc(S["ld_small"], 16)
            with nc.allow_non_contiguous_dma("a few short columns"):
                pool.dma_start(m_in[:, :], A["state_mlstm_m"][0].rearrange("b h -> h b")).then_inc(S["ld_small"], 16)
                pool.dma_start(gnT[:, 0:H], A["m_gn"][0].rearrange("(h p) -> p h", p=P)).then_inc(S["ld_small"], 16)
                pool.dma_start(gnT[:, H:2 * H], A["r_gn"][0].rearrange("(h p) -> p h", p=P)).then_inc(S["ld_small"], 16)
                for w in range(CW):
                    pool.dma_start(cwT[:, :, w], A["conv_w"][0, w].rearrange("(c p) -> p c", p=P)).then_inc(S["ld_small"], 16)
                pool.dma_start(cbT[:, :], A["conv_b"][0].rearrange("(c p) -> p c", p=P)).then_inc(S["ld_small"], 16)
                pool.dma_start(bgate[:, :], A["b_gates"][0].rearrange("(k h) -> h k", h=H)).then_inc(S["ld_small"], 16)
                pool.dma_start(wgate[:, :, :], w_in[:, :, OG:OG + 2 * H]).then_inc(S["ld_wg"], 16)
            pool.wait_ge(S["modA"], 1)
            pool.dma_start(mod_d[:, 0:2 * D], mod[:, 0:2, :].rearrange("p a b -> p (a b)")).then_inc(S["mod_st"], 16)
            pool.wait_ge(S["mod_st"], 16)
            spread(pool, bcA[:, 0], 1, S["mod_ld1"])
            spread(pool, bcA[:, 1], 0, S["mod_ld1"])
            pool.wait_ge(S["modA"], 4)
            pool.dma_start(mod_d[:, 2 * D:6 * D], mod[:, 2:6, :].rearrange("p a b -> p (a b)")).then_inc(S["mod_st"], 16)
            pool.wait_ge(S["cvo_ready"], 1)
            pool.dma_start(O[5][0, 0], cv_out[0:CW - 1, :]).then_inc(S["st_cv"], 16)
            pool.dma_start(O[10][0].rearrange("b w c -> (b w) c"), cv_out[CW - 1:NCV, :]).then_inc(S["st_cv"], 16)
            pool.wait_ge(S["g_exp"], 4)
            with nc.allow_non_contiguous_dma("one value per head and sequence"):
                pool.dma_start(O[4][0].rearrange("b h -> h b"), GR["fx"][:, SEQ - 1:SEQ]).then_inc(S["st_out"], 16)
                pool.dma_start(O[9][0].rearrange("b h -> h b"), GR["fx"][:, SEQ + LB - 1::LB]).then_inc(S["st_out"], 16)
            pool.wait_ge(S["sdu"], NB * H)
            pool.wait_ge(S["nchunk"], NCH * H)
            pool.dma_start(O[2][0, 0].rearrange("h d e -> d h e"), prC[:, :, 0:DH]).then_inc(S["st_out"], 16)
            for b in range(NB):
                pool.dma_start(O[7][0, b].rearrange("h d e -> d h e"), stC[:, b, :, 0:DH]).then_inc(S["st_out"], 16)
            pool.wait_ge(S["n_out_ready"], 1)
            pool.dma_start(O[3][0, 0], n_out[0:H, :]).then_inc(S["st_out"], 16)
            pool.dma_start(O[8][0].rearrange("b h d -> (b h) d"), n_out[H:(1 + NB) * H, :]).then_inc(S["st_out"], 16)
            pool.wait_ge(S["sdu"], 2 * NB * H)
            pool.wait_ge(S["nchunk"], NCH * 2 * H)
            pool.dma_start(O[6][0, 0].rearrange("h d e -> d h e"), prS).then_inc(S["st_out"], 16)
            pool.dma_start(O[11][0].rearrange("b h d e -> d (b h) e"), stS.rearrange("p b h e -> p (b h) e")).then_inc(S["st_out"], 16)
            pool.wait_ge(S["mod_st"], 32)
            pool.wait_ge(S["st_out"], 16 * NST)
            for i, part in enumerate((2, 4, 3)):
                spread(pool, bcB[:, i], part, S["ld_bc2"])
            for t in range(NT):
                pool.wait_ge(S["h2_ready"], t + 1)
                pool.dma_start(h_d[t * P:t * P + ROWS[t], :], hrow2[0:ROWS[t], t % 2, :]).then_inc(S[f"h2_st{t % 2}"], 16)
            pool.wait_ge(S["h2T_t"], NT)
            spread(pool, bcG, 5, S["ld_bcg"])
            pool.memset(xg, 0.0).then_inc(S["pch"], 1)
            pool.wait_ge(S["pch"], 1)
            pool.wait_ge(S["h2_st0"], 16 * ((NT + 1) // 2))
            pool.wait_ge(S["h2_st1"], 16 * (NT // 2))

            def gather(j):
                pool.indirect_dma_start(xg[:, j % 2, :], None, h_d[:, :], bass.IndirectOffsetOnAxis(idxg[:, j:j + 1], 0),
                                        bounds_check=T - 1, oob_is_err=False).then_inc(S[f"gat{j % 2}"], 16)

            def body(n, j, ahead, s=None):
                pool.wait_ge(S["idx_ready"], n + 3)
                pool.wait_ge(S["xgT_t"], n + 1)
                pool.sem_inc(S["pool_step"], 1)
                gather((j + 2) % 4)
                pool.wait_ge(S["eout_a"], n + 1)
                pool.wait_ge(S["eout_d"], n + 1)
                pool.sem_inc(S["pool_step"], 1)
                pool.indirect_dma_start(y_d[:, :], bass.IndirectOffsetOnAxis(idxs[:, j:j + 1], 0), yo[:, j % 2, :], None,
                                        bounds_check=T * TOPK - 1, oob_is_err=False).then_inc(S[f"sct{j % 2}"], 16)

            def first(j):
                pool.wait_ge(S["idx_ready"], j + 1)
                gather(j)

            first(0)
            first(1)
            nov = ladder(pool, body)
            pool.wait_ge(S["sct0"], 16 * (NE // 2) + 16 * ((nov + 1) // 2))
            pool.wait_ge(S["sct1"], 16 * (NE // 2) + 16 * (nov // 2))
            pool.tensor_tensor(pchk[:, :], epsc[:, :], epsc[:, :], ALU.add).then_inc(S["sctr"], 1)

        @block.scalar
        def _(act):
            def step(ins):
                step.n += 1
                ins.then_inc(S["ach"], 1)
                act.wait_ge(S["ach"], step.n)
            step.n = 0
            a = act.activation
            act.wait_ge(S["ld_cond"], 32)
            a(crow, crow, ACT.Silu).then_inc(S["c_silu"], 1)
            act.wait_ge(S["ld_x"], 16 * NT)
            act.wait_ge(S["sets"], 2)
            for t in range(NT):
                n = ROWS[t]
                step(a(junk[0:n], x_sb[0:n, t, :], ACT.Square, accum_out=stat[0:n, 0, t:t + 1]))
            for t in range(NT):
                n = ROWS[t]
                a(stat[0:n, 1, t:t + 1], stat[0:n, 0, t:t + 1], ACT.Sqrt, bias=epsc[0:n, :], scale=1.0 / D).then_inc(S["rt_done"], 1)

            def evac_hT(t, s_t, s_ready):
                act.wait_ge(S[s_t], t + 1)
                for k in range(2):
                    n = ROWS[t]
                    src = ps[4 + 2 * (t % 2) + k][:, :].rearrange("p (c q) -> p c q", c=4)[:, :, 0:n]
                    a(hT[:, 4 * k:4 * k + 4, t * P:t * P + n], src, ACT.Copy).then_inc(S[s_ready], 1)

            for t in range(NT):
                evac_hT(t, "hT_t", "hT_ready")
            act.wait_ge(S["mod_st"], 32)
            for u, (kind, nm, bi, c) in enumerate(UNITS):
                act.wait_ge(S["proj_mm"], u + 1)
                A0, A1 = ps[2 * (u % 2)], ps[2 * (u % 2) + 1]
                if kind == "gate":
                    dst = GR["li" if c == 0 else "fx"]
                    act.wait_ge(S["ld_small"], 16 * 10)
                    a(dst[:, 0:SEQ], A0[0:H, :], ACT.Identity, bias=bgate[:, c:c + 1])
                    a(dst[:, SEQ:T], A1[0:H, 0:NS], ACT.Identity, bias=bgate[:, c:c + 1]).then_inc(S["proj_evac"], 1)
                elif kind == "tok":
                    h0 = 0 if nm == "mv" else H
                    n = ROWS[c]
                    a(vv[0:n, c, h0:h0 + H, 0:DH], A0[0:n, :].rearrange("p (h d) -> p h d", h=H), ACT.Copy).then_inc(S["proj_evac"], 1)
                elif nm[:2] == "qk":
                    ch = c + 4 * int(nm[2])
                    a(qk[:, ch, CW - 1:PADP], A0[:, :], ACT.Copy)
                    a(qk[:, ch, PADP:QW].rearrange("p (b l) -> p b l", b=NB)[:, :, CW - 1:PADS],
                      A1[:, 0:NS].rearrange("p (b l) -> p b l", b=NB), ACT.Copy).then_inc(S["proj_evac"], 1)
                else:
                    dst, f = {"mo": (gate[:, c, :], ACT.Sigmoid), "rg": (gate[:, H + c, :], ACT.Silu),
                              "rq": (rqk[:, c, :], ACT.Copy), "rk": (rqk[:, H + c, :], ACT.Copy)}[nm]
                    a(dst[:, 0:SEQ], A0[:, :], f)
                    a(dst[:, SEQ:T], A1[:, 0:NS], f).then_inc(S["proj_evac"], 1)
                if 1 <= u <= 2 * H:
                    act.wait_ge(S["conv_acc"], u)
                    a(qk[:, u - 1, 0:T], acc[:, (u - 1) % 2, :], ACT.Silu).then_inc(S["conv_silu"], 1)
            act.wait_ge(S["g_ax"], 1)
            step(a(GR["u"], GR["u"], ACT.Exp, scale=-1.0))
            a(GR["u"], GR["u"], ACT.Ln, bias=1.0).then_inc(S["g_ln"], 1)
            act.wait_ge(S["g_t"], 1)
            a(woldr[:, 0:NCH], GR["li"][:, P - 1:SEQ:P], ACT.Exp)
            a(woldr[:, NCH:NCH + NB], GR["li"][:, SEQ + LB - 1::LB], ACT.Exp).then_inc(S["g_exp"], 1)
            a(rowst[32:32 + H, :], GR["li"], ACT.Exp).then_inc(S["g_exp"], 1)
            a(rowst[64:64 + H, :], GR["fx"], ACT.Exp, scale=-1.0).then_inc(S["g_exp"], 1)
            a(rowst[96:96 + H, :], GR["b"], ACT.Exp).then_inc(S["g_exp"], 1)
            for k in range(2):
                act.wait_ge(S["xc_t"], 1)
                i = a(cv_out[:, k * 512:(k + 1) * 512], ps[6 + k][0:NCV, :], ACT.Copy)
            i.then_inc(S["cvo_ready"], 1)

            def head_a(h):
                if h < H:
                    act.wait_ge(S["wm"], h + 1)
                    for c in range(NCH):
                        a(wi[:, c, :], wi[:, c, :], ACT.Exp, bias=cols[:, c, 0, h:h + 1], scale=-1.0)
                    a(wi_s, wi_s, ACT.Exp, bias=cols[0:NS, NCH, 0, h:h + 1], scale=-1.0).then_inc(S["wexp"], 1)
                act.wait_ge(S["mixA"], h + 1)
                if h >= 1:
                    act.wait_ge(S["s_nc"], h)
                for c in range(NCH):
                    col = cols[:, c, 3, h:h + 1] if h < H else cst["kw"][:, h - H:h - H + 1]
                    i = a(kwr[:, c, :], ps[2][:, c * P:(c + 1) * P], ACT.Copy, scale=col)
                i.then_inc(S["kwa"], 1)

            def head_c(h):
                w = DH + 1 if h < H else DH
                for c in range(1, NCH):
                    act.wait_ge(S["o2"], h * (NCH - 1) + c)
                    if c >= 2:
                        pass
                    act.wait_ge(S["nchunk"], h * NCH + c)
                    col = cols[:, c, 1, h:h + 1] if h < H else cst["inter"][:, h - H:h - H + 1]
                    a(inter_t[:, c % 2, 0:w], ps[6 + c % 2][:, 0:w], ACT.Copy, scale=col).then_inc(S["o2a"], 1)
                act.wait_ge(S["so2"], h + 1)
                act.wait_ge(S["nchunk"], h * NCH + NCH)
                col = cols[0:NS, NCH, 1, h:h + 1] if h < H else cst["inter_s"][:, h - H:h - H + 1]
                a(inter_t[0:NS, 0, 0:w], ps[6][0:NS, 0:w], ACT.Copy, scale=col).then_inc(S["so2a"], 1)

            act.wait_ge(S["cols_ready"], 1)
            head_a(0)
            for h in range(2 * H):
                head_c(h)
                if h + 1 < 2 * H:
                    head_a(h + 1)
                act.wait_ge(S["nrm_v"], h + 1)
                a(hstat[:, 2, :], hstat[:, 1, :], ACT.Sqrt, bias=epsc[:, :]).then_inc(S["nrm_s"], 1)
            for t in range(NT):
                n = ROWS[t]
                act.wait_ge(S["y_mm"], t + 1)
                step(a(junk2[0:n, 0:512], ps[2 * (t % 2)][0:n, :], ACT.Square, accum_out=stat[0:n, 2, t:t + 1]))
                a(junk2[0:n, 512:D], ps[2 * (t % 2) + 1][0:n, :], ACT.Square, accum_out=stat[0:n, 3, t:t + 1]).then_inc(S["y_ss"], 1)
                act.wait_ge(S["y_s2"], t + 1)
                a(stat[0:n, 5, t:t + 1], stat[0:n, 4, t:t + 1], ACT.Sqrt, bias=epsc[0:n, :], scale=1.0 / D).then_inc(S["y_rt"], 1)
                act.wait_ge(S["x1_done"], t + 1)
                step(a(junk2[0:n], x_sb[0:n, t, :], ACT.Square, accum_out=stat[0:n, 7, t:t + 1]))
                a(stat[0:n, 8, t:t + 1], stat[0:n, 7, t:t + 1], ACT.Sqrt, bias=epsc[0:n, :], scale=1.0 / D).then_inc(S["y_rt2"], 1)
                evac_hT(t, "h2T_t", "h2T_ready")
            for t in range(NT):
                n = ROWS[t]
                act.wait_ge(S["rl_mm"], t + 1)
                a(smat[0:n, t, :], ps[t % 2][0:n, 0:NE], ACT.Sigmoid).then_inc(S["rl_sig"], 1)
            for t in range(NT):
                n = ROWS[t]
                act.wait_ge(S["gu_mm"], t + 1)
                if t >= 1:
                    act.wait_ge(S["hh_ready"], t)
                a(sg[0:n], ps[2][0:n, 0:FE], ACT.Silu).then_inc(S["gu_silu"], 1)
                act.wait_ge(S["hhT_t"], t + 1)
                hv = hhT.rearrange("p (j q) -> p j q", j=FJ)
                pv = ps[3][:, 0:FJ * P].rearrange("p (j q) -> p j q", j=FJ)
                a(hv[:, :, 0:n], pv[:, :, 0:n], ACT.Copy).then_inc(S["hhT_ready"], 1)
                act.wait_ge(S["dn_mm"], t + 1)
                a(shout[0:n, t, 0:512], ps[4][0:n, :], ACT.Copy)
                a(shout[0:n, t, 512:D], ps[5][0:n, :], ACT.Copy).then_inc(S["dn_evac"], 1)

            def xT_evac(n, j, s=None):
                act.wait_ge(S["xgT_t"], n + 1)
                a(xT[:, j % 2, 0:4 * BLK], ps[0][:, :], ACT.Copy).then_inc(S["xgT_a"], 1)

            def body(n, j, ahead, s=None):
                act.wait_ge(S["egu"], n + 1)
                a(sg, ps[2][:, 0:FE], ACT.Silu).then_inc(S["egs"], 1)
                xT_evac(n + 1, j + 1)
                act.wait_ge(S["ehT_t"], n + 1)
                a(hhT, ps[3][:, 0:FJ * BLK], ACT.Copy).then_inc(S["ehT"], 1)
                act.wait_ge(S["edn"], n + 1)
                if not (isinstance(n, int) and n < 2):
                    act.wait_ge(S[f"sct{j % 2}"], scount(n, j, s) - 16)
                a(yo[:, j % 2, 0:512], ps[4][:, :], ACT.Copy).then_inc(S["eout_a"], 1)

            xT_evac(0, 0)
            ladder(act, body)
            for t in range(NT):
                n = ROWS[t]
                act.wait_ge(S["yl_sum"], t + 1)
                step(a(yo[0:n, 1, :], yo[0:n, 0, :], ACT.Square, accum_out=stat[0:n, 10, t:t + 1]))
                a(stat[0:n, 11, t:t + 1], stat[0:n, 10, t:t + 1], ACT.Sqrt, bias=epsc[0:n, :], scale=1.0 / D).then_inc(S["yf_rt"], 1)

        @block.tensor
        def _(pe):
            mm, tr = pe.matmul, pe.transpose
            pe.wait_ge(S["ld_const"], 16 * len(CONSTS))
            pe.wait_ge(S["c_silu"], 1)
            cv = crow.rearrange("p (q c) -> p c q", c=KC)
            for c in range(KC):
                i = tr(ps[7][:, 16 * c:16 * c + NCOND], cv[:, c, :], ident[0:NCOND, 0:NCOND])
            i.then_inc(S["cT_t"], 1)
            pe.wait_ge(S["ld_small"], 160)
            tr(ps[5][:, 0:NB * H], n_in[:, :], ident[0:NB * H, 0:NB * H]).then_inc(S["nin_t"], 1)
            pe.wait_ge(S["ld_cv"], 16)
            for c in range(2 * H):
                i = tr(ps[6][:, 24 * c:24 * c + 24], cv_in[:, c * P:(c + 1) * P], ident[0:24, 0:24])
            i.then_inc(S["nin_t"], 1)

            def ring_wait(n):
                pe.wait_ge(S[f"ld_w{n % 2}"], 16 * (n // 2 + 1))
                return ring[:, n % 2, :].rearrange("p (c f) -> p c f", c=KC)

            pe.wait_ge(S["cT_ready"], 1)
            for g in range(NADA):
                w = ring_wait(g)
                if g >= 2:
                    pe.wait_ge(S["mod_evac"], g - 1)
                for c in range(KC):
                    i = mm(ps[g % 2][0:NCOND, :], cTs[:, c, 0:NCOND], w[:, c, :], start=c == 0, stop=c == KC - 1)
                i.then_inc(S["ring_used"], 1)

            def rows_T(src, t, s_t):
                n = ROWS[t]
                for c in range(KC):
                    i = tr(ps[4 + 2 * (t % 2) + c // 4][:, (c % 4) * P:(c % 4) * P + n], src[0:n, t % 2, c * P:(c + 1) * P],
                           ident[0:n, 0:n])
                i.then_inc(S[s_t], 1)

            pe.wait_ge(S["cv_pad"], 1)
            for t in range(NT):
                pe.wait_ge(S["h_ready"], t + 1)
                if t >= 2:
                    pe.wait_ge(S["hT_ready"], 2 * (t - 1))
                rows_T(hrow, t, "hT_t")
            pe.wait_ge(S["hT_ready"], 2 * NT)
            pe.wait_ge(S["mod_evac"], NADA)
            for u, (kind, nm, bi, c) in enumerate(UNITS):
                w = ring_wait(NADA + bi) if kind != "gate" else None
                A0, A1 = ps[2 * (u % 2)], ps[2 * (u % 2) + 1]
                if u >= 2:
                    pe.wait_ge(S["proj_evac"], u - 1)
                if kind == "tok":
                    n = ROWS[c]
                    for k in range(KC):
                        i = mm(A0[0:n, :], hT[:, k, c * P:c * P + n], w[:, k, :], start=k == 0, stop=k == KC - 1)
                else:
                    if kind == "gate":
                        pe.wait_ge(S["ld_wg"], 16)
                    for k in range(KC):
                        st = w[:, k, c * P:(c + 1) * P] if kind == "chan" else wgate[:, k, c * H:(c + 1) * H]
                        m = P if kind == "chan" else H
                        mm(A0[0:m, :], st, hT[:, k, 0:SEQ], start=k == 0, stop=k == KC - 1)
                        i = mm(A1[0:m, 0:NS], st, hT[:, k, SEQ:T], start=k == 0, stop=k == KC - 1)
                i.then_inc(S["proj_mm"], 1)
            pe.wait_ge(S["proj_evac"], NU)
            pe.wait_ge(S["conv_acc"], 2 * H)
            for c in range(2 * H):
                i = tr(ps[6 + c // 4][0:NCV, (c % 4) * P:(c % 4 + 1) * P], xc[:, c, :], ident[:, :])
            i.then_inc(S["xc_t"], 1)
            pe.wait_ge(S["g_exp"], 4)
            for t in range(NT):
                n = ROWS[t]
                i = tr(ps[4 + t // NCH][0:n, (t % NCH) * P:(t % NCH + 1) * P], rowst[:, t * P:t * P + n], ident[:, :])
            i.then_inc(S["cols_t"], 1)
            for h in range(H):
                i = mm(ps[0][:, 16 * h:16 * h + NCH + NB], cst["sel"][:, h, :], woldr[:, :], start=True, stop=True)
            i.then_inc(S["wold_mm"], 1)

            def QK(h):
                return (qk[:, h, 0:T], qk[:, H + h, 0:T]) if h < H else (rqk[:, h - H, :], rqk[:, h, :])

            def head_a(h):
                q, k = QK(h)
                if h >= 1:
                    pe.wait_ge(S["stq"], h)
                    pe.wait_ge(S["kwa"], h)
                if h == H:
                    pe.wait_ge(S["rot_done"], 2 * H)
                for c in range(NCH):
                    mm(ps[1][:, c * P:(c + 1) * P], k[:, c * P:(c + 1) * P], q[:, c * P:(c + 1) * P], start=True, stop=True)
                mm(ps[3][0:NS, NS:2 * NS], k[:, SEQ:T], q[:, SEQ:T], start=True, stop=True)
                if h < H:
                    mm(ps[3][0:NS, 0:NS], cst["sel"][:, h, 0:NS], GR["m"][:, SEQ:T], start=True, stop=True)
                    mm(ps[0][:, :], cst["sel"][:, h, :], GR["m"][:, 0:SEQ], start=True, stop=True)
                for c in range(NCH):
                    tr(ps[2][:, c * P:(c + 1) * P], k[:, c * P:(c + 1) * P], ident[:, :])
                tr(ps[3][0:NS, P:2 * P], k[:, SEQ:T], ident[:, :]).then_inc(S["mixA"], 1)

            def head_c(h):
                q, k = QK(h)
                w = DH + 1 if h < H else DH
                if h >= 1:
                    pe.wait_ge(S["sdu"], h * NB)
                pe.wait_ge(S["stq"], h + 1)
                pe.wait_ge(S["kwa"], h + 1)
                for c in range(NCH):
                    o1 = ps[4 + c % 2]
                    if c >= 2:
                        pe.wait_ge(S["nchunk"], h * NCH + c - 1)
                    mm(o1[:, 0:w], sT[:, c, :], vv[:, c, h, 0:w], start=True, stop=True)
                    mm(o1[:, 256:256 + w], kwr[:, c, :], vv[:, c, h, 0:w], start=True, stop=True).then_inc(S["o1d"], 1)
                    if c >= 1:
                        pe.wait_ge(S["nchunk"], h * NCH + c)
                        st = prC[:, h, 0:w] if h < H else prS[:, h - H, :]
                        mm(ps[6 + c % 2][:, 0:w], q[:, c * P:(c + 1) * P], st, start=True, stop=True).then_inc(S["o2"], 1)
                if h == 0:
                    pe.wait_ge(S["ld_stC"], 16 * NB)
                    pe.wait_ge(S["n_cols"], 1)
                if h == H:
                    pe.wait_ge(S["ld_stS"], 16 * NB)
                pe.wait_ge(S["nchunk"], h * NCH + NCH)
                mm(ps[4][0:NS, 0:w], sT_s, vv[0:NS, NCH, h, 0:w], start=True, stop=True).then_inc(S["so1"], 1)
                for b in range(NB):
                    st = stC[:, b, h, 0:w] if h < H else stS[:, b, h - H, :]
                    i = mm(ps[6][0:NS, 0:w], q8[:, b, :], st, start=b == 0, stop=b == NB - 1)
                i.then_inc(S["so2"], 1)
                pe.wait_ge(S["s_nc"], h + 1)
                for b in range(NB):
                    if b >= 2:
                        pe.wait_ge(S["sdu"], h * NB + b - 1)
                    mm(ps[4 + b % 2][:, 0:w], kw8[:, b, :], vv[0:NS, NCH, h, 0:w], start=True, stop=True).then_inc(S["sdb"], 1)

            pe.wait_ge(S["cols_ready"], 1)
            head_a(0)
            for h in range(2 * H):
                head_c(h)
                if h == H:
                    pe.wait_ge(S["n_cols"], 2)
                    tr(ps[7][0:(1 + NB) * H, 0:DH], n_col[:, :], ident[:, :]).then_inc(S["n_cols_t"], 1)
                    pe.wait_ge(S["n_out_ready"], 1)
                if h + 1 < 2 * H:
                    head_a(h + 1)
                pe.wait_ge(S["yn_ready"], h + 1)
                for t in range(NT):
                    n = ROWS[t]
                    bk, o = (ps[7], t * P) if t < NCH else (ps[6], 256)
                    i = tr(bk[:, o:o + n], yn[0:n, t, :], ident[0:n, 0:n])
                i.then_inc(S["yn_t"], 1)
                pe.wait_ge(S["ynT_ready"], 2 * (h + 1))

            def y_mm(t):
                n = ROWS[t]
                if t == 0:
                    pe.wait_ge(S["ld_wo"], 32)
                if t >= 2:
                    pe.wait_ge(S["x1_done"], t - 1)
                for hf in range(2):
                    for k in range(2 * H):
                        i = mm(ps[2 * (t % 2) + hf][0:n, :], yT(k)[:, t * P:t * P + n], wo[:, k, hf * 512:(hf + 1) * 512],
                               start=k == 0, stop=k == 2 * H - 1)
                i.then_inc(S["y_mm"], 1)

            y_mm(0)
            for t in range(NT):
                if t + 1 < NT:
                    y_mm(t + 1)
                pe.wait_ge(S["h2_ready"], t + 1)
                if t >= 2:
                    pe.wait_ge(S["h2T_ready"], 2 * (t - 1))
                rows_T(hrow2, t, "h2T_t")
            pe.wait_ge(S["h2T_ready"], 2 * NT)
            pe.wait_ge(S["ld_wr"], 16)
            for t in range(NT):
                n = ROWS[t]
                if t >= 2:
                    pe.wait_ge(S["rl_sig"], t - 1)
                for k in range(KC):
                    i = mm(ps[t % 2][0:n, 0:NE], hT[:, k, t * P:t * P + n], wr[:, k, :], start=k == 0, stop=k == KC - 1)
                i.then_inc(S["rl_mm"], 1)
            pe.wait_ge(S["ld_ws"], 48)
            gu, dn = wview(1)
            for t in range(NT):
                n = ROWS[t]
                if t >= 1:
                    pe.wait_ge(S["hh_ready"], t)
                for k in range(KC):
                    i = mm(ps[2][0:n, :].rearrange("p (m f) -> p m f", m=2), hT[:, k, t * P:t * P + n], gu[:, :, k, :],
                           start=k == 0, stop=k == KC - 1)
                i.then_inc(S["gu_mm"], 1)
                pe.wait_ge(S["hh_ready"], t + 1)
                for jj in range(FJ):
                    i = tr(ps[3][:, jj * P:jj * P + n], hh[0:n, jj * P:(jj + 1) * P], ident[0:n, 0:n])
                i.then_inc(S["hhT_t"], 1)
                pe.wait_ge(S["hhT_ready"], t + 1)
                if t >= 1:
                    pe.wait_ge(S["dn_evac"], t)
                for hf in range(2):
                    for jj in range(FJ):
                        i = mm(ps[4 + hf][0:n, :], hhT[:, jj * P:jj * P + n], dn[:, jj, hf * 512:(hf + 1) * 512],
                               start=jj == 0, stop=jj == FJ - 1)
                i.then_inc(S["dn_mm"], 1)
            for t in range(NT):
                n = ROWS[t]
                pe.wait_ge(S["msk_ready"], t + 1)
                if t >= 1:
                    pe.wait_ge(S["pos_done"], t)
                for tt in range(t):
                    mm(ps[6][0:n, 0:NE], ones[:, 0:n], maskm[:, tt, :], start=tt == 0, stop=False)
                mm(ps[6][0:n, 0:NE], cst["tri"][0:n, 0:n], maskm[0:n, t, :], start=t == 0, stop=True).then_inc(S["pos_mm"], 1)
            for t in range(NT):
                n = ROWS[t]
                i = mm(ps[7][:, 0:NE], ones[0:n, :], maskm[0:n, t, :], start=t == 0, stop=t == NT - 1)
            i.then_inc(S["pos_mm"], 1)
            pe.wait_ge(S["dn_evac"], NT)

            def find_idx(n, j, e):
                pe.wait_ge(S["P_ready"], n + 1)
                if not (isinstance(n, int) and n == 0):
                    pe.wait_ge(S["idx_ready"], n)
                for tt in range(NT):
                    k = ROWS[tt]
                    r = R[0:k, tt, e, :] if isinstance(e, int) else R[0:k, tt, bass.ds(e, 1), :].rearrange("p a b -> p (a b)")
                    i = mm(ps[6][:, 0:3], Pm[0:k, j % 2, tt * BLK:(tt + 1) * BLK], r, start=tt == 0, stop=tt == NT - 1)
                i.then_inc(S["idx_mm"], 1)

            def x_T(n, j, s=None):
                jj = j % 2
                pe.wait_ge(S[f"gat{jj}"], scount(n, j, s))
                if not (isinstance(n, int) and n == 0):
                    pe.wait_ge(S["xgT_a"], n)
                    pe.wait_ge(S["xgT_d"], n)
                for c in range(KC):
                    i = tr(ps[c // 4][:, (c % 4) * BLK:(c % 4 + 1) * BLK], xg[:, jj, c * P:(c + 1) * P], ident[:, :])
                i.then_inc(S["xgT_t"], 1)

            def body(n, j, ahead, s=None):
                jj = j % 2
                gu, dn = wview(jj)
                pe.wait_ge(S["xgT_a"], n + 1)
                pe.wait_ge(S["xgT_d"], n + 1)
                pe.wait_ge(S[f"ld_e{jj}"], ecount(n, j, s))
                if not (isinstance(n, int) and n == 0):
                    pe.wait_ge(S["ehh"], n)
                for c in range(KC):
                    i = mm(ps[2][:, :].rearrange("p (m f) -> p m f", m=2), xT[:, jj, c * BLK:(c + 1) * BLK], gu[:, :, c, :],
                           start=c == 0, stop=c == KC - 1)
                i.then_inc(S["egu"], 1)
                x_T(n + 1, j + 1, s if s is None else s + 1)
                if s is not None:
                    e = pe.value_load(etab[0:1, bass.ds(s + 2, 1)], min_val=0, max_val=NE - 1)
                elif isinstance(ahead, int) and ahead >= NE:
                    e = pe.value_load(etab[0:1, ahead - NE:ahead - NE + 1], min_val=0, max_val=NE - 1)
                else:
                    e = ahead
                find_idx(n + 2, j + 2, e)
                pe.wait_ge(S["ehh"], n + 1)
                for k in range(FJ):
                    i = tr(ps[3][:, k * BLK:(k + 1) * BLK], hh[:, k * P:(k + 1) * P], ident[:, :])
                i.then_inc(S["ehT_t"], 1)
                pe.wait_ge(S["ehT"], n + 1)
                if not (isinstance(n, int) and n == 0):
                    pe.wait_ge(S["eout_a"], n)
                    pe.wait_ge(S["eout_d"], n)
                for hf in range(2):
                    for k in range(FJ):
                        i = mm(ps[4 + hf][:, :], hhT[:, k * BLK:(k + 1) * BLK], dn[:, k, hf * 512:(hf + 1) * 512],
                               start=k == 0, stop=k == FJ - 1)
                i.then_inc(S["edn"], 1)

            find_idx(0, 0, 0)
            find_idx(1, 1, 1)
            x_T(0, 0)
            ladder(pe, body)

        @block.vector
        def _(dve):
            def step(ins):
                step.n += 1
                ins.then_inc(S["dch"], 1)
                dve.wait_ge(S["dch"], step.n)
            step.n = 0
            tt_, ts, stt, cp = dve.tensor_tensor, dve.tensor_scalar, dve.scalar_tensor_tensor, dve.tensor_copy
            dve.wait_ge(S["cT_t"], 1)
            cp(cTs[:, :, 0:NCOND], ps[7][:, 0:16 * KC].rearrange("p (c n) -> p c n", c=KC)[:, :, 0:NCOND]).then_inc(S["cT_ready"], 1)
            dve.wait_ge(S["nin_t"], 2)
            cp(n_col[:, 0:NB * H], ps[5][:, 0:NB * H])
            cp(cvbuf[:, :], ps[6][:, 0:2 * H * 24]).then_inc(S["cv_pad"], 1)
            dve.memset(cols[:, :, :, :], 1.0)
            dve.wait_ge(S["ld_bg"], 16 * 5)
            MODF = mod.rearrange("p a b -> p (a b)")
            for g in range(NADA):
                dve.wait_ge(S["ring_used"], g + 1)
                sl = MODF[:, g * 512:(g + 1) * 512]
                tt_(sl, sl, ps[g % 2][0:NCOND, :], ALU.add).then_inc(S["mod_evac"], 1)
                if g == 3:
                    dve.wait_ge(S["mod_evac"], g + 1)
                    stt(mod[:, 1, :], mod[:, 1, :], 1.0, g4[:, 0, :], ALU.add, ALU.mult).then_inc(S["modA"], 1)
            dve.wait_ge(S["mod_evac"], NADA)
            tt_(mod[:, 2, :], mod[:, 2, :], g4[:, 1, :], ALU.mult).then_inc(S["modA"], 1)
            stt(mod[:, 4, :], mod[:, 4, :], 1.0, g4[:, 2, :], ALU.add, ALU.mult).then_inc(S["modA"], 1)
            tt_(mod[:, 5, :], mod[:, 5, :], g4[:, 3, :], ALU.mult).then_inc(S["modA"], 1)

            def by_chunk(rows):
                return rows.rearrange("p (c q) -> p q c", c=KC)

            dve.wait_ge(S["mod_ld1"], 2 * SPREAD)
            dve.wait_ge(S["rt_done"], NT)
            step(dve.reciprocal(stat[:, 2, 0:NCH], stat[:, 1, 0:NCH]))
            step(dve.reciprocal(stat[0:NS, 2, NCH:NT], stat[0:NS, 1, NCH:NT]))
            for t in range(NT):
                n, o = ROWS[t], int(t == NCH)
                if t >= 1:
                    dve.wait_ge(S["h_ready"], t)
                step(stt(junk[0:n], x_sb[0:n, t, :], stat[0:n, 2, t:t + 1], bcA[0:n, 0, o, :], ALU.mult, ALU.mult))
                if t >= 2:
                    dve.wait_ge(S["hT_t"], t - 1)
                tt_(by_chunk(hrow[0:n, t % 2, :]), junk[0:n].rearrange("p (q c) -> p q c", c=KC),
                    bcA[0:n, 1, o, :].rearrange("p (q c) -> p q c", c=KC), ALU.add).then_inc(S["h_ready"], 1)
            dve.wait_ge(S["mod_st"], 32)
            dve.wait_ge(S["h_ready"], NT)
            step(dve.memset(qk[:, :, 0:CW - 1], 0.0))
            for b in range(NB):
                i = cp(qk[:, :, PADP + b * PADS:PADP + b * PADS + CW - 1],
                       cvbuf[:, :].rearrange("p (c b w) -> p c b w", c=2 * H, b=NB)[:, :, b, :])
            step(i)
            step(dve.memset(vv[:, :, :, DH:DH + 1], 1.0))
            for ch in range(2 * H):
                dve.wait_ge(S["proj_evac"], ch + 1)
                last = QW - NB * PADS
                step(cp(xc[:, ch, 0:CW - 1], qk[:, ch, SEQ:PADP]))
                step(cp(xc[:, ch, CW - 1:NCV].rearrange("p (b w) -> p b w", b=NB),
                        qk[:, ch, PADP:QW].rearrange("p (b l) -> p b l", b=NB)[:, :, LB:PADS]))
                if ch >= 2:
                    dve.wait_ge(S["conv_silu"], ch - 1)
                ap, as_ = acc[:, ch % 2, 0:SEQ], acc[:, ch % 2, SEQ:T].rearrange("p (b l) -> p b l", b=NB)
                qs = qk[:, ch, PADP:QW].rearrange("p (b l) -> p b l", b=NB)
                for w in range(CW):
                    tap = cwT[:, ch, w:w + 1]
                    xp, xs = qk[:, ch, w:w + SEQ], qs[:, :, w:w + LB]
                    if w == 0:
                        ts(ap, xp, tap, cbT[:, ch:ch + 1], ALU.mult, ALU.add)
                        step(ts(as_, xs, tap, cbT[:, ch:ch + 1], ALU.mult, ALU.add))
                    else:
                        stt(ap, xp, tap, ap, ALU.mult, ALU.add)
                        i = stt(as_, xs, tap, as_, ALU.mult, ALU.add)
                        if w < CW - 1:
                            step(i)
                i.then_inc(S["conv_acc"], 1)
            dve.wait_ge(S["proj_evac"], UEND["g"])
            stt(GR["u"], GR["fx"], -1.0, GR["fx"], ALU.mult, ALU.max).then_inc(S["g_ax"], 1)
            dve.wait_ge(S["g_ln"], 1)
            step(ts(GR["fx"], GR["fx"], 0.0, None, ALU.min))
            step(tt_(GR["u"], GR["fx"], GR["u"], ALU.subtract))
            step(dve.tensor_tensor_scan(GR["b"], cst["seg"][:, :], GR["u"], 0.0, ALU.mult, ALU.add))
            step(tt_(GR["u"], GR["li"], GR["b"], ALU.subtract))
            step(dve.memset(mprev[:, :], 0.0))
            for c in range(NCH):
                cs = slice(c * P, (c + 1) * P)
                step(dve.tensor_tensor_scan(GR["m"][:, cs], GR["u"][:, cs], GR["u"][:, cs], mprev[:, c:c + 1], ALU.max, ALU.max))
                step(tt_(mprev[:, c + 1:c + 2], GR["m"][:, c * P + P - 1:c * P + P], GR["b"][:, c * P + P - 1:c * P + P], ALU.add))
            step(cp(GR["mp"][:, SEQ:T], GR["u"][:, SEQ:T]))
            st0 = GR["mp"][:, SEQ::LB]
            dve.wait_ge(S["ld_small"], 160)
            step(tt_(st0, st0, m_in[:, :], ALU.max))
            step(dve.tensor_tensor_scan(GR["m"][:, SEQ:T], cst["segneg"][:, 0:NS], GR["mp"][:, SEQ:T], 0.0, ALU.add, ALU.max))
            step(cp(GR["mp"][:, 0:SEQ].rearrange("p (c l) -> p c l", c=NCH), mprev[:, 0:NCH].unsqueeze(2).to_broadcast([H, NCH, P])))
            step(cp(GR["mp"][:, SEQ:T].rearrange("p (b l) -> p b l", b=NB), m_in[:, :].unsqueeze(2).to_broadcast([H, NB, LB])))
            step(tt_(GR["fx"], GR["b"], GR["m"], ALU.add))
            step(tt_(GR["li"], GR["mp"], GR["m"], ALU.subtract))
            step(tt_(GR["b"][:, 0:SEQ].rearrange("p (c l) -> p c l", c=NCH), GR["u"][:, 0:SEQ].rearrange("p (c l) -> p c l", c=NCH),
                     GR["m"][:, P - 1:SEQ:P].unsqueeze(2).to_broadcast([H, NCH, P]), ALU.subtract))
            step(tt_(GR["b"][:, SEQ:T].rearrange("p (b l) -> p b l", b=NB), GR["u"][:, SEQ:T].rearrange("p (b l) -> p b l", b=NB),
                     GR["m"][:, SEQ + LB - 1::LB].unsqueeze(2).to_broadcast([H, NB, LB]), ALU.subtract))
            dve.wait_ge(S["hT_t"], NT)
            step(dve.memset(rowst, 0.0))
            step(cp(rowst[0:H, :], GR["u"]))
            dve.memset(q8, 0.0).then_inc(S["g_t"], 1)
            dve.memset(num, 0.0)
            step(dve.memset(bnag, 1.0))
            dve.wait_ge(S["conv_silu"], 2 * H)
            for i8 in range(2 * H):
                dve.wait_ge(S["proj_evac"], UEND["rq" if i8 < H else "rk"] - H + i8 % H + 1)
                x = rqk[:, i8, :]
                if i8 >= 1:
                    dve.wait_ge(S["rot_done"], i8)
                HF = P // 2
                tt_(rotT[0:HF], x[HF:P], cst["sin"][HF:P, :], ALU.mult)
                step(tt_(rotT[HF:P], x[0:HF], cst["sin"][0:HF, :], ALU.mult))
                step(tt_(x, x, cst["cos"][:, :], ALU.mult))
                tt_(x, x, rotT, ALU.add).then_inc(S["rot_done"], 1)
            dve.wait_ge(S["ld_stC"], 16 * NB)
            cp(stC[:, :, :, DH], n_col[:, 0:NB * H].rearrange("p (b h) -> p b h", b=NB)).then_inc(S["n_cols"], 1)
            dve.wait_ge(S["cols_t"], 1)
            for t in range(NT):
                n = ROWS[t]
                src = ps[4 + t // NCH][0:n, (t % NCH) * P:(t % NCH + 1) * P].rearrange("p (k r) -> p k r", k=4)[:, :, 0:H]
                i = cp(cols[0:n, t, :, :], src)
            step(i)
            dve.wait_ge(S["wold_mm"], 1)
            step(cp(wold_sb[:, :, :], ps[0][:, 0:16 * H].rearrange("p (h n) -> p h n", h=H)[:, :, 0:NCH + NB]))
            step(ts(cols[:, 0:NCH, 3, :], cols[:, 0:NCH, 3, :], KSCALE, None, ALU.mult))
            ts(cols[0:NS, NCH, 3, :], cols[0:NS, NCH, 3, :], KSCALE, None, ALU.mult).then_inc(S["cols_ready"], 1)

            def head_a(h):
                q, k = (qk[:, h, 0:T], None) if h < H else (rqk[:, h - H, :], None)
                dve.wait_ge(S["mixA"], h + 1)
                S1 = ps[1][:, :].rearrange("p (c l) -> p c l", c=NCH)
                if h < H:
                    tt_(wi, ps[0][:, :].rearrange("p (c l) -> p c l", c=NCH),
                        cst["causal"][:, :].unsqueeze(1).to_broadcast([P, NCH, P]), ALU.add)
                    tt_(wi_s, ps[3][0:NS, 0:NS], cst["causal_s"][:, :], ALU.add).then_inc(S["wm"], 1)
                    dve.wait_ge(S["wexp"], h + 1)
                    stt(sT, S1, KSCALE, wi, ALU.mult, ALU.mult)
                    stt(sT_s, ps[3][0:NS, NS:2 * NS], KSCALE, wi_s, ALU.mult, ALU.mult)
                else:
                    tt_(sT, S1, cst["decay"][:, h - H, :].unsqueeze(1).to_broadcast([P, NCH, P]), ALU.mult)
                    tt_(sT_s, ps[3][0:NS, NS:2 * NS], cst["decay_s"][:, h - H, :], ALU.mult)
                q8d = q8.rearrange("p b m -> p (b m)")
                for b in range(NB):
                    cp(q8[:, b, b * LB:(b + 1) * LB], q[:, SEQ + b * LB:SEQ + (b + 1) * LB])
                col = cols[0:NS, NCH, 3, h:h + 1] if h < H else cst["kw_s"][:, h - H:h - H + 1]
                step(ts(kw_s, ps[3][0:NS, P:2 * P], col, None, ALU.mult))
                tt_(kw8, kw_s.unsqueeze(1).to_broadcast([NS, NB, P]), cst["bmask"][:, :].unsqueeze(2).to_broadcast([NS, NB, P]),
                    ALU.mult).then_inc(S["stq"], 1)

            def head_c(h):
                w = DH + 1 if h < H else DH
                for c in range(NCH):
                    o1 = ps[4 + c % 2]
                    st = prC[:, h, 0:w] if h < H else prS[:, h - H, :]
                    dve.wait_ge(S["o1d"], h * NCH + c + 1)
                    if c == 0:
                        cp(num[:, c, 0:w], o1[:, 0:w])
                        cp(st, o1[:, 256:256 + w]).then_inc(S["nchunk"], 1)
                    else:
                        dve.wait_ge(S["o2a"], h * (NCH - 1) + c)
                        tt_(num[:, c, 0:w], o1[:, 0:w], inter_t[:, c % 2, 0:w], ALU.add)
                        dec = wold_sb[:, h, c:c + 1] if h < H else cst["gL"][:, h - H:h - H + 1]
                        stt(st, st, dec, o1[:, 256:256 + w], ALU.mult, ALU.add).then_inc(S["nchunk"], 1)
                dve.wait_ge(S["so1"], h + 1)
                dve.wait_ge(S["so2a"], h + 1)
                tt_(num[0:NS, NCH, 0:w], ps[4][0:NS, 0:w], inter_t[0:NS, 0, 0:w], ALU.add).then_inc(S["s_nc"], 1)
                for b in range(NB):
                    dve.wait_ge(S["sdb"], h * NB + b + 1)
                    st = stC[:, b, h, 0:w] if h < H else stS[:, b, h - H, :]
                    dec = wold_sb[:, h, NCH + b:NCH + b + 1] if h < H else cst["gL"][:, H + h - H:H + h - H + 1]
                    stt(st, st, dec, ps[4 + b % 2][:, 0:w], ALU.mult, ALU.add).then_inc(S["sdu"], 1)

            def head_norm(h):
                dve.wait_ge(S["s_nc"], h + 1)
                dve.wait_ge(S["nchunk"], (h + 1) * NCH)
                for t in range(NT):
                    n = ROWS[t]
                    i = dve.bn_stats(bnst[0:n, t, :], num[0:n, t, 0:DH])
                step(i)
                for t in range(NT):
                    n = ROWS[t]
                    i = dve.bn_aggr(bnag[0:n, t, :], bnst[0:n, t, :])
                if h < H:
                    step(i)
                    step(stt(hstat[:, 0, :], num[:, :, DH], -1.0, num[:, :, DH], ALU.mult, ALU.max))
                    step(tt_(hstat[:, 0, :], hstat[:, 0, :], cols_em(h), ALU.max))
                    step(dve.reciprocal(hstat[:, 3, :], hstat[:, 0, :]))
                    step(tt_(hstat[:, 4, :], hstat[:, 3, :], hstat[:, 3, :], ALU.mult))
                    if h >= 1:
                        dve.wait_ge(S["nrm_s"], h)
                    tt_(hstat[:, 1, :], bnag[:, :, 1], hstat[:, 4, :], ALU.mult).then_inc(S["nrm_v"], 1)
                else:
                    step(i)
                    cp(hstat[:, 1, :], bnag[:, :, 1]).then_inc(S["nrm_v"], 1)
                dve.wait_ge(S["nrm_s"], h + 1)
                step(dve.reciprocal(hstat[:, 5, :], hstat[:, 2, :]))
                if h < H:
                    step(tt_(hstat[:, 5, :], hstat[:, 5, :], hstat[:, 3, :], ALU.mult))
                for t in range(NT):
                    n = ROWS[t]
                    i = ts(yn[0:n, t, :], num[0:n, t, 0:DH], bnag[0:n, t, 0:1], hstat[0:n, 5, t:t + 1], ALU.subtract, ALU.mult)
                i.then_inc(S["yn_ready"], 1)
                dve.wait_ge(S["yn_t"], h + 1)
                y = yT(h)
                g = gnT[:, h:h + 1]
                stt(y[:, 0:SEQ], ps[7][:, :], g, gate[:, h, 0:SEQ], ALU.mult, ALU.mult).then_inc(S["ynT_ready"], 1)
                stt(y[:, SEQ:T], ps[6][:, 256:256 + NS], g, gate[:, h, SEQ:T], ALU.mult, ALU.mult).then_inc(S["ynT_ready"], 1)

            def cols_em(h):
                return cols[:, :, 2, h]

            dve.wait_ge(S["proj_evac"], NU)
            dve.wait_ge(S["xc_t"], 1)
            dve.wait_ge(S["st_cv"], 32)
            head_a(0)
            for h in range(2 * H):
                head_c(h)
                if h == H - 1:
                    dve.wait_ge(S["sdu"], NB * H)
                    dve.wait_ge(S["nchunk"], NCH * H)
                    cp(n_col[:, 0:H], prC[:, :, DH])
                    cp(n_col[:, H:].rearrange("p (b h) -> p b h", b=NB), stC[:, :, :, DH]).then_inc(S["n_cols"], 1)
                if h == H:
                    dve.wait_ge(S["n_cols_t"], 1)
                    cp(n_out[:, :], ps[7][0:(1 + NB) * H, 0:DH]).then_inc(S["n_out_ready"], 1)
                if h + 1 < 2 * H:
                    head_a(h + 1)
                head_norm(h)
            dve.wait_ge(S["ld_bc2"], 3 * SPREAD)
            for t in range(NT):
                n, o = ROWS[t], int(t == NCH)
                dve.wait_ge(S["y_ss"], t + 1)
                tt_(stat[0:n, 4, t:t + 1], stat[0:n, 2, t:t + 1], stat[0:n, 3, t:t + 1], ALU.add).then_inc(S["y_s2"], 1)
                dve.wait_ge(S["y_rt"], t + 1)
                if t >= 1:
                    dve.wait_ge(S["h2_ready"], t)
                step(dve.reciprocal(stat[0:n, 6, t:t + 1], stat[0:n, 5, t:t + 1]))
                for k in range(2):
                    i = stt(yrow[0:n, k * 512:(k + 1) * 512], ps[2 * (t % 2) + k][0:n, :], stat[0:n, 6, t:t + 1],
                            bcB[0:n, 0, o, k * 512:(k + 1) * 512], ALU.mult, ALU.mult)
                step(i)
                tt_(x_sb[0:n, t, :], x_sb[0:n, t, :], yrow[0:n], ALU.add).then_inc(S["x1_done"], 1)
                dve.wait_ge(S["y_rt2"], t + 1)
                step(dve.reciprocal(stat[0:n, 9, t:t + 1], stat[0:n, 8, t:t + 1]))
                step(stt(yrow[0:n], x_sb[0:n, t, :], stat[0:n, 9, t:t + 1], bcB[0:n, 1, o, :], ALU.mult, ALU.mult))
                if t >= 2:
                    dve.wait_ge(S["h2T_t"], t - 1)
                    dve.wait_ge(S[f"h2_st{t % 2}"], 16 * (t // 2))
                tt_(by_chunk(hrow2[0:n, t % 2, :]), yrow[0:n].rearrange("p (q c) -> p q c", c=KC),
                    bcB[0:n, 2, o, :].rearrange("p (q c) -> p q c", c=KC), ALU.add).then_inc(S["h2_ready"], 1)
            dve.wait_ge(S["ld_br"], 16)
            step(dve.memset(gs12, -MARK))
            step(dve.memset(r8, -MARK))
            for t in range(NT):
                n = ROWS[t]
                dve.wait_ge(S["rl_sig"], t + 1)
                s_, sbias, srt, sel_, cum = smat[0:n, t, :], rt[0:n, 0, :], rt[0:n, 1, :], rt[0:n, 2, :], rt[0:n, 3, :]
                step(tt_(sbias, s_, brow[0:n], ALU.add))
                for g in range(NG):
                    i = dve.max(srt[:, g * GSZ:(g + 1) * GSZ], sbias[:, g * GSZ:(g + 1) * GSZ])
                step(i)
                top = srt.rearrange("p (g k) -> p g k", g=NG)
                gs = gs12[0:n, 0, :]
                step(tt_(gs[:, 0:NG], top[:, :, 0], top[:, :, 1], ALU.add))
                step(dve.max(r8[0:n, 0, :], gs[:, 0:NG]))
                step(cp(r8[0:n, 1, 0:4], r8[0:n, 0, 0:4]))
                step(dve.match_replace(gs12[0:n, 1, :], r8[0:n, 1, :], gs, MARK))
                step(ts(r8[0:n, 2, :], gs12[0:n, 1, 0:NG], MARK, None, ALU.is_equal))
                step(ts(r8[0:n, 3, :], r8[0:n, 2, :], BIG, -BIG, ALU.mult, ALU.add))
                step(tt_(sel_.rearrange("p (g k) -> p g k", g=NG), sbias.rearrange("p (g k) -> p g k", g=NG),
                         r8[0:n, 3, :].unsqueeze(2).to_broadcast([n, NG, GSZ]), ALU.add))
                step(dve.max(r8[0:n, 0, :], sel_))
                step(dve.match_replace(cum, r8[0:n, 0, :], sel_, MARK))
                M = maskm[0:n, t, :]
                ts(M, cum, MARK, None, ALU.is_equal).then_inc(S["msk_ready"], 1)
                dve.wait_ge(S["msk_ready"], t + 1)
                step(tt_(sel_, s_, M, ALU.mult))
                step(dve.tensor_reduce(stat[0:n, 12, t:t + 1], sel_, AX.X, ALU.add))
                step(dve.reciprocal(stat[0:n, 13, t:t + 1], stat[0:n, 12, t:t + 1]))
                Rt = R[0:n, t, :, :]
                ts(Rt[:, :, 1], sel_, stat[0:n, 13, t:t + 1], ROUTED, ALU.mult, ALU.mult)
                step(dve.tensor_tensor_scan(cum, ones[0:n, 0:NE], M, 0.0, ALU.mult, ALU.add))
                ts(Rt[:, :, 2], cum, -1.0, cst["dstcol"][0:n, t:t + 1], ALU.mult, ALU.add)
                step(ts(Rt[:, :, 0], cum, 0.0, cst["tokcol"][0:n, t:t + 1], ALU.mult, ALU.add))
                dve.wait_ge(S["gu_silu"], t + 1)
                if t >= 1:
                    dve.wait_ge(S["hhT_t"], t)
                tt_(hh[0:n], sg[0:n], ps[2][0:n, FE:2 * FE], ALU.mult).then_inc(S["hh_ready"], 1)
            for t in range(NT):
                n = ROWS[t]
                dve.wait_ge(S["pos_mm"], t + 1)
                step(stt(pos[0:n, t, :], ps[6][0:n, 0:NE], FAR, maskm[0:n, t, :], ALU.add, ALU.mult))
                ts(pos[0:n, t, :], pos[0:n, t, :], -FAR, None, ALU.add).then_inc(S["pos_done"], 1)
            dve.wait_ge(S["pos_mm"], NT + 1)
            step(cp(ovf[:, 0, :], ps[7][:, 0:NE]))
            dve.wait_ge(S["pos_done"], NT)

            def table():
                cnt, ob = ovf[:, 0, :], ovf[:, 1, :]
                step(ts(ob, cnt, float(BLK), None, ALU.is_gt))
                for m in range(2, DEEP):
                    step(stt(ob, cnt, float(BLK * m), ob, ALU.is_gt, ALU.add))
                step(dve.tensor_tensor_scan(cnt, ones[:, 0:NE], ob, 0.0, ALU.mult, ALU.add))
                step(cp(ntab[:, :], cnt[:, NE - 1:NE]))
                s_ = iota[:, 0:NO]
                dve.wait_ge(S["st_out"], 16 * NST)
                step(tt_(ocmp, s_.unsqueeze(2).to_broadcast([P, NO, NE]), cnt.unsqueeze(1).to_broadcast([P, NO, NE]), ALU.is_ge))
                step(dve.tensor_reduce(ovs[:, 0, :], ocmp, AX.X, ALU.add))
                step(tt_(ocmp, ocmp, ob.unsqueeze(1).to_broadcast([P, NO, NE]), ALU.mult))
                step(dve.tensor_reduce(ovs[:, 1, :], ocmp, AX.X, ALU.add))
                step(ts(ovs[:, 2, :], ovs[:, 0, :], float(NE), -FAR, ALU.is_ge, ALU.mult))
                step(tt_(ovs[:, 1, :], ovs[:, 1, :], s_, ALU.subtract))
                step(ts(ovs[:, 1, :], ovs[:, 1, :], float(BLK), -float(BLK), ALU.mult, ALU.add))
                step(tt_(negoff[:, :], ovs[:, 1, :], ovs[:, 2, :], ALU.add))
                ts(etab[:, :], ovs[:, 0, :], float(NE - 1), None, ALU.min).then_inc(S["tab_ready"], 1)

            def place(n, j, e, off):
                if not (isinstance(n, int) and n < 2):
                    dve.wait_ge(S["idx_mm"], n - 1)
                for tt in range(NT):
                    k = ROWS[tt]
                    p = pos[0:k, tt, e:e + 1] if isinstance(e, int) else pos[0:k, tt, bass.ds(e, 1)]
                    i = ts(Pm[0:k, j % 2, tt * BLK:(tt + 1) * BLK], iota[0:k, 0:BLK], p,
                           off if isinstance(off, float) else off[0:k], ALU.subtract, ALU.is_equal)
                i.then_inc(S["P_ready"], 1)

            def idx_out(n, j, s=None):
                dve.wait_ge(S["idx_mm"], n + 1)
                q = j % 4
                if not (isinstance(n, int) and n < 4):
                    dve.wait_ge(S[f"sct{j % 2}"], icount(n, j, s))
                ts(idxg[:, q:q + 1], ps[6][:, 0:1], -1.0, OOB, ALU.mult, ALU.add)
                cp(wtab[:, q:q + 1], ps[6][:, 1:2])
                ts(idxs[:, q:q + 1], ps[6][:, 2:3], -1.0, OOB, ALU.mult, ALU.add).then_inc(S["idx_ready"], 1)

            def icount(n, j, s):
                if isinstance(n, int):
                    return 16 * ((n - 4) // 2 + 1)
                if s is None:
                    return (n - j) * 8 + 16 * (j // 2 - 1)
                return (s - j) * 8 + 16 * (NE // 2 + j // 2 - 1)

            def xT_evac(n):
                dve.wait_ge(S["xgT_t"], n + 1)

            def body(n, j, ahead, s=None):
                if s is not None:
                    e = dve.value_load(etab[0:1, bass.ds(s + 2, 1)], min_val=0, max_val=NE - 1)
                    off = negoff[:, bass.ds(s + 2, 1)]
                elif isinstance(ahead, int) and ahead >= NE:
                    a_ = ahead - NE
                    e = dve.value_load(etab[0:1, a_:a_ + 1], min_val=0, max_val=NE - 1)
                    off = negoff[:, a_:a_ + 1]
                else:
                    e, off = ahead, 0.0
                place(n + 2, j, e, off)
                dve.wait_ge(S["egs"], n + 1)
                if not (isinstance(n, int) and n == 0):
                    dve.wait_ge(S["ehT_t"], n)
                stt(hh, sg, wtab[:, j:j + 1], ps[2][:, FE:2 * FE], ALU.mult, ALU.mult).then_inc(S["ehh"], 1)
                dve.wait_ge(S["xgT_t"], n + 2)
                cp(xT[:, (j + 1) % 2, 4 * BLK:8 * BLK], ps[1][:, :]).then_inc(S["xgT_d"], 1)
                idx_out(n + 2, j + 2, s if s is None else s + 2)
                if isinstance(n, int) and n == 1:
                    table()
                dve.wait_ge(S["edn"], n + 1)
                if not (isinstance(n, int) and n < 2):
                    dve.wait_ge(S[f"sct{j % 2}"], scount(n, j, s) - 16)
                cp(yo[:, j % 2, 512:D], ps[5][:, :]).then_inc(S["eout_d"], 1)

            for n in range(2):
                place(n, n, n, 0.0)
            for n in range(2):
                idx_out(n, n)
            dve.wait_ge(S["xgT_t"], 1)
            cp(xT[:, 0, 4 * BLK:8 * BLK], ps[1][:, :]).then_inc(S["xgT_d"], 1)
            dve.wait_ge(S["xgT_d"], 1)
            ladder(dve, body)
            dve.wait_ge(S["ld_bcg"], SPREAD)
            for t in range(NT):
                n, o = ROWS[t], int(t == NCH)
                dve.wait_ge(S[f"yl{t % 2}"], 16 * (t // 2 + 1))
                yc = ycomb[0:n, t % 2, :].rearrange("p (k d) -> p d k", k=TOPK)
                if t >= 1:
                    dve.wait_ge(S["x2_done"], t)
                else:
                    dve.wait_ge(S["sctr"], 1)
                step(dve.tensor_reduce(yo[0:n, 0, :], yc, AX.X, ALU.add))
                tt_(yo[0:n, 0, :], yo[0:n, 0, :], shout[0:n, t, :], ALU.add).then_inc(S["yl_sum"], 1)
                dve.wait_ge(S["yf_rt"], t + 1)
                step(dve.reciprocal(stat[0:n, 12, t:t + 1], stat[0:n, 11, t:t + 1]))
                step(stt(yo[0:n, 0, :], yo[0:n, 0, :], stat[0:n, 12, t:t + 1], bcG[0:n, o, :], ALU.mult, ALU.mult))
                tt_(x_sb[0:n, t, :], x_sb[0:n, t, :], yo[0:n, 0, :], ALU.add).then_inc(S["x2_done"], 1)


def shape_constants():
    import numpy as np
    f = np.float32
    i = np.arange(P)
    k = {"ident": np.eye(P, dtype=f), "iota": np.tile(i.astype(f), (P, 1)), "tri": (i[:, None] < i[None, :]).astype(f)}
    k["causal"] = np.where(i[None, :] >= i[:, None], 0.0, BIG).astype(f)
    s = np.arange(NS)
    same = (s[:, None] // LB == s[None, :] // LB) & (s[None, :] >= s[:, None])
    k["causal_s"] = np.where(same, 0.0, BIG).astype(f)
    lg = np.log1p(-np.exp2(-5.0 - np.arange(H, dtype=f))).astype(f)
    rel = (i[None, :] - i[:, None]).astype(f)
    k["decay"] = np.stack([np.where(rel >= 0, np.exp(np.maximum(rel, 0) * g), 0.0) * KSCALE for g in lg], 1).astype(f)
    rel = (s[None, :] - s[:, None]).astype(f)
    k["decay_s"] = np.stack([np.where(same, np.exp(np.maximum(rel, 0) * g), 0.0) * KSCALE for g in lg], 1).astype(f)
    half = DH // 2
    fr = (f(10000.0) ** (-np.arange(half, dtype=f) / f(half))).astype(f)
    pos = np.concatenate([np.arange(SEQ), 4096 + np.tile(np.arange(LB), NB)]).astype(f)
    ang = (pos[None, :] * fr[:, None]).astype(f).astype(np.float64)
    k["cos"] = np.concatenate([np.cos(ang), np.cos(ang)]).astype(f)
    k["sin"] = np.concatenate([np.sin(ang), -np.sin(ang)]).astype(f)
    sel = np.zeros((H, H, P), f)
    for h in range(H):
        sel[h, h] = 1.0
    k["sel"] = sel
    k["bmask"] = (s[:, None] // LB == np.arange(NB)[None, :]).astype(f)
    k["inter"] = np.exp((i[:, None] + 1.0) * lg[None, :]).astype(f)
    k["inter_s"] = np.exp((s[:, None] % LB + 1.0) * lg[None, :]).astype(f)
    k["kw"] = (np.exp((P - 1.0 - i)[:, None] * lg[None, :]) * KSCALE).astype(f)
    k["kw_s"] = (np.exp((LB - 1.0 - s % LB)[:, None] * lg[None, :]) * KSCALE).astype(f)
    seg = np.ones((H, T), f)
    seg[:, 0:SEQ:P] = 0.0
    seg[:, SEQ::LB] = 0.0
    k["seg"] = seg
    sn = np.zeros((H, NS), f)
    sn[:, ::LB] = -BIG
    k["segneg"] = sn
    tok = (np.arange(NT)[None, :] * P + i[:, None]).astype(f)
    k["tokcol"] = (OOB - tok).astype(f)
    k["dstcol"] = (OOB - TOPK * tok + 1).astype(f)
    k["gL"] = np.tile(np.concatenate([np.exp(P * lg), np.exp(LB * lg)])[None, :], (P, 1)).astype(f)
    return {n: np.ascontiguousarray(v) for n, v in k.items()}


_OUTS = [(1, SEQ, D), (NB, LB, D), (1, 1, H, DH, DH), (1, 1, H, DH), (1, 1, H), (1, 1, CW - 1, D), (1, 1, H, DH, DH),
         (1, NB, H, DH, DH), (1, NB, H, DH), (1, NB, H), (1, NB, CW - 1, D), (1, NB, H, DH, DH)]


def kernel(**inputs):
    import numpy as np
    import concourse.bacc as bacc
    from concourse.bass_utils import run_bass_kernel_spmd

    nc = bacc.Bacc("TRN2", target_bir_lowering=False, num_devices=1)
    arrays, args, consts = {}, {}, {}
    for name, v in inputs.items():
        v = np.ascontiguousarray(v)
        arrays["in_" + name] = v
        args[name] = nc.dram_tensor("in_" + name, v.shape, mybir.dt.from_np(v.dtype), kind="ExternalInput").ap()
    for name, v in shape_constants().items():
        arrays["k_" + name] = v
        consts[name] = nc.dram_tensor("k_" + name, v.shape, F32, kind="ExternalInput").ap()
    outs = [nc.dram_tensor(f"out_{i}", s, F32, kind="ExternalOutput").ap() for i, s in enumerate(_OUTS)]
    build(nc, args, outs, consts)
    r = run_bass_kernel_spmd(nc, [arrays], core_ids=[0])
    return tuple(r.results[0][f"out_{i}"] for i in range(len(_OUTS)))
```

```python
from contextlib import ExitStack

import concourse.bass as bass
from concourse import mybir

F32 = mybir.dt.float32
BF16 = mybir.dt.bfloat16
U32 = mybir.dt.uint32
I32 = mybir.dt.int32
ALU = mybir.AluOpType
ACT = mybir.ActivationFunctionType
AX = mybir.AxisListType

P = 128
D = 1024
KC = D // P
SEQ = 512
NCH = SEQ // P
NB, LB = 8, 8
NS = NB * LB
T = SEQ + NS
NT = NCH + 1
ROWS = [P] * NCH + [NS]
NCOND = 1 + NB
H = 4
DH = 128
CW = 4
PADP = SEQ + CW - 1
PADS = LB + CW - 1
QW = PADP + NB * PADS
NE = 64
TOPK = 8
KPE = 4
NG, GSZ = 8, 8
FE = 256
FJ = FE // P
BLK = 128
OVMAX = T * TOPK // BLK
DEEP = (T + BLK - 1) // BLK
EPS = 1e-6
KSCALE = DH ** -0.5
BIG = 1e30
FAR = 1e6
OOB = 1024
MARK = 3e38
ROUTED = 2.5
CONSTS = ["ident", "iota", "tri", "causal", "causal_s", "decay", "decay_s", "cos", "sin", "sel", "bmask",
          "inter", "inter_s", "kw", "kw_s", "seg", "segneg", "tokcol", "gL"]


def carve(region, at, shape, rows=P, dt=F32):
    n = 1
    for s in shape:
        n *= s
    if dt != F32:
        n //= 2
    v = region[0:rows, at:at + n]
    if dt != F32:
        v = v.bitcast(dt)
    if len(shape) == 2:
        v = v.rearrange("p (a b) -> p a b", a=shape[0])
    elif len(shape) == 3:
        v = v.rearrange("p (a b c) -> p a b c", a=shape[0], b=shape[1])
    return v, at + n


def tcols(t):
    return slice(t * P, t * P + ROWS[t])


def build(nc, A, O, K):
    ctx = ExitStack()
    with ctx:
        def sb(name, shape, dt=F32):
            return ctx.enter_context(nc.sbuf_tensor(name, shape, dt))

        def sem(name):
            return ctx.enter_context(nc.semaphore(name))

        mod_d = nc.dram_tensor("mod_rows", [NCOND, 6 * D], F32, kind="Internal").ap()
        h_d = nc.dram_tensor("ffn_in_rows", [T, D], F32, kind="Internal").ap()
        y_d = nc.dram_tensor("expert_out_rows", [T * TOPK, D], F32, kind="Internal").ap()

        x_sb = sb("x_sb", [P, NT, D])
        hT = sb("hT", [P, KC, T])
        cst = {k: sb("c_" + k, list(K[k].shape)) for k in CONSTS}
        ident, iota = cst["ident"], cst["iota"]
        ones = sb("ones", [P, P])
        epsc = sb("epsc", [P, 1])
        pchk = sb("pchk", [P, 1])
        stat = sb("stat", [P, 14, NT])
        hstat = sb("hstat", [P, 6, NT])
        cols = sb("cols", [P, NT, 4, H])
        wold_sb = sb("wold_sb", [P, H, NCH + NB])
        gnT = sb("gnT", [P, 2 * H])
        cwT = sb("cwT", [P, 2 * H, CW])
        cbT = sb("cbT", [P, 2 * H])
        bgate = sb("bgate", [H, 2])
        wgate = sb("wgate", [P, KC, 2 * H])
        GRN = ["li", "fx", "b", "u", "m", "mp"]
        grows = sb("grows", [H, len(GRN), T])
        GR = {n: grows[:, i, :] for i, n in enumerate(GRN)}
        mprev = sb("mprev", [H, NCH + 1])
        m_in = sb("m_in", [H, NB])
        woldr = sb("woldr", [H, NCH + NB])
        cvbuf = sb("cvbuf", [P, 2 * H * NB * (CW - 1)])
        n_in = sb("n_in", [NB * H, DH])
        n_col = sb("n_col", [P, (1 + NB) * H])
        n_out = sb("n_out", [(1 + NB) * H, DH])
        wtab = sb("wtab", [P, 4])
        idxg = sb("idxg", [P, 4], U32)
        idxs = sb("idxs", [P, 4], U32)
        NO = OVMAX + 4
        etab = sb("etab", [P, NO], I32)
        ntab = sb("ntab", [P, 1], I32)
        negoff = sb("negoff", [P, NO])
        ovf = sb("ovf", [P, 2, NE])
        ovs = sb("ovs", [P, 3, NO])

        NM = 34200
        mem = sb("mem", [P, NM])
        ring, at = carve(mem, 0, [2, KC * 512])
        at += 32
        stC, e_ = carve(mem, 0, [NB, H, DH + 1])
        stS, e_ = carve(mem, e_, [NB, H, DH])
        bcB, _ = carve(mem, 0, [3, 2, D])
        assert e_ <= at
        temps0 = at
        wi, at = carve(mem, at, [NCH, P])
        sT, at = carve(mem, at, [NCH, P])
        kwr, at = carve(mem, at, [NCH, P])
        wi_s, at = carve(mem, at, [NS], NS)
        sT_s, at = carve(mem, at, [NS], NS)
        kw_s, at = carve(mem, at, [P], NS)
        kw8, at = carve(mem, at, [NB, P], NS)
        q8, at = carve(mem, at, [NB, NS])
        num_at = at
        num2, at = carve(mem, at, [2 * NT, DH + 1])
        num_end = at
        yn, at = carve(mem, at, [NT, DH])
        inter_t, at = carve(mem, at, [2, DH + 1])
        bnst, at = carve(mem, at, [NT, 6])
        bnag, at = carve(mem, at, [NT, 2])
        temps1 = at
        hrow, e_ = carve(mem, temps0, [2, D])
        junk, e_ = carve(mem, e_, [D])
        crow, e_ = carve(mem, e_, [D], NCOND)
        cTs, e_ = carve(mem, e_, [KC, 16])
        assert e_ <= temps1
        NCV = (CW - 1) * (1 + NB)
        rowst, e_ = carve(mem, temps0, [T])
        xc, e_ = carve(mem, e_, [2 * H, NCV])
        cv_out, e_ = carve(mem, e_, [D], NCV)
        assert e_ <= num_at
        yrow, e_ = carve(mem, temps0, [D])
        hrow2, e_ = carve(mem, e_, [2, D])
        junk2, e_ = carve(mem, e_, [D])
        assert e_ <= temps1
        v_at = at
        vv, at = carve(mem, at, [NT, 2 * H, DH + 1])
        g4, g4_end = carve(mem, v_at, [4, D], NCOND)
        gate_at = at
        gate, at = carve(mem, at, [2 * H, T])
        bcA, _ = carve(mem, gate_at, [2, 2, D])
        wo, e_ = carve(mem, v_at, [2 * H, D])
        assert e_ <= at
        qk_at = at
        qk, at = carve(mem, at, [2 * H, QW])
        mod, _ = carve(mem, qk_at, [6, D], NCOND)
        rqk, at = carve(mem, at, [2 * H, T])
        exp_end = at
        prC, at = carve(mem, at, [H, DH + 1])
        prS, at = carve(mem, at, [H, DH])
        acc, e_ = carve(mem, num_at, [2, T])
        assert e_ <= num_end
        cv_in, e_ = carve(mem, g4_end, [D], NB * (CW - 1))
        assert e_ <= gate_at
        rotT = acc[:, 0, :]
        assert at <= NM, at

        def yT(h):
            return qk[:, h, 0:T] if h < H else rqk[:, h - H, :]

        W, at = carve(mem, 0, [2, 3 * KC * FE])
        ycomb, _ = carve(mem, 0, [2, TOPK * D])
        wr, at = carve(mem, at, [KC, NE])
        xg, at = carve(mem, at, [2, D])
        Pm, at = carve(mem, at, [2, NT * BLK], dt=BF16)
        xT, at = carve(mem, at, [2, KC * BLK])
        at = max(at, 2 * TOPK * D)
        yo, at = carve(mem, at, [2, D])
        R, at = carve(mem, at, [NT, NE, 8], dt=BF16)
        Re, at = carve(mem, at, [2, NT * 8], dt=BF16)
        hh, at = carve(mem, at, [FE])
        sg, at = carve(mem, at, [FE])
        hhT, at = carve(mem, at, [FJ * BLK])
        shout, at = carve(mem, at, [NT, D])
        bcG, at = carve(mem, at, [2, D])
        smat, at = carve(mem, at, [NT, NE])
        maskm, at = carve(mem, at, [NT, NE])
        pos, at = carve(mem, at, [NT, NE])
        rt, at = carve(mem, at, [6, NE])
        gs12, at = carve(mem, at, [2, 12])
        r8, at = carve(mem, at, [4, 8])
        brow, at = carve(mem, at, [NE])
        assert at <= exp_end, (at, exp_end)
        ocmp, _ = carve(hT[:, :, :].rearrange("p c t -> p (c t)"), 0, [NO, NE])

        ps = [ctx.enter_context(nc.psum_tensor(f"bank{i}", [P, 512], F32)) for i in range(8)]

        names = """ld_id ld_const ld_x ld_cond ld_bg ld_small ld_w0 ld_w1 ld_wg sets ld_cv
            c_silu cT_t cT_ready nin_t mod_evac modA mod_st mod_ld1 ss_done rt_done h_ready hT_t hT_ready
            ring_used proj_mm proj_evac cv_pad conv_acc conv_silu st_cv xc_t cvo_ready st_out
            g_ax g_ln g_lf g_t g_exp cols_t cols_ready rot_done
            ld_stC ld_stS mixA wm wexp kwa stm stq o1d o2 o2a nchunk so1 so2 so2a s_nc sdb sdu
            nrm_v nrm_s yn_ready yn_t ynT_ready n_cols n_cols_t n_out_ready ld_wo y_mm y_ss y_s2 y_rt x1_done y_ss2
            y_rt2 h2_ready h2T_t h2T_ready h2_st0 h2_st1 ld_bc2 ld_wr rl_mm rl_sig ld_ws ld_bcg ld_br
            msk_ready pos_mm pos_done tab_ready gu_mm gu_silu hh_ready hhT_t hhT_ready dn_mm dn_evac
            P_ready idx_mm idx_ready gat0 gat1 xgT_t xgT_a xgT_d egu egs ehh ehT_t ehT edn eout_a eout_d sct0 sct1
            ld_e0 ld_e1 ld_d0 ld_d1 sctr yp_mm yl0 yl1 yl_sum yf_ss yf_rt x2_done out_st dch ach pch pool_step""".split()
        S = {n: sem(n) for n in names}
        block = ctx.enter_context(nc.Block())
        w_in = A["w_in"][0].rearrange("(p c) n -> p c n", c=KC)
        w_ada = A["w_ada"][0].rearrange("(p c) n -> p c n", c=KC)
        MW = H * DH
        OG = 4 * MW
        BLOCKS = [("qk0", 0), ("qk1", MW), ("mv", 2 * MW), ("mo", 3 * MW), ("rq", OG + 2 * H),
                  ("rk", OG + 2 * H + MW), ("rv", OG + 2 * H + 2 * MW), ("rg", OG + 2 * H + 3 * MW)]
        NADA = 6 * D // 512
        NBLK = NADA + len(BLOCKS)
        UNITS = []
        for bi, (nm, _) in enumerate(BLOCKS):
            if nm in ("mv", "rv"):
                UNITS += [("tok", nm, bi, t) for t in range(NT)]
            else:
                UNITS += [("chan", nm, bi, c) for c in range(4)]
            if nm == "qk1":
                UNITS += [("gate", "g", bi, 0), ("gate", "g", bi, 1)]
        NU = len(UNITS)
        UEND = {}
        for u, x in enumerate(UNITS):
            UEND[x[1]] = u + 1
        NST = 2 + 1 + NB + 2 + 2

        def wview(j):
            gu = W[:, j, 0:2 * KC * FE].rearrange("p (m c f) -> p m c f", m=2, c=KC)
            dn = W[:, j, 2 * KC * FE:3 * KC * FE].rearrange("p (j d) -> p j d", j=FJ)
            return gu, dn

        def load_gate_up(sp, j, g, u, s):
            gu, _ = wview(j)
            sp.dma_start(gu[:, 0, :, :], g.rearrange("(p c) f -> p c f", c=KC)).then_inc(s, 16)
            sp.dma_start(gu[:, 1, :, :], u.rearrange("(p c) f -> p c f", c=KC)).then_inc(s, 16)

        def load_down(sp, j, d, s):
            sp.dma_start(wview(j)[1], d.rearrange("(j p) d -> p j d", p=P)).then_inc(s, 16)

        def one_expert(name, e):
            return A[name][0, bass.ds(e, 1)].rearrange("a d f -> (a d) f")

        def ladder(eng, body, load_table=True):
            for n in range(4):
                body(n, n, n + 2)
            with eng.Fori(1, NE // 4 - 1) as i:
                for j in range(4):
                    body(4 * i + j, j, 4 * i + j + 2)
            if load_table:
                eng.wait_ge(S["tab_ready"], 1)
            for n in range(NE - 4, NE):
                body(n, n % 4, n + 2)
            nov = eng.value_load(ntab[0:1, 0:1], min_val=0, max_val=OVMAX)
            with eng.Fori(0, OVMAX // 4) as i:
                with eng.If(4 * i < nov):
                    for j in range(4):
                        with eng.If(4 * i + j < nov):
                            body(4 * i + (NE + j), j, None, 4 * i + j)
            return nov

        def scount(n, j, s=None):
            if isinstance(n, int):
                return 16 * (n // 2 + 1)
            if s is None:
                return (n - j) * 8 + 16 * (j // 2 + 1)
            return (s - j) * 8 + 16 * (NE // 2 + j // 2 + 1)

        def ecount(n, j, s=None):
            if isinstance(n, int):
                return 32 * (n // 2 + 1)
            if s is None:
                return (n - j) * 16 + 32 * (j // 2 + 1)
            return (s - j) * 16 + 32 * (NE // 2 + j // 2 + 1)

        @block.sync
        def _(sp):
            def ring_load(n):
                if 2 <= n < NADA + 2:
                    sp.wait_ge(S["ring_used"], n - 1)
                elif n >= 2:
                    sp.wait_ge(S["proj_mm"], UEND[BLOCKS[n - NADA - 2][0]])
                src = w_ada[:, :, n * 512:(n + 1) * 512] if n < NADA else \
                    w_in[:, :, BLOCKS[n - NADA][1]:BLOCKS[n - NADA][1] + 512]
                dst = ring[:, n % 2, :].rearrange("p (c f) -> p c f", c=KC)
                sp.dma_start(dst, src).then_inc(S[f"ld_w{n % 2}"], 16)

            sp.dma_start(ident[:, :], K["ident"]).then_inc(S["ld_id"], 16)
            sp.dma_start(crow[0:1, :], A["c_prompt"]).then_inc(S["ld_cond"], 16)
            sp.dma_start(crow[1:NCOND, :], A["c_sample"]).then_inc(S["ld_cond"], 16)
            sp.dma_start(mod.rearrange("p a b -> p (a b)"), A["b_ada"][0].partition_broadcast(NCOND)).then_inc(S["ld_bg"], 16)
            ring_load(0)
            ring_load(1)
            for i, g in enumerate(["g_mix_pre", "g_mix_post", "g_ffn_pre", "g_ffn_post"]):
                sp.dma_start(g4[:, i, :], A[g][0].partition_broadcast(NCOND)).then_inc(S["ld_bg"], 16)
            sp.dma_start(cv_in, A["state_mlstm_conv"][0].rearrange("b w c -> (b w) c")).then_inc(S["ld_cv"], 16)

            for t in range(NT):
                src = A["x_prompt"][0, t * P:(t + 1) * P, :] if t < NCH else A["x_sample"].rearrange("b l d -> (b l) d")
                sp.dma_start(x_sb[0:ROWS[t], t, :], src).then_inc(S["ld_x"], 16)
            for k in CONSTS[1:]:
                dst = cst[k][:, :] if len(K[k].shape) == 2 else cst[k][:, :, :]
                sp.dma_start(dst, K[k]).then_inc(S["ld_const"], 16)
            for n in range(2, NBLK):
                ring_load(n)
            sp.wait_ge(S["proj_mm"], NU)
            for b in range(NB):
                sp.dma_start(stC[:, b, :, 0:DH], A["state_mlstm_C"][0, b].rearrange("h d e -> d h e")).then_inc(S["ld_stC"], 16)
            for b in range(NB):
                sp.dma_start(stS[:, b, :, :], A["state_ret_S"][0, b].rearrange("h d e -> d h e")).then_inc(S["ld_stS"], 16)
            sp.wait_ge(S["ynT_ready"], 4 * H)
            sp.wait_ge(S["sdu"], 2 * NB * H)
            wos = A["w_out"][0].rearrange("(c p) n -> p c n", p=P)
            for hf in range(2):
                sp.dma_start(wo[:, :, hf * 512:(hf + 1) * 512], wos[:, :, hf * 512:(hf + 1) * 512]).then_inc(S["ld_wo"], 16)
            sp.wait_ge(S["h2T_t"], NT)
            sp.wait_ge(S["h2_st0"], 16 * ((NT + 1) // 2))
            sp.wait_ge(S["h2_st1"], 16 * (NT // 2))
            sp.wait_ge(S["st_out"], 16 * NST)
            sp.dma_start(wr, A["w_router"][0].rearrange("(p c) n -> p c n", c=KC)).then_inc(S["ld_wr"], 16)
            sp.dma_start(brow, A["b_router"][0].partition_broadcast(P)).then_inc(S["ld_br"], 16)
            load_gate_up(sp, 1, A["w_sh_gate"][0], A["w_sh_up"][0], S["ld_ws"])
            load_down(sp, 1, A["w_sh_down"][0], S["ld_ws"])

            def body(n, j, ahead, s=None):
                if not (isinstance(n, int) and n < 2):
                    sp.wait_ge(S["egu"], n - 1)
                if isinstance(n, int) and n == 1:
                    sp.wait_ge(S["dn_mm"], NT)
                e = n if s is None else sp.value_load(etab[0:1, bass.ds(s, 1)], min_val=0, max_val=NE - 1)
                load_gate_up(sp, j % 2, one_expert("w_exp_gate", e), one_expert("w_exp_up", e), S[f"ld_e{j % 2}"])
                if not (isinstance(n, int) and n < 2):
                    sp.wait_ge(S["edn"], n - 1)
                load_down(sp, j % 2, one_expert("w_exp_down", e), S[f"ld_d{j % 2}"])

            ladder(sp, body)
            sp.wait_ge(S["sctr"], 1)
            yv = y_d.rearrange("(t k) d -> t (k d)", k=TOPK)
            for t in range(NT):
                if t >= 2:
                    sp.wait_ge(S["yl_sum"], t - 1)
                sp.dma_start(ycomb[0:ROWS[t], t % 2, :], yv[t * P:t * P + ROWS[t], :]).then_inc(S[f"yl{t % 2}"], 16)
            for t in range(NT):
                sp.wait_ge(S["x2_done"], t + 1)
                dst = O[0][0, t * P:(t + 1) * P, :] if t < NCH else O[1].rearrange("b l d -> (b l) d")
                sp.dma_start(dst, x_sb[0:ROWS[t], t, :]).then_inc(S["out_st"], 16)
            sp.wait_ge(S["st_cv"], 32)
            sp.wait_ge(S["out_st"], 16 * NT)

        def spread(pool, dst, part, s):
            src = mod_d[:, part * D:(part + 1) * D]
            pool.dma_start(dst[:, 0, :], src[0].partition_broadcast(P)).then_inc(s, 16)
            for b in range(NB):
                pool.dma_start(dst[b * LB:(b + 1) * LB, 1, :], src[1 + b].partition_broadcast(LB)).then_inc(s, 16)

        SPREAD = 16 * (1 + NB)

        @block.gpsimd
        def _(pool):
            pool.memset(ones[:, :], 1.0).then_inc(S["sets"], 1)
            pool.memset(epsc[:, :], EPS).then_inc(S["sets"], 1)
            pool.dma_start(n_in[:, :], A["state_mlstm_n"][0].rearrange("b h d -> (b h) d")).then_inc(S["ld_small"], 16)
            with nc.allow_non_contiguous_dma("a few short columns"):
                pool.dma_start(m_in[:, :], A["state_mlstm_m"][0].rearrange("b h -> h b")).then_inc(S["ld_small"], 16)
                pool.dma_start(gnT[:, 0:H], A["m_gn"][0].rearrange("(h p) -> p h", p=P)).then_inc(S["ld_small"], 16)
                pool.dma_start(gnT[:, H:2 * H], A["r_gn"][0].rearrange("(h p) -> p h", p=P)).then_inc(S["ld_small"], 16)
                for w in range(CW):
                    pool.dma_start(cwT[:, :, w], A["conv_w"][0, w].rearrange("(c p) -> p c", p=P)).then_inc(S["ld_small"], 16)
                pool.dma_start(cbT[:, :], A["conv_b"][0].rearrange("(c p) -> p c", p=P)).then_inc(S["ld_small"], 16)
                pool.dma_start(bgate[:, :], A["b_gates"][0].rearrange("(k h) -> h k", h=H)).then_inc(S["ld_small"], 16)
                pool.dma_start(wgate[:, :, :], w_in[:, :, OG:OG + 2 * H]).then_inc(S["ld_wg"], 16)
            pool.wait_ge(S["modA"], 1)
            pool.dma_start(mod_d[:, 0:2 * D], mod[:, 0:2, :].rearrange("p a b -> p (a b)")).then_inc(S["mod_st"], 16)
            pool.wait_ge(S["mod_st"], 16)
            spread(pool, bcA[:, 0], 1, S["mod_ld1"])
            spread(pool, bcA[:, 1], 0, S["mod_ld1"])
            pool.wait_ge(S["modA"], 4)
            pool.dma_start(mod_d[:, 2 * D:6 * D], mod[:, 2:6, :].rearrange("p a b -> p (a b)")).then_inc(S["mod_st"], 16)
            pool.wait_ge(S["cvo_ready"], 1)
            pool.dma_start(O[5][0, 0], cv_out[0:CW - 1, :]).then_inc(S["st_cv"], 16)
            pool.dma_start(O[10][0].rearrange("b w c -> (b w) c"), cv_out[CW - 1:NCV, :]).then_inc(S["st_cv"], 16)
            pool.wait_ge(S["g_exp"], 4)
            with nc.allow_non_contiguous_dma("one value per head and sequence"):
                pool.dma_start(O[4][0].rearrange("b h -> h b"), GR["fx"][:, SEQ - 1:SEQ]).then_inc(S["st_out"], 16)
                pool.dma_start(O[9][0].rearrange("b h -> h b"), GR["fx"][:, SEQ + LB - 1::LB]).then_inc(S["st_out"], 16)
            pool.wait_ge(S["sdu"], NB * H)
            pool.wait_ge(S["nchunk"], NCH * H)
            pool.dma_start(O[2][0, 0].rearrange("h d e -> d h e"), prC[:, :, 0:DH]).then_inc(S["st_out"], 16)
            for b in range(NB):
                pool.dma_start(O[7][0, b].rearrange("h d e -> d h e"), stC[:, b, :, 0:DH]).then_inc(S["st_out"], 16)
            pool.wait_ge(S["n_out_ready"], 1)
            pool.dma_start(O[3][0, 0], n_out[0:H, :]).then_inc(S["st_out"], 16)
            pool.dma_start(O[8][0].rearrange("b h d -> (b h) d"), n_out[H:(1 + NB) * H, :]).then_inc(S["st_out"], 16)
            pool.wait_ge(S["sdu"], 2 * NB * H)
            pool.wait_ge(S["nchunk"], NCH * 2 * H)
            pool.dma_start(O[6][0, 0].rearrange("h d e -> d h e"), prS).then_inc(S["st_out"], 16)
            pool.dma_start(O[11][0].rearrange("b h d e -> d (b h) e"), stS.rearrange("p b h e -> p (b h) e")).then_inc(S["st_out"], 16)
            pool.wait_ge(S["mod_st"], 32)
            pool.wait_ge(S["st_out"], 16 * NST)
            for i, part in enumerate((2, 4, 3)):
                spread(pool, bcB[:, i], part, S["ld_bc2"])
            for t in range(NT):
                pool.wait_ge(S["h2_ready"], t + 1)
                pool.dma_start(h_d[t * P:t * P + ROWS[t], :], hrow2[0:ROWS[t], t % 2, :]).then_inc(S[f"h2_st{t % 2}"], 16)
            pool.wait_ge(S["h2T_t"], NT)
            spread(pool, bcG, 5, S["ld_bcg"])
            pool.memset(xg, 0.0).then_inc(S["pch"], 1)
            pool.wait_ge(S["pch"], 1)
            pool.wait_ge(S["h2_st0"], 16 * ((NT + 1) // 2))
            pool.wait_ge(S["h2_st1"], 16 * (NT // 2))

            def gather(j):
                pool.indirect_dma_start(xg[:, j % 2, :], None, h_d[:, :], bass.IndirectOffsetOnAxis(idxg[:, j:j + 1], 0),
                                        bounds_check=T - 1, oob_is_err=False).then_inc(S[f"gat{j % 2}"], 16)

            def body(n, j, ahead, s=None):
                pool.wait_ge(S["idx_ready"], n + 3)
                pool.wait_ge(S["xgT_t"], n + 1)
                pool.sem_inc(S["pool_step"], 1)
                gather((j + 2) % 4)
                pool.wait_ge(S["eout_a"], n + 1)
                pool.wait_ge(S["eout_d"], n + 1)
                pool.sem_inc(S["pool_step"], 1)
                pool.indirect_dma_start(y_d[:, :], bass.IndirectOffsetOnAxis(idxs[:, j:j + 1], 0), yo[:, j % 2, :], None,
                                        bounds_check=T * TOPK - 1, oob_is_err=False).then_inc(S[f"sct{j % 2}"], 16)

            def first(j):
                pool.wait_ge(S["idx_ready"], j + 1)
                gather(j)

            first(0)
            first(1)
            nov = ladder(pool, body)
            pool.wait_ge(S["sct0"], 16 * (NE // 2) + 16 * ((nov + 1) // 2))
            pool.wait_ge(S["sct1"], 16 * (NE // 2) + 16 * (nov // 2))
            pool.tensor_tensor(pchk[:, :], epsc[:, :], epsc[:, :], ALU.add).then_inc(S["sctr"], 1)

        @block.scalar
        def _(act):
            def step(ins):
                step.n += 1
                ins.then_inc(S["ach"], 1)
                act.wait_ge(S["ach"], step.n)
            step.n = 0
            a = act.activation
            act.wait_ge(S["ld_cond"], 32)
            a(crow, crow, ACT.Silu).then_inc(S["c_silu"], 1)
            act.wait_ge(S["ld_x"], 16 * NT)
            act.wait_ge(S["sets"], 2)
            for t in range(NT):
                n = ROWS[t]
                step(a(junk[0:n], x_sb[0:n, t, :], ACT.Square, accum_out=stat[0:n, 0, t:t + 1]))
            for t in range(NT):
                n = ROWS[t]
                a(stat[0:n, 1, t:t + 1], stat[0:n, 0, t:t + 1], ACT.Sqrt, bias=epsc[0:n, :], scale=1.0 / D).then_inc(S["rt_done"], 1)

            def evac_hT(t, s_t, s_ready):
                act.wait_ge(S[s_t], t + 1)
                for k in range(2):
                    n = ROWS[t]
                    src = ps[4 + 2 * (t % 2) + k][:, :].rearrange("p (c q) -> p c q", c=4)[:, :, 0:n]
                    a(hT[:, 4 * k:4 * k + 4, t * P:t * P + n], src, ACT.Copy).then_inc(S[s_ready], 1)

            for t in range(NT):
                evac_hT(t, "hT_t", "hT_ready")
            act.wait_ge(S["mod_st"], 32)
            for u, (kind, nm, bi, c) in enumerate(UNITS):
                act.wait_ge(S["proj_mm"], u + 1)
                A0, A1 = ps[2 * (u % 2)], ps[2 * (u % 2) + 1]
                if kind == "gate":
                    dst = GR["li" if c == 0 else "fx"]
                    act.wait_ge(S["ld_small"], 16 * 10)
                    a(dst[:, 0:SEQ], A0[0:H, :], ACT.Identity, bias=bgate[:, c:c + 1])
                    a(dst[:, SEQ:T], A1[0:H, 0:NS], ACT.Identity, bias=bgate[:, c:c + 1]).then_inc(S["proj_evac"], 1)
                elif kind == "tok":
                    h0 = 0 if nm == "mv" else H
                    n = ROWS[c]
                    a(vv[0:n, c, h0:h0 + H, 0:DH], A0[0:n, :].rearrange("p (h d) -> p h d", h=H), ACT.Copy).then_inc(S["proj_evac"], 1)
                elif nm[:2] == "qk":
                    ch = c + 4 * int(nm[2])
                    a(qk[:, ch, CW - 1:PADP], A0[:, :], ACT.Copy)
                    a(qk[:, ch, PADP:QW].rearrange("p (b l) -> p b l", b=NB)[:, :, CW - 1:PADS],
                      A1[:, 0:NS].rearrange("p (b l) -> p b l", b=NB), ACT.Copy).then_inc(S["proj_evac"], 1)
                else:
                    dst, f = {"mo": (gate[:, c, :], ACT.Sigmoid), "rg": (gate[:, H + c, :], ACT.Silu),
                              "rq": (rqk[:, c, :], ACT.Copy), "rk": (rqk[:, H + c, :], ACT.Copy)}[nm]
                    a(dst[:, 0:SEQ], A0[:, :], f)
                    a(dst[:, SEQ:T], A1[:, 0:NS], f).then_inc(S["proj_evac"], 1)
                if 1 <= u <= 2 * H:
                    act.wait_ge(S["conv_acc"], u)
                    a(qk[:, u - 1, 0:T], acc[:, (u - 1) % 2, :], ACT.Silu).then_inc(S["conv_silu"], 1)
                if u == UEND["g"] + 1:
                    act.wait_ge(S["g_ax"], 1)
                    step(a(GR["u"], GR["u"], ACT.Exp, scale=-1.0))
                    a(GR["u"], GR["u"], ACT.Ln, bias=1.0).then_inc(S["g_ln"], 1)
                if u == UEND["mo"]:
                    act.wait_ge(S["g_t"], 1)
                    a(woldr[:, 0:NCH], GR["li"][:, P - 1:SEQ:P], ACT.Exp)
                    a(woldr[:, NCH:NCH + NB], GR["li"][:, SEQ + LB - 1::LB], ACT.Exp).then_inc(S["g_exp"], 1)
                    a(rowst[32:32 + H, :], GR["li"], ACT.Exp).then_inc(S["g_exp"], 1)
                    a(rowst[64:64 + H, :], GR["fx"], ACT.Exp, scale=-1.0).then_inc(S["g_exp"], 1)
                    a(rowst[96:96 + H, :], GR["b"], ACT.Exp).then_inc(S["g_exp"], 1)
                if u == UEND["rk"]:
                    act.wait_ge(S["xc_t"], 1)
                    for k in range(2):
                        i = a(cv_out[:, k * 512:(k + 1) * 512], ps[6 + k][0:NCV, :], ACT.Copy)
                    i.then_inc(S["cvo_ready"], 1)
            def head_a(h):
                if h < H:
                    act.wait_ge(S["wm"], h + 1)
                    for c in range(NCH):
                        a(wi[:, c, :], wi[:, c, :], ACT.Exp, bias=cols[:, c, 0, h:h + 1], scale=-1.0)
                    a(wi_s, wi_s, ACT.Exp, bias=cols[0:NS, NCH, 0, h:h + 1], scale=-1.0).then_inc(S["wexp"], 1)
                act.wait_ge(S["mixA"], h + 1)
                if h >= 1:
                    act.wait_ge(S["s_nc"], h)
                for c in range(NCH):
                    col = cols[:, c, 3, h:h + 1] if h < H else cst["kw"][:, h - H:h - H + 1]
                    i = a(kwr[:, c, :], ps[2][:, c * P:(c + 1) * P], ACT.Copy, scale=col)
                i.then_inc(S["kwa"], 1)

            def root(h):
                act.wait_ge(S["nrm_v"], h + 1)
                a(hstat[:, 2, :], hstat[:, 1, :], ACT.Sqrt, bias=epsc[:, :]).then_inc(S["nrm_s"], 1)

            def head_c(h):
                w = DH + 1 if h < H else DH
                for c in range(1, NCH):
                    act.wait_ge(S["o2"], h * (NCH - 1) + c)
                    act.wait_ge(S["nchunk"], h * NCH + c)
                    col = cols[:, c, 1, h:h + 1] if h < H else cst["inter"][:, h - H:h - H + 1]
                    a(inter_t[:, c % 2, 0:w], ps[6 + c % 2][:, 0:w], ACT.Copy, scale=col).then_inc(S["o2a"], 1)
                    if c == 1 and h >= 1:
                        root(h - 1)
                act.wait_ge(S["so2"], h + 1)
                act.wait_ge(S["nchunk"], h * NCH + NCH)
                col = cols[0:NS, NCH, 1, h:h + 1] if h < H else cst["inter_s"][:, h - H:h - H + 1]
                a(inter_t[0:NS, 0, 0:w], ps[6][0:NS, 0:w], ACT.Copy, scale=col).then_inc(S["so2a"], 1)

            act.wait_ge(S["cols_ready"], 1)
            head_a(0)
            for h in range(2 * H):
                head_c(h)
                if h + 1 < 2 * H:
                    head_a(h + 1)
            root(2 * H - 1)
            for t in range(NT):
                n = ROWS[t]
                act.wait_ge(S["y_mm"], t + 1)
                step(a(junk2[0:n, 0:512], ps[2 * (t % 2)][0:n, :], ACT.Square, accum_out=stat[0:n, 2, t:t + 1]))
                a(junk2[0:n, 512:D], ps[2 * (t % 2) + 1][0:n, :], ACT.Square, accum_out=stat[0:n, 3, t:t + 1]).then_inc(S["y_ss"], 1)
                act.wait_ge(S["y_s2"], t + 1)
                a(stat[0:n, 5, t:t + 1], stat[0:n, 4, t:t + 1], ACT.Sqrt, bias=epsc[0:n, :], scale=1.0 / D).then_inc(S["y_rt"], 1)
                act.wait_ge(S["x1_done"], t + 1)
                step(a(junk2[0:n], x_sb[0:n, t, :], ACT.Square, accum_out=stat[0:n, 7, t:t + 1]))
                a(stat[0:n, 8, t:t + 1], stat[0:n, 7, t:t + 1], ACT.Sqrt, bias=epsc[0:n, :], scale=1.0 / D).then_inc(S["y_rt2"], 1)
                evac_hT(t, "h2T_t", "h2T_ready")
            for t in range(NT):
                n = ROWS[t]
                act.wait_ge(S["rl_mm"], t + 1)
                a(smat[0:n, t, :], ps[t % 2][0:n, 0:NE], ACT.Sigmoid).then_inc(S["rl_sig"], 1)
            for t in range(NT):
                n = ROWS[t]
                act.wait_ge(S["gu_mm"], t + 1)
                if t >= 1:
                    act.wait_ge(S["hh_ready"], t)
                a(sg[0:n], ps[2][0:n, 0:FE], ACT.Silu).then_inc(S["gu_silu"], 1)
                act.wait_ge(S["hhT_t"], t + 1)
                hv = hhT.rearrange("p (j q) -> p j q", j=FJ)
                pv = ps[3][:, 0:FJ * P].rearrange("p (j q) -> p j q", j=FJ)
                a(hv[:, :, 0:n], pv[:, :, 0:n], ACT.Copy).then_inc(S["hhT_ready"], 1)
                act.wait_ge(S["dn_mm"], t + 1)
                a(shout[0:n, t, 0:512], ps[4][0:n, :], ACT.Copy)
                a(shout[0:n, t, 512:D], ps[5][0:n, :], ACT.Copy).then_inc(S["dn_evac"], 1)

            def xT_evac(n, j, s=None):
                act.wait_ge(S["xgT_t"], n + 1)
                a(xT[:, j % 2, 0:4 * BLK], ps[0][:, :], ACT.Copy).then_inc(S["xgT_a"], 1)

            def body(n, j, ahead, s=None):
                act.wait_ge(S["egu"], n + 1)
                a(sg, ps[2][:, 0:FE], ACT.Silu).then_inc(S["egs"], 1)
                for k in range(FJ):
                    act.wait_ge(S["ehT_t"], FJ * n + (k + 1))
                    a(hhT[:, k * BLK:(k + 1) * BLK], ps[3 + 4 * k][:, 0:BLK], ACT.Copy).then_inc(S["ehT"], 1)
                xT_evac(n + 1, j + 1)
                act.wait_ge(S["edn"], n + 1)
                if not (isinstance(n, int) and n < 2):
                    act.wait_ge(S[f"sct{j % 2}"], scount(n, j, s) - 16)
                a(yo[:, j % 2, 0:512], ps[4][:, :], ACT.Copy).then_inc(S["eout_a"], 1)

            xT_evac(0, 0)
            ladder(act, body)
            for t in range(NT):
                n = ROWS[t]
                act.wait_ge(S["yl_sum"], t + 1)
                step(a(yo[0:n, 1, :], yo[0:n, 0, :], ACT.Square, accum_out=stat[0:n, 10, t:t + 1]))
                a(stat[0:n, 11, t:t + 1], stat[0:n, 10, t:t + 1], ACT.Sqrt, bias=epsc[0:n, :], scale=1.0 / D).then_inc(S["yf_rt"], 1)

        @block.tensor
        def _(pe):
            mm, tr = pe.matmul, pe.transpose
            pe.wait_ge(S["ld_id"], 16)
            pe.wait_ge(S["c_silu"], 1)
            cv = crow.rearrange("p (q c) -> p c q", c=KC)
            for c in range(KC):
                i = tr(ps[7][:, 16 * c:16 * c + NCOND], cv[:, c, :], ident[0:NCOND, 0:NCOND])
            i.then_inc(S["cT_t"], 1)
            def ring_wait(n):
                pe.wait_ge(S[f"ld_w{n % 2}"], 16 * (n // 2 + 1))
                return ring[:, n % 2, :].rearrange("p (c f) -> p c f", c=KC)

            pe.wait_ge(S["cT_ready"], 1)
            for g in range(NADA):
                w = ring_wait(g)
                if g >= 2:
                    pe.wait_ge(S["mod_evac"], g - 1)
                for c in range(KC):
                    i = mm(ps[g % 2][0:NCOND, :], cTs[:, c, 0:NCOND], w[:, c, :], start=c == 0, stop=c == KC - 1)
                i.then_inc(S["ring_used"], 1)

            pe.wait_ge(S["ld_const"], 16 * (len(CONSTS) - 1))
            pe.wait_ge(S["ld_small"], 160)
            tr(ps[5][:, 0:NB * H], n_in[:, :], ident[0:NB * H, 0:NB * H]).then_inc(S["nin_t"], 1)
            pe.wait_ge(S["ld_cv"], 16)
            for c in range(2 * H):
                i = tr(ps[6][:, 24 * c:24 * c + 24], cv_in[:, c * P:(c + 1) * P], ident[0:24, 0:24])
            i.then_inc(S["nin_t"], 1)

            def rows_T(src, t, s_t):
                n = ROWS[t]
                for c in range(KC):
                    i = tr(ps[4 + 2 * (t % 2) + c // 4][:, (c % 4) * P:(c % 4) * P + n], src[0:n, t % 2, c * P:(c + 1) * P],
                           ident[0:n, 0:n])
                i.then_inc(S[s_t], 1)

            pe.wait_ge(S["cv_pad"], 1)
            for t in range(NT):
                pe.wait_ge(S["h_ready"], t + 1)
                if t >= 2:
                    pe.wait_ge(S["hT_ready"], 2 * (t - 1))
                rows_T(hrow, t, "hT_t")
            pe.wait_ge(S["hT_ready"], 2 * NT)
            pe.wait_ge(S["mod_evac"], NADA)
            for u, (kind, nm, bi, c) in enumerate(UNITS):
                w = ring_wait(NADA + bi) if kind != "gate" else None
                A0, A1 = ps[2 * (u % 2)], ps[2 * (u % 2) + 1]
                if u >= 2:
                    pe.wait_ge(S["proj_evac"], u - 1)
                if kind == "tok":
                    n = ROWS[c]
                    for k in range(KC):
                        i = mm(A0[0:n, :], hT[:, k, c * P:c * P + n], w[:, k, :], start=k == 0, stop=k == KC - 1)
                else:
                    if kind == "gate":
                        pe.wait_ge(S["ld_wg"], 16)
                    for k in range(KC):
                        st = w[:, k, c * P:(c + 1) * P] if kind == "chan" else wgate[:, k, c * H:(c + 1) * H]
                        m = P if kind == "chan" else H
                        mm(A0[0:m, :], st, hT[:, k, 0:SEQ], start=k == 0, stop=k == KC - 1)
                        i = mm(A1[0:m, 0:NS], st, hT[:, k, SEQ:T], start=k == 0, stop=k == KC - 1)
                i.then_inc(S["proj_mm"], 1)
                if u == UEND["rq"]:
                    pe.wait_ge(S["conv_acc"], 2 * H)
                    for c in range(2 * H):
                        i = tr(ps[6 + c // 4][0:NCV, (c % 4) * P:(c % 4 + 1) * P], xc[:, c, :], ident[:, :])
                    i.then_inc(S["xc_t"], 1)
                    pe.wait_ge(S["g_exp"], 4)
                    for t in range(NT):
                        n = ROWS[t]
                        i = tr(ps[4 + t // NCH][0:n, (t % NCH) * P:(t % NCH + 1) * P], rowst[:, t * P:t * P + n], ident[:, :])
                    for h in range(H):
                        i = mm(ps[5][:, 256 + 16 * h:256 + 16 * h + NCH + NB], cst["sel"][:, h, :], woldr[:, :], start=True, stop=True)
                    i.then_inc(S["cols_t"], 1)
            def QK(h):
                return (qk[:, h, 0:T], qk[:, H + h, 0:T]) if h < H else (rqk[:, h - H, :], rqk[:, h, :])

            def scores(h):
                q, k = QK(h)
                if h == H:
                    pe.wait_ge(S["rot_done"], 2 * H)
                for c in range(NCH):
                    mm(ps[1][:, c * P:(c + 1) * P], k[:, c * P:(c + 1) * P], q[:, c * P:(c + 1) * P], start=True, stop=True)

            def key_rows(h):
                _, k = QK(h)
                for c in range(NCH):
                    tr(ps[2][:, c * P:(c + 1) * P], k[:, c * P:(c + 1) * P], ident[:, :])

            def head_a(h):
                q, k = QK(h)
                if h >= 2:
                    pe.wait_ge(S["ynT_ready"], 2 * (h - 1))
                if h < H:
                    mm(ps[0][:, :], cst["sel"][:, h, :], GR["m"][:, 0:SEQ], start=True, stop=True)
                    mm(ps[3][0:NS, 0:NS], cst["sel"][:, h, 0:NS], GR["m"][:, SEQ:T], start=True, stop=True)
                mm(ps[3][0:NS, NS:2 * NS], k[:, SEQ:T], q[:, SEQ:T], start=True, stop=True)
                tr(ps[3][0:NS, P:2 * P], k[:, SEQ:T], ident[:, :]).then_inc(S["mixA"], 1)

            def chunks(h):
                q, k = QK(h)
                w = DH + 1 if h < H else DH
                if h >= 1:
                    pe.wait_ge(S["sdu"], h * NB)
                pe.wait_ge(S["stm"], h + 1)
                pe.wait_ge(S["kwa"], h + 1)
                for c in range(NCH):
                    o1 = ps[4 + c % 2]
                    if c >= 2:
                        pe.wait_ge(S["nchunk"], h * NCH + c - 1)
                    mm(o1[:, 0:w], sT[:, c, :], vv[:, c, h, 0:w], start=True, stop=True)
                    mm(o1[:, 256:256 + w], kwr[:, c, :], vv[:, c, h, 0:w], start=True, stop=True).then_inc(S["o1d"], 1)
                    if c >= 1:
                        pe.wait_ge(S["nchunk"], h * NCH + c)
                        st = prC[:, h, 0:w] if h < H else prS[:, h - H, :]
                        mm(ps[6 + c % 2][:, 0:w], q[:, c * P:(c + 1) * P], st, start=True, stop=True).then_inc(S["o2"], 1)
                    if h + 1 < 2 * H:
                        if c == 1:
                            scores(h + 1)
                        if c == 2:
                            key_rows(h + 1)

            def samples(h):
                w = DH + 1 if h < H else DH
                pe.wait_ge(S["stq"], h + 1)
                if h == 0:
                    pe.wait_ge(S["ld_stC"], 16 * NB)
                    pe.wait_ge(S["n_cols"], 1)
                if h == H:
                    pe.wait_ge(S["ld_stS"], 16 * NB)
                pe.wait_ge(S["nchunk"], h * NCH + NCH)
                mm(ps[4][0:NS, 0:w], sT_s, vv[0:NS, NCH, h, 0:w], start=True, stop=True).then_inc(S["so1"], 1)
                for b in range(NB):
                    st = stC[:, b, h, 0:w] if h < H else stS[:, b, h - H, :]
                    i = mm(ps[6][0:NS, 0:w], q8[:, b, :], st, start=b == 0, stop=b == NB - 1)
                i.then_inc(S["so2"], 1)

            def deltas(h):
                w = DH + 1 if h < H else DH
                pe.wait_ge(S["s_nc"], h + 1)
                for b in range(NB):
                    if b >= 4:
                        pe.wait_ge(S["sdu"], h * NB + b - 3)
                    mm(ps[4 + b % 4][:, 0:w], kw8[:, b, :], vv[0:NS, NCH, h, 0:w], start=True, stop=True).then_inc(S["sdb"], 1)

            def out_T(h):
                pe.wait_ge(S["yn_ready"], h + 1)
                for t in range(NT):
                    n = ROWS[t]
                    bk, o = (ps[0], t * P) if t < NCH else (ps[3], 256)
                    i = tr(bk[:, o:o + n], yn[0:n, t, :], ident[0:n, 0:n])
                i.then_inc(S["yn_t"], 1)

            pe.wait_ge(S["cols_ready"], 1)
            pe.wait_ge(S["proj_evac"], NU)
            scores(0)
            key_rows(0)
            head_a(0)
            for h in range(2 * H):
                chunks(h)
                samples(h)
                if h >= 1:
                    out_T(h - 1)
                if h == H:
                    pe.wait_ge(S["n_cols"], 2)
                    tr(ps[7][0:(1 + NB) * H, 0:DH], n_col[:, :], ident[:, :]).then_inc(S["n_cols_t"], 1)
                    pe.wait_ge(S["n_out_ready"], 1)
                if h + 1 < 2 * H:
                    head_a(h + 1)
                deltas(h)
            out_T(2 * H - 1)
            pe.wait_ge(S["ynT_ready"], 4 * H)
            pe.wait_ge(S["sdu"], 2 * H * NB)

            def y_mm(t):
                n = ROWS[t]
                if t == 0:
                    pe.wait_ge(S["ld_wo"], 32)
                if t >= 2:
                    pe.wait_ge(S["x1_done"], t - 1)
                for hf in range(2):
                    for k in range(2 * H):
                        i = mm(ps[2 * (t % 2) + hf][0:n, :], yT(k)[:, t * P:t * P + n], wo[:, k, hf * 512:(hf + 1) * 512],
                               start=k == 0, stop=k == 2 * H - 1)
                i.then_inc(S["y_mm"], 1)

            y_mm(0)
            for t in range(NT):
                if t + 1 < NT:
                    y_mm(t + 1)
                pe.wait_ge(S["h2_ready"], t + 1)
                if t >= 2:
                    pe.wait_ge(S["h2T_ready"], 2 * (t - 1))
                rows_T(hrow2, t, "h2T_t")
            pe.wait_ge(S["h2T_ready"], 2 * NT)
            pe.wait_ge(S["ld_wr"], 16)
            for t in range(NT):
                n = ROWS[t]
                if t >= 2:
                    pe.wait_ge(S["rl_sig"], t - 1)
                for k in range(KC):
                    i = mm(ps[t % 2][0:n, 0:NE], hT[:, k, t * P:t * P + n], wr[:, k, :], start=k == 0, stop=k == KC - 1)
                i.then_inc(S["rl_mm"], 1)
            pe.wait_ge(S["ld_ws"], 48)
            gu, dn = wview(1)
            for t in range(NT):
                n = ROWS[t]
                if t >= 1:
                    pe.wait_ge(S["hh_ready"], t)
                for k in range(KC):
                    i = mm(ps[2][0:n, :].rearrange("p (m f) -> p m f", m=2), hT[:, k, t * P:t * P + n], gu[:, :, k, :],
                           start=k == 0, stop=k == KC - 1)
                i.then_inc(S["gu_mm"], 1)
                pe.wait_ge(S["hh_ready"], t + 1)
                for jj in range(FJ):
                    i = tr(ps[3][:, jj * P:jj * P + n], hh[0:n, jj * P:(jj + 1) * P], ident[0:n, 0:n])
                i.then_inc(S["hhT_t"], 1)
                pe.wait_ge(S["hhT_ready"], t + 1)
                if t >= 1:
                    pe.wait_ge(S["dn_evac"], t)
                for hf in range(2):
                    for jj in range(FJ):
                        i = mm(ps[4 + hf][0:n, :], hhT[:, jj * P:jj * P + n], dn[:, jj, hf * 512:(hf + 1) * 512],
                               start=jj == 0, stop=jj == FJ - 1)
                i.then_inc(S["dn_mm"], 1)
            for t in range(NT):
                n = ROWS[t]
                pe.wait_ge(S["msk_ready"], t + 1)
                if t >= 1:
                    pe.wait_ge(S["pos_done"], t)
                for tt in range(t):
                    mm(ps[6][0:n, 0:NE], ones[:, 0:n], maskm[:, tt, :], start=tt == 0, stop=False)
                mm(ps[6][0:n, 0:NE], cst["tri"][0:n, 0:n], maskm[0:n, t, :], start=t == 0, stop=True).then_inc(S["pos_mm"], 1)
            for t in range(NT):
                n = ROWS[t]
                i = mm(ps[7][:, 0:NE], ones[0:n, :], maskm[0:n, t, :], start=t == 0, stop=t == NT - 1)
            i.then_inc(S["pos_mm"], 1)
            pe.wait_ge(S["dn_evac"], NT)

            def find_idx(n, j, part=range(NT)):
                if part[0] == 0:
                    pe.wait_ge(S["P_ready"], n + 1)
                    if not (isinstance(n, int) and n == 0):
                        pe.wait_ge(S["idx_ready"], n)
                for tt in part:
                    k = ROWS[tt]
                    pm, at_ = Pm[0:k, j % 2, tt * BLK:(tt + 1) * BLK], tt * 8
                    mm(ps[6][:, 0:3], pm, Re[0:k, j % 2, at_:at_ + 3], start=tt == 0, stop=False)
                    mm(ps[6][:, 0:3], pm, Re[0:k, j % 2, at_ + 3:at_ + 6], start=False, stop=False)
                    i = mm(ps[6][:, 1:2], pm, Re[0:k, j % 2, at_ + 6:at_ + 7], start=False, stop=tt == NT - 1)
                if part[-1] == NT - 1:
                    i.then_inc(S["idx_mm"], 1)

            def x_T(n, j, s=None):
                jj = j % 2
                pe.wait_ge(S[f"gat{jj}"], scount(n, j, s))
                if not (isinstance(n, int) and n == 0):
                    pe.wait_ge(S["xgT_a"], n)
                    pe.wait_ge(S["xgT_d"], n)
                for c in range(KC):
                    i = tr(ps[c // 4][:, (c % 4) * BLK:(c % 4 + 1) * BLK], xg[:, jj, c * P:(c + 1) * P], ident[:, :])
                i.then_inc(S["xgT_t"], 1)

            def body(n, j, ahead, s=None):
                jj = j % 2
                gu, dn = wview(jj)
                pe.wait_ge(S["xgT_a"], n + 1)
                pe.wait_ge(S["xgT_d"], n + 1)
                pe.wait_ge(S[f"ld_e{jj}"], ecount(n, j, s))
                if not (isinstance(n, int) and n == 0):
                    pe.wait_ge(S["ehh"], FJ * n)
                for c in range(KC):
                    i = mm(ps[2][:, :].rearrange("p (m f) -> p m f", m=2), xT[:, jj, c * BLK:(c + 1) * BLK], gu[:, :, c, :],
                           start=c == 0, stop=c == KC - 1)
                i.then_inc(S["egu"], 1)
                x_T(n + 1, j + 1, s if s is None else s + 1)
                find_idx(n + 2, j + 2, range(1))
                for k in range(FJ):
                    pe.wait_ge(S["ehh"], FJ * n + (k + 1))
                    tr(ps[3 + 4 * k][:, 0:BLK], hh[:, k * P:(k + 1) * P], ident[:, :]).then_inc(S["ehT_t"], 1)
                find_idx(n + 2, j + 2, range(1, NT))
                pe.wait_ge(S[f"ld_d{jj}"], scount(n, j, s))
                if not (isinstance(n, int) and n == 0):
                    pe.wait_ge(S["eout_a"], n)
                    pe.wait_ge(S["eout_d"], n)
                for k in range(FJ):
                    pe.wait_ge(S["ehT"], FJ * n + (k + 1))
                    for hf in range(2):
                        i = mm(ps[4 + hf][:, :], hhT[:, k * BLK:(k + 1) * BLK], dn[:, k, hf * 512:(hf + 1) * 512],
                               start=k == 0, stop=k == FJ - 1)
                i.then_inc(S["edn"], 1)

            find_idx(0, 0)
            find_idx(1, 1)
            x_T(0, 0)
            ladder(pe, body)
            for t in range(NT):
                n = ROWS[t]
                pe.wait_ge(S[f"yl{t % 2}"], 16 * (t // 2 + 1))
                if t >= 2:
                    pe.wait_ge(S["yl_sum"], t - 1)
                for hf in range(2):
                    parts = [shout[0:n, t, hf * 512:(hf + 1) * 512]] + \
                        [ycomb[0:n, t % 2, k * D + hf * 512:k * D + (hf + 1) * 512] for k in range(KPE)]
                    for k, y in enumerate(parts):
                        i = mm(ps[2 * (t % 2) + hf][0:n, :], ident[0:n, 0:n], y, start=k == 0, stop=k == KPE)
                i.then_inc(S["yp_mm"], 1)

        @block.vector
        def _(dve):
            def step(ins):
                step.n += 1
                ins.then_inc(S["dch"], 1)
                dve.wait_ge(S["dch"], step.n)
            step.n = 0
            tt_, ts, stt, cp = dve.tensor_tensor, dve.tensor_scalar, dve.scalar_tensor_tensor, dve.tensor_copy
            dve.wait_ge(S["cT_t"], 1)
            cp(cTs[:, :, 0:NCOND], ps[7][:, 0:16 * KC].rearrange("p (c n) -> p c n", c=KC)[:, :, 0:NCOND]).then_inc(S["cT_ready"], 1)
            dve.memset(cols[:, :, :, :], 1.0)
            dve.wait_ge(S["ld_bg"], 16 * 5)
            MODF = mod.rearrange("p a b -> p (a b)")
            for g in range(NADA):
                dve.wait_ge(S["ring_used"], g + 1)
                sl = MODF[:, g * 512:(g + 1) * 512]
                tt_(sl, sl, ps[g % 2][0:NCOND, :], ALU.add).then_inc(S["mod_evac"], 1)
                if g == 3:
                    dve.wait_ge(S["mod_evac"], g + 1)
                    stt(mod[:, 1, :], mod[:, 1, :], 1.0, g4[:, 0, :], ALU.add, ALU.mult).then_inc(S["modA"], 1)
            dve.wait_ge(S["mod_evac"], NADA)
            tt_(mod[:, 2, :], mod[:, 2, :], g4[:, 1, :], ALU.mult).then_inc(S["modA"], 1)
            stt(mod[:, 4, :], mod[:, 4, :], 1.0, g4[:, 2, :], ALU.add, ALU.mult).then_inc(S["modA"], 1)
            tt_(mod[:, 5, :], mod[:, 5, :], g4[:, 3, :], ALU.mult).then_inc(S["modA"], 1)

            def by_chunk(rows):
                return rows.rearrange("p (c q) -> p q c", c=KC)

            dve.wait_ge(S["nin_t"], 2)
            cp(n_col[:, 0:NB * H], ps[5][:, 0:NB * H])
            cp(cvbuf[:, :], ps[6][:, 0:2 * H * 24]).then_inc(S["cv_pad"], 1)
            dve.wait_ge(S["mod_ld1"], 2 * SPREAD)
            dve.wait_ge(S["rt_done"], NT)
            step(dve.reciprocal(stat[:, 2, 0:NCH], stat[:, 1, 0:NCH]))
            step(dve.reciprocal(stat[0:NS, 2, NCH:NT], stat[0:NS, 1, NCH:NT]))
            for t in range(NT):
                n, o = ROWS[t], int(t == NCH)
                if t >= 1:
                    dve.wait_ge(S["h_ready"], t)
                step(stt(junk[0:n], x_sb[0:n, t, :], stat[0:n, 2, t:t + 1], bcA[0:n, 0, o, :], ALU.mult, ALU.mult))
                if t >= 2:
                    dve.wait_ge(S["hT_t"], t - 1)
                tt_(by_chunk(hrow[0:n, t % 2, :]), junk[0:n].rearrange("p (q c) -> p q c", c=KC),
                    bcA[0:n, 1, o, :].rearrange("p (q c) -> p q c", c=KC), ALU.add).then_inc(S["h_ready"], 1)
            dve.wait_ge(S["mod_st"], 32)
            dve.wait_ge(S["h_ready"], NT)
            step(dve.memset(qk[:, :, 0:CW - 1], 0.0))
            for b in range(NB):
                i = cp(qk[:, :, PADP + b * PADS:PADP + b * PADS + CW - 1],
                       cvbuf[:, :].rearrange("p (c b w) -> p c b w", c=2 * H, b=NB)[:, :, b, :])
            step(i)
            step(dve.memset(vv[:, :, :, DH:DH + 1], 1.0))
            for ch in range(2 * H):
                dve.wait_ge(S["proj_evac"], ch + 1)
                last = QW - NB * PADS
                step(cp(xc[:, ch, 0:CW - 1], qk[:, ch, SEQ:PADP]))
                step(cp(xc[:, ch, CW - 1:NCV].rearrange("p (b w) -> p b w", b=NB),
                        qk[:, ch, PADP:QW].rearrange("p (b l) -> p b l", b=NB)[:, :, LB:PADS]))
                if ch >= 2:
                    dve.wait_ge(S["conv_silu"], ch - 1)
                ap, as_ = acc[:, ch % 2, 0:SEQ], acc[:, ch % 2, SEQ:T].rearrange("p (b l) -> p b l", b=NB)
                qs = qk[:, ch, PADP:QW].rearrange("p (b l) -> p b l", b=NB)
                for w in range(CW):
                    tap = cwT[:, ch, w:w + 1]
                    xp, xs = qk[:, ch, w:w + SEQ], qs[:, :, w:w + LB]
                    if w == 0:
                        ts(ap, xp, tap, cbT[:, ch:ch + 1], ALU.mult, ALU.add)
                        step(ts(as_, xs, tap, cbT[:, ch:ch + 1], ALU.mult, ALU.add))
                    else:
                        stt(ap, xp, tap, ap, ALU.mult, ALU.add)
                        i = stt(as_, xs, tap, as_, ALU.mult, ALU.add)
                        if w < CW - 1:
                            step(i)
                i.then_inc(S["conv_acc"], 1)
            dve.wait_ge(S["proj_evac"], UEND["g"])
            stt(GR["u"], GR["fx"], -1.0, GR["fx"], ALU.mult, ALU.max).then_inc(S["g_ax"], 1)
            dve.wait_ge(S["g_ln"], 1)
            step(ts(GR["fx"], GR["fx"], 0.0, None, ALU.min))
            step(tt_(GR["u"], GR["fx"], GR["u"], ALU.subtract))
            step(dve.tensor_tensor_scan(GR["b"], cst["seg"][:, :], GR["u"], 0.0, ALU.mult, ALU.add))
            step(tt_(GR["u"], GR["li"], GR["b"], ALU.subtract))
            step(dve.memset(mprev[:, :], 0.0))
            for c in range(NCH):
                cs = slice(c * P, (c + 1) * P)
                step(dve.tensor_tensor_scan(GR["m"][:, cs], GR["u"][:, cs], GR["u"][:, cs], mprev[:, c:c + 1], ALU.max, ALU.max))
                step(tt_(mprev[:, c + 1:c + 2], GR["m"][:, c * P + P - 1:c * P + P], GR["b"][:, c * P + P - 1:c * P + P], ALU.add))
            step(cp(GR["mp"][:, SEQ:T], GR["u"][:, SEQ:T]))
            st0 = GR["mp"][:, SEQ::LB]
            dve.wait_ge(S["ld_small"], 160)
            step(tt_(st0, st0, m_in[:, :], ALU.max))
            step(dve.tensor_tensor_scan(GR["m"][:, SEQ:T], cst["segneg"][:, 0:NS], GR["mp"][:, SEQ:T], 0.0, ALU.add, ALU.max))
            step(cp(GR["mp"][:, 0:SEQ].rearrange("p (c l) -> p c l", c=NCH), mprev[:, 0:NCH].unsqueeze(2).to_broadcast([H, NCH, P])))
            step(cp(GR["mp"][:, SEQ:T].rearrange("p (b l) -> p b l", b=NB), m_in[:, :].unsqueeze(2).to_broadcast([H, NB, LB])))
            step(tt_(GR["fx"], GR["b"], GR["m"], ALU.add))
            step(tt_(GR["li"], GR["mp"], GR["m"], ALU.subtract))
            step(tt_(GR["b"][:, 0:SEQ].rearrange("p (c l) -> p c l", c=NCH), GR["u"][:, 0:SEQ].rearrange("p (c l) -> p c l", c=NCH),
                     GR["m"][:, P - 1:SEQ:P].unsqueeze(2).to_broadcast([H, NCH, P]), ALU.subtract))
            step(tt_(GR["b"][:, SEQ:T].rearrange("p (b l) -> p b l", b=NB), GR["u"][:, SEQ:T].rearrange("p (b l) -> p b l", b=NB),
                     GR["m"][:, SEQ + LB - 1::LB].unsqueeze(2).to_broadcast([H, NB, LB]), ALU.subtract))
            dve.wait_ge(S["hT_t"], NT)
            step(dve.memset(rowst, 0.0))
            step(cp(rowst[0:H, :], GR["u"]))
            dve.memset(q8, 0.0).then_inc(S["g_t"], 1)
            step(dve.memset(bnag, 1.0))
            dve.wait_ge(S["conv_silu"], 2 * H)
            for i8 in range(2 * H):
                if i8 == H:
                    dve.wait_ge(S["cols_t"], 1)
                    for t in range(NT):
                        n = ROWS[t]
                        src = ps[4 + t // NCH][0:n, (t % NCH) * P:(t % NCH + 1) * P].rearrange("p (k r) -> p k r", k=4)[:, :, 0:H]
                        i = cp(cols[0:n, t, :, :], src)
                    step(i)
                    step(cp(wold_sb[:, :, :], ps[5][:, 256:256 + 16 * H].rearrange("p (h n) -> p h n", h=H)[:, :, 0:NCH + NB]))
                    step(ts(cols[:, 0:NCH, 3, :], cols[:, 0:NCH, 3, :], KSCALE, None, ALU.mult))
                    ts(cols[0:NS, NCH, 3, :], cols[0:NS, NCH, 3, :], KSCALE, None, ALU.mult).then_inc(S["cols_ready"], 1)
                dve.wait_ge(S["proj_evac"], UEND["rq" if i8 < H else "rk"] - H + i8 % H + 1)
                x = rqk[:, i8, :]
                if i8 >= 1:
                    dve.wait_ge(S["rot_done"], i8)
                HF = P // 2
                tt_(rotT[0:HF], x[HF:P], cst["sin"][HF:P, :], ALU.mult)
                step(tt_(rotT[HF:P], x[0:HF], cst["sin"][0:HF, :], ALU.mult))
                step(tt_(x, x, cst["cos"][:, :], ALU.mult))
                tt_(x, x, rotT, ALU.add).then_inc(S["rot_done"], 1)
            dve.wait_ge(S["ld_stC"], 16 * NB)
            cp(stC[:, :, :, DH], n_col[:, 0:NB * H].rearrange("p (b h) -> p b h", b=NB)).then_inc(S["n_cols"], 1)

            def masks(h):
                dve.wait_ge(S["mixA"], h + 1)
                if h < H:
                    tt_(wi, ps[0][:, :].rearrange("p (c l) -> p c l", c=NCH),
                        cst["causal"][:, :].unsqueeze(1).to_broadcast([P, NCH, P]), ALU.add)
                    tt_(wi_s, ps[3][0:NS, 0:NS], cst["causal_s"][:, :], ALU.add).then_inc(S["wm"], 1)

            def scores(h):
                S1 = ps[1][:, :].rearrange("p (c l) -> p c l", c=NCH)
                if h < H:
                    dve.wait_ge(S["wexp"], h + 1)
                    stt(sT, S1, KSCALE, wi, ALU.mult, ALU.mult)
                    stt(sT_s, ps[3][0:NS, NS:2 * NS], KSCALE, wi_s, ALU.mult, ALU.mult).then_inc(S["stm"], 1)
                else:
                    tt_(sT, S1, cst["decay"][:, h - H, :].unsqueeze(1).to_broadcast([P, NCH, P]), ALU.mult)
                    tt_(sT_s, ps[3][0:NS, NS:2 * NS], cst["decay_s"][:, h - H, :], ALU.mult).then_inc(S["stm"], 1)
                q = qk[:, h, 0:T] if h < H else rqk[:, h - H, :]
                for b in range(NB):
                    cp(q8[:, b, b * LB:(b + 1) * LB], q[:, SEQ + b * LB:SEQ + (b + 1) * LB])
                col = cols[0:NS, NCH, 3, h:h + 1] if h < H else cst["kw_s"][:, h - H:h - H + 1]
                step(ts(kw_s, ps[3][0:NS, P:2 * P], col, None, ALU.mult))
                tt_(kw8, kw_s.unsqueeze(1).to_broadcast([NS, NB, P]), cst["bmask"][:, :].unsqueeze(2).to_broadcast([NS, NB, P]),
                    ALU.mult).then_inc(S["stq"], 1)

            def chunk(h, c):
                num, w = num2[:, (h % 2) * NT:(h % 2 + 1) * NT, :], DH + 1 if h < H else DH
                o1 = ps[4 + c % 2]
                st = prC[:, h, 0:w] if h < H else prS[:, h - H, :]
                dve.wait_ge(S["o1d"], h * NCH + c + 1)
                if c == 0:
                    cp(st, o1[:, 256:256 + w])
                    cp(num[:, c, 0:w], o1[:, 0:w]).then_inc(S["nchunk"], 1)
                else:
                    dve.wait_ge(S["o2a"], h * (NCH - 1) + c)
                    tt_(num[:, c, 0:w], o1[:, 0:w], inter_t[:, c % 2, 0:w], ALU.add)
                    dec = wold_sb[:, h, c:c + 1] if h < H else cst["gL"][:, h - H:h - H + 1]
                    stt(st, st, dec, o1[:, 256:256 + w], ALU.mult, ALU.add).then_inc(S["nchunk"], 1)

            def samples(h):
                num, w = num2[:, (h % 2) * NT:(h % 2 + 1) * NT, :], DH + 1 if h < H else DH
                dve.wait_ge(S["so1"], h + 1)
                dve.wait_ge(S["so2a"], h + 1)
                tt_(num[0:NS, NCH, 0:w], ps[4][0:NS, 0:w], inter_t[0:NS, 0, 0:w], ALU.add).then_inc(S["s_nc"], 1)

            def deltas(h):
                w = DH + 1 if h < H else DH
                for b in range(NB):
                    dve.wait_ge(S["sdb"], h * NB + b + 1)
                    st = stC[:, b, h, 0:w] if h < H else stS[:, b, h - H, :]
                    dec = wold_sb[:, h, NCH + b:NCH + b + 1] if h < H else cst["gL"][:, H + h - H:H + h - H + 1]
                    stt(st, st, dec, ps[4 + b % 4][:, 0:w], ALU.mult, ALU.add).then_inc(S["sdu"], 1)

            def norm_a(h):
                num = num2[:, (h % 2) * NT:(h % 2 + 1) * NT, :]
                dve.wait_ge(S["s_nc"], h + 1)
                dve.wait_ge(S["nchunk"], (h + 1) * NCH)
                for t in range(NT):
                    n = ROWS[t]
                    i = dve.bn_stats(bnst[0:n, t, :], num[0:n, t, 0:DH])
                step(i)
                for t in range(NT):
                    n = ROWS[t]
                    i = dve.bn_aggr(bnag[0:n, t, :], bnst[0:n, t, :])
                step(i)
                if h < H:
                    step(stt(hstat[:, 0, :], num[:, :, DH], -1.0, num[:, :, DH], ALU.mult, ALU.max))
                    step(tt_(hstat[:, 0, :], hstat[:, 0, :], cols[:, :, 2, h], ALU.max))
                    step(dve.reciprocal(hstat[:, 3, :], hstat[:, 0, :]))
                    step(tt_(hstat[:, 4, :], hstat[:, 3, :], hstat[:, 3, :], ALU.mult))
                    tt_(hstat[:, 1, :], bnag[:, :, 1], hstat[:, 4, :], ALU.mult).then_inc(S["nrm_v"], 1)
                else:
                    cp(hstat[:, 1, :], bnag[:, :, 1]).then_inc(S["nrm_v"], 1)

            def norm_b(h):
                num = num2[:, (h % 2) * NT:(h % 2 + 1) * NT, :]
                dve.wait_ge(S["nrm_s"], h + 1)
                step(dve.reciprocal(hstat[:, 5, :], hstat[:, 2, :]))
                if h < H:
                    step(tt_(hstat[:, 5, :], hstat[:, 5, :], hstat[:, 3, :], ALU.mult))
                for t in range(NT):
                    n = ROWS[t]
                    i = ts(yn[0:n, t, :], num[0:n, t, 0:DH], bnag[0:n, t, 0:1], hstat[0:n, 5, t:t + 1], ALU.subtract, ALU.mult)
                i.then_inc(S["yn_ready"], 1)

            def out_T(h):
                dve.wait_ge(S["yn_t"], h + 1)
                y = yT(h)
                g = gnT[:, h:h + 1]
                stt(y[:, 0:SEQ], ps[0][:, :], g, gate[:, h, 0:SEQ], ALU.mult, ALU.mult).then_inc(S["ynT_ready"], 1)
                stt(y[:, SEQ:T], ps[3][:, 256:256 + NS], g, gate[:, h, SEQ:T], ALU.mult, ALU.mult).then_inc(S["ynT_ready"], 1)

            dve.wait_ge(S["rot_done"], 2 * H)
            step(dve.memset(num2, 0.0))
            dve.wait_ge(S["proj_evac"], NU)
            dve.wait_ge(S["xc_t"], 1)
            dve.wait_ge(S["st_cv"], 32)
            masks(0)
            scores(0)
            for h in range(2 * H):
                chunk(h, 0)
                if h >= 1:
                    norm_a(h - 1)
                chunk(h, 1)
                if h >= 1:
                    norm_b(h - 1)
                for c in range(2, NCH):
                    chunk(h, c)
                samples(h)
                if h >= 1:
                    out_T(h - 1)
                if h == H:
                    dve.wait_ge(S["n_cols_t"], 1)
                    cp(n_out[:, :], ps[7][0:(1 + NB) * H, 0:DH]).then_inc(S["n_out_ready"], 1)
                if h + 1 < 2 * H:
                    masks(h + 1)
                deltas(h)
                if h == H - 1:
                    dve.wait_ge(S["sdu"], NB * H)
                    dve.wait_ge(S["nchunk"], NCH * H)
                    cp(n_col[:, 0:H], prC[:, :, DH])
                    cp(n_col[:, H:].rearrange("p (b h) -> p b h", b=NB), stC[:, :, :, DH]).then_inc(S["n_cols"], 1)
                if h + 1 < 2 * H:
                    scores(h + 1)
            norm_a(2 * H - 1)
            norm_b(2 * H - 1)
            out_T(2 * H - 1)
            dve.wait_ge(S["ld_bc2"], 3 * SPREAD)
            for t in range(NT):
                n, o = ROWS[t], int(t == NCH)
                dve.wait_ge(S["y_ss"], t + 1)
                tt_(stat[0:n, 4, t:t + 1], stat[0:n, 2, t:t + 1], stat[0:n, 3, t:t + 1], ALU.add).then_inc(S["y_s2"], 1)
                dve.wait_ge(S["y_rt"], t + 1)
                if t >= 1:
                    dve.wait_ge(S["h2_ready"], t)
                step(dve.reciprocal(stat[0:n, 6, t:t + 1], stat[0:n, 5, t:t + 1]))
                for k in range(2):
                    i = stt(yrow[0:n, k * 512:(k + 1) * 512], ps[2 * (t % 2) + k][0:n, :], stat[0:n, 6, t:t + 1],
                            bcB[0:n, 0, o, k * 512:(k + 1) * 512], ALU.mult, ALU.mult)
                step(i)
                tt_(x_sb[0:n, t, :], x_sb[0:n, t, :], yrow[0:n], ALU.add).then_inc(S["x1_done"], 1)
                dve.wait_ge(S["y_rt2"], t + 1)
                step(dve.reciprocal(stat[0:n, 9, t:t + 1], stat[0:n, 8, t:t + 1]))
                step(stt(yrow[0:n], x_sb[0:n, t, :], stat[0:n, 9, t:t + 1], bcB[0:n, 1, o, :], ALU.mult, ALU.mult))
                if t >= 2:
                    dve.wait_ge(S["h2T_t"], t - 1)
                    dve.wait_ge(S[f"h2_st{t % 2}"], 16 * (t // 2))
                tt_(by_chunk(hrow2[0:n, t % 2, :]), yrow[0:n].rearrange("p (q c) -> p q c", c=KC),
                    bcB[0:n, 2, o, :].rearrange("p (q c) -> p q c", c=KC), ALU.add).then_inc(S["h2_ready"], 1)
            dve.wait_ge(S["ld_br"], 16)
            step(dve.memset(gs12, -MARK))
            step(dve.memset(r8, -MARK))
            tok = cst["tokcol"][:, :].unsqueeze(2).to_broadcast([P, NT, NE])
            step(dve.memset(R[:, :, :, :], 0.0))
            step(cp(R[:, :, :, 0], tok))
            ts(R[:, :, :, 2], R[:, :, :, 0], float(TOPK), None, ALU.mult)
            step(tt_(R[:, :, :, 3], tok, R[:, :, :, 0], ALU.subtract))
            for t in range(NT):
                n = ROWS[t]
                dve.wait_ge(S["rl_sig"], t + 1)
                s_, sbias, srt, sel_, cum = smat[0:n, t, :], rt[0:n, 0, :], rt[0:n, 1, :], rt[0:n, 2, :], rt[0:n, 3, :]
                step(tt_(sbias, s_, brow[0:n], ALU.add))
                for g in range(NG):
                    i = dve.max(srt[:, g * GSZ:(g + 1) * GSZ], sbias[:, g * GSZ:(g + 1) * GSZ])
                step(i)
                top = srt.rearrange("p (g k) -> p g k", g=NG)
                gs = gs12[0:n, 0, :]
                step(tt_(gs[:, 0:NG], top[:, :, 0], top[:, :, 1], ALU.add))
                step(dve.max(r8[0:n, 0, :], gs[:, 0:NG]))
                step(cp(r8[0:n, 1, 0:4], r8[0:n, 0, 0:4]))
                step(dve.match_replace(gs12[0:n, 1, :], r8[0:n, 1, :], gs, MARK))
                step(ts(r8[0:n, 2, :], gs12[0:n, 1, 0:NG], MARK, None, ALU.is_equal))
                step(ts(r8[0:n, 3, :], r8[0:n, 2, :], BIG, -BIG, ALU.mult, ALU.add))
                step(tt_(sel_.rearrange("p (g k) -> p g k", g=NG), sbias.rearrange("p (g k) -> p g k", g=NG),
                         r8[0:n, 3, :].unsqueeze(2).to_broadcast([n, NG, GSZ]), ALU.add))
                step(dve.max(r8[0:n, 0, :], sel_))
                step(dve.match_replace(cum, r8[0:n, 0, :], sel_, MARK))
                M = maskm[0:n, t, :]
                ts(M, cum, MARK, None, ALU.is_equal).then_inc(S["msk_ready"], 1)
                dve.wait_ge(S["msk_ready"], t + 1)
                step(tt_(sel_, s_, M, ALU.mult))
                step(dve.tensor_reduce(stat[0:n, 12, t:t + 1], sel_, AX.X, ALU.add))
                step(dve.reciprocal(stat[0:n, 13, t:t + 1], stat[0:n, 12, t:t + 1]))
                step(ts(rt[0:n, 4, :], sel_, stat[0:n, 13, t:t + 1], ROUTED, ALU.mult, ALU.mult))
                w_, w1, w2, w3 = rt[0:n, 4, :], R[0:n, t, :, 1], R[0:n, t, :, 4], R[0:n, t, :, 6]
                step(cp(w1, w_))
                step(tt_(w_, w_, w1, ALU.subtract))
                step(cp(w2, w_))
                tt_(w3, w_, w2, ALU.subtract)
                step(dve.tensor_tensor_scan(cum, ones[0:n, 0:NE], M, 0.0, ALU.mult, ALU.add))
                step(ts(cum, cum, -1.0, 1.0, ALU.mult, ALU.add))
                step(stt(R[0:n, t, :, 5], R[0:n, t, :, 3], float(TOPK), cum, ALU.mult, ALU.add))
                dve.wait_ge(S["gu_silu"], t + 1)
                if t >= 1:
                    dve.wait_ge(S["hhT_t"], t)
                tt_(hh[0:n], sg[0:n], ps[2][0:n, FE:2 * FE], ALU.mult).then_inc(S["hh_ready"], 1)
            for t in range(NT):
                n = ROWS[t]
                dve.wait_ge(S["pos_mm"], t + 1)
                step(stt(pos[0:n, t, :], ps[6][0:n, 0:NE], FAR, maskm[0:n, t, :], ALU.add, ALU.mult))
                ts(pos[0:n, t, :], pos[0:n, t, :], -FAR, None, ALU.add).then_inc(S["pos_done"], 1)
            dve.wait_ge(S["pos_mm"], NT + 1)
            step(cp(ovf[:, 0, :], ps[7][:, 0:NE]))
            dve.wait_ge(S["pos_done"], NT)

            def table():
                cnt, ob = ovf[:, 0, :], ovf[:, 1, :]
                step(ts(ob, cnt, float(BLK), None, ALU.is_gt))
                for m in range(2, DEEP):
                    step(stt(ob, cnt, float(BLK * m), ob, ALU.is_gt, ALU.add))
                step(dve.tensor_tensor_scan(cnt, ones[:, 0:NE], ob, 0.0, ALU.mult, ALU.add))
                step(cp(ntab[:, :], cnt[:, NE - 1:NE]))
                s_ = iota[:, 0:NO]
                step(tt_(ocmp, s_.unsqueeze(2).to_broadcast([P, NO, NE]), cnt.unsqueeze(1).to_broadcast([P, NO, NE]), ALU.is_ge))
                step(dve.tensor_reduce(ovs[:, 0, :], ocmp, AX.X, ALU.add))
                step(tt_(ocmp, ocmp, ob.unsqueeze(1).to_broadcast([P, NO, NE]), ALU.mult))
                step(dve.tensor_reduce(ovs[:, 1, :], ocmp, AX.X, ALU.add))
                step(ts(ovs[:, 2, :], ovs[:, 0, :], float(NE), -FAR, ALU.is_ge, ALU.mult))
                step(tt_(ovs[:, 1, :], ovs[:, 1, :], s_, ALU.subtract))
                step(ts(ovs[:, 1, :], ovs[:, 1, :], float(BLK), -float(BLK), ALU.mult, ALU.add))
                step(tt_(negoff[:, :], ovs[:, 1, :], ovs[:, 2, :], ALU.add))
                ts(etab[:, :], ovs[:, 0, :], float(NE - 1), None, ALU.min).then_inc(S["tab_ready"], 1)

            def place(n, j, e, off):
                if not (isinstance(n, int) and n < 2):
                    dve.wait_ge(S["idx_mm"], n - 1)
                re_ = Re[:, j % 2, :].rearrange("p (t k) -> p t k", t=NT)
                cp(re_, R[:, :, e, :] if isinstance(e, int) else R[:, :, bass.ds(e, 1), :].rearrange("p t a k -> p t (a k)"))
                for tt in range(NT):
                    k = ROWS[tt]
                    p = pos[0:k, tt, e:e + 1] if isinstance(e, int) else pos[0:k, tt, bass.ds(e, 1)]
                    i = ts(Pm[0:k, j % 2, tt * BLK:(tt + 1) * BLK], iota[0:k, 0:BLK], p,
                           off if isinstance(off, float) else off[0:k], ALU.subtract, ALU.is_equal)
                i.then_inc(S["P_ready"], 1)

            def idx_out(n, j, s=None):
                dve.wait_ge(S["idx_mm"], n + 1)
                q = j % 4
                if not (isinstance(n, int) and n < 4):
                    dve.wait_ge(S[f"sct{j % 2}"], icount(n, j, s))
                ts(idxg[:, q:q + 1], ps[6][:, 0:1], -1.0, float(OOB), ALU.mult, ALU.add)
                cp(wtab[:, q:q + 1], ps[6][:, 1:2])
                ts(idxs[:, q:q + 1], ps[6][:, 2:3], -1.0, float(TOPK * OOB), ALU.mult, ALU.add).then_inc(S["idx_ready"], 1)

            def icount(n, j, s):
                if isinstance(n, int):
                    return 16 * ((n - 4) // 2 + 1)
                if s is None:
                    return (n - j) * 8 + 16 * (j // 2 - 1)
                return (s - j) * 8 + 16 * (NE // 2 + j // 2 - 1)

            def xT_evac(n):
                dve.wait_ge(S["xgT_t"], n + 1)

            def body(n, j, ahead, s=None):
                if s is not None:
                    e = dve.value_load(etab[0:1, bass.ds(s + 2, 1)], min_val=0, max_val=NE - 1)
                    off = negoff[:, bass.ds(s + 2, 1)]
                elif isinstance(ahead, int) and ahead >= NE:
                    a_ = ahead - NE
                    e = dve.value_load(etab[0:1, a_:a_ + 1], min_val=0, max_val=NE - 1)
                    off = negoff[:, a_:a_ + 1]
                else:
                    e, off = ahead, 0.0
                place(n + 2, j, e, off)
                dve.wait_ge(S["egs"], n + 1)
                if not (isinstance(n, int) and n == 0):
                    dve.wait_ge(S["ehT_t"], FJ * n)
                for k in range(FJ):
                    cs = slice(k * P, (k + 1) * P)
                    stt(hh[:, cs], sg[:, cs], wtab[:, j:j + 1], ps[2][:, FE + k * P:FE + (k + 1) * P],
                        ALU.mult, ALU.mult).then_inc(S["ehh"], 1)
                dve.wait_ge(S["xgT_t"], n + 2)
                cp(xT[:, (j + 1) % 2, 4 * BLK:8 * BLK], ps[1][:, :]).then_inc(S["xgT_d"], 1)
                idx_out(n + 2, j + 2, s if s is None else s + 2)
                if isinstance(n, int) and n == 1:
                    table()
                dve.wait_ge(S["edn"], n + 1)
                if not (isinstance(n, int) and n < 2):
                    dve.wait_ge(S[f"sct{j % 2}"], scount(n, j, s) - 16)
                cp(yo[:, j % 2, 512:D], ps[5][:, :]).then_inc(S["eout_d"], 1)

            for n in range(2):
                place(n, n, n, 0.0)
            for n in range(2):
                idx_out(n, n)
            dve.wait_ge(S["xgT_t"], 1)
            cp(xT[:, 0, 4 * BLK:8 * BLK], ps[1][:, :]).then_inc(S["xgT_d"], 1)
            dve.wait_ge(S["xgT_d"], 1)
            ladder(dve, body)
            dve.wait_ge(S["ld_bcg"], SPREAD)
            for t in range(NT):
                n, o = ROWS[t], int(t == NCH)
                dve.wait_ge(S[f"yl{t % 2}"], 16 * (t // 2 + 1))
                yc = ycomb[0:n, t % 2, KPE * D:].rearrange("p (k d) -> p d k", k=TOPK - KPE)
                if t >= 1:
                    dve.wait_ge(S["x2_done"], t)
                else:
                    dve.wait_ge(S["sctr"], 1)
                step(dve.tensor_reduce(yo[0:n, 0, :], yc, AX.X, ALU.add))
                dve.wait_ge(S["yp_mm"], t + 1)
                for hf in range(2):
                    half = yo[0:n, 0, hf * 512:(hf + 1) * 512]
                    i = tt_(half, half, ps[2 * (t % 2) + hf][0:n, :], ALU.add)
                i.then_inc(S["yl_sum"], 1)
                dve.wait_ge(S["yf_rt"], t + 1)
                step(dve.reciprocal(stat[0:n, 12, t:t + 1], stat[0:n, 11, t:t + 1]))
                step(stt(yo[0:n, 0, :], yo[0:n, 0, :], stat[0:n, 12, t:t + 1], bcG[0:n, o, :], ALU.mult, ALU.mult))
                tt_(x_sb[0:n, t, :], x_sb[0:n, t, :], yo[0:n, 0, :], ALU.add).then_inc(S["x2_done"], 1)


def shape_constants():
    import numpy as np
    f = np.float32
    i = np.arange(P)
    k = {"ident": np.eye(P, dtype=f), "iota": np.tile(i.astype(f), (P, 1)), "tri": (i[:, None] < i[None, :]).astype(f)}
    k["causal"] = np.where(i[None, :] >= i[:, None], 0.0, BIG).astype(f)
    s = np.arange(NS)
    same = (s[:, None] // LB == s[None, :] // LB) & (s[None, :] >= s[:, None])
    k["causal_s"] = np.where(same, 0.0, BIG).astype(f)
    lg = np.log1p(-np.exp2(-5.0 - np.arange(H, dtype=f))).astype(f)
    rel = (i[None, :] - i[:, None]).astype(f)
    k["decay"] = np.stack([np.where(rel >= 0, np.exp(np.maximum(rel, 0) * g), 0.0) * KSCALE for g in lg], 1).astype(f)
    rel = (s[None, :] - s[:, None]).astype(f)
    k["decay_s"] = np.stack([np.where(same, np.exp(np.maximum(rel, 0) * g), 0.0) * KSCALE for g in lg], 1).astype(f)
    half = DH // 2
    fr = (f(10000.0) ** (-np.arange(half, dtype=f) / f(half))).astype(f)
    pos = np.concatenate([np.arange(SEQ), 4096 + np.tile(np.arange(LB), NB)]).astype(f)
    ang = (pos[None, :] * fr[:, None]).astype(f).astype(np.float64)
    k["cos"] = np.concatenate([np.cos(ang), np.cos(ang)]).astype(f)
    k["sin"] = np.concatenate([np.sin(ang), -np.sin(ang)]).astype(f)
    sel = np.zeros((H, H, P), f)
    for h in range(H):
        sel[h, h] = 1.0
    k["sel"] = sel
    k["bmask"] = (s[:, None] // LB == np.arange(NB)[None, :]).astype(f)
    k["inter"] = np.exp((i[:, None] + 1.0) * lg[None, :]).astype(f)
    k["inter_s"] = np.exp((s[:, None] % LB + 1.0) * lg[None, :]).astype(f)
    k["kw"] = (np.exp((P - 1.0 - i)[:, None] * lg[None, :]) * KSCALE).astype(f)
    k["kw_s"] = (np.exp((LB - 1.0 - s % LB)[:, None] * lg[None, :]) * KSCALE).astype(f)
    seg = np.ones((H, T), f)
    seg[:, 0:SEQ:P] = 0.0
    seg[:, SEQ::LB] = 0.0
    k["seg"] = seg
    sn = np.zeros((H, NS), f)
    sn[:, ::LB] = -BIG
    k["segneg"] = sn
    tok = (np.arange(NT)[None, :] * P + i[:, None]).astype(f)
    k["tokcol"] = (OOB - tok).astype(f)
    k["gL"] = np.tile(np.concatenate([np.exp(P * lg), np.exp(LB * lg)])[None, :], (P, 1)).astype(f)
    return {n: np.ascontiguousarray(v) for n, v in k.items()}


_OUTS = [(1, SEQ, D), (NB, LB, D), (1, 1, H, DH, DH), (1, 1, H, DH), (1, 1, H), (1, 1, CW - 1, D), (1, 1, H, DH, DH),
         (1, NB, H, DH, DH), (1, NB, H, DH), (1, NB, H), (1, NB, CW - 1, D), (1, NB, H, DH, DH)]


def kernel(**inputs):
    import numpy as np
    import concourse.bacc as bacc
    from concourse.bass_utils import run_bass_kernel_spmd

    nc = bacc.Bacc("TRN2", target_bir_lowering=False, num_devices=1)
    arrays, args, consts = {}, {}, {}
    for name, v in inputs.items():
        v = np.ascontiguousarray(v)
        arrays["in_" + name] = v
        args[name] = nc.dram_tensor("in_" + name, v.shape, mybir.dt.from_np(v.dtype), kind="ExternalInput").ap()
    for name, v in shape_constants().items():
        arrays["k_" + name] = v
        consts[name] = nc.dram_tensor("k_" + name, v.shape, F32, kind="ExternalInput").ap()
    outs = [nc.dram_tensor(f"out_{i}", s, F32, kind="ExternalOutput").ap() for i, s in enumerate(_OUTS)]
    build(nc, args, outs, consts)
    r = run_bass_kernel_spmd(nc, [arrays], core_ids=[0])
    return tuple(r.results[0][f"out_{i}"] for i in range(len(_OUTS)))
```

```python
from contextlib import ExitStack

import concourse.bass as bass
from concourse import mybir

F32 = mybir.dt.float32
BF16 = mybir.dt.bfloat16
U32 = mybir.dt.uint32
I32 = mybir.dt.int32
ALU = mybir.AluOpType
ACT = mybir.ActivationFunctionType
AX = mybir.AxisListType

P = 128
D = 1024
KC = D // P
SEQ = 512
NCH = SEQ // P
NB, LB = 8, 8
NS = NB * LB
T = SEQ + NS
NT = NCH + 1
ROWS = [P] * NCH + [NS]
NCOND = 1 + NB
H = 4
DH = 128
CW = 4
PADP = SEQ + CW - 1
PADS = LB + CW - 1
QW = PADP + NB * PADS
NE = 64
TOPK = 8
KPE = 4
NG, GSZ = 8, 8
FE = 256
FJ = FE // P
BLK = 128
OVMAX = T * TOPK // BLK
DEEP = (T + BLK - 1) // BLK
EPS = 1e-6
KSCALE = DH ** -0.5
BIG = 1e30
FAR = 1e6
OOB = 1024
MARK = 3e38
ROUTED = 2.5
CONSTS = ["ident", "iota", "tri", "causal", "causal_s", "decay", "decay_s", "cos", "sin", "sel", "bmask",
          "inter", "inter_s", "kw", "kw_s", "seg", "segneg", "tokcol", "gL"]


def carve(region, at, shape, rows=P, dt=F32):
    n = 1
    for s in shape:
        n *= s
    if dt != F32:
        n //= 2
    v = region[0:rows, at:at + n]
    if dt != F32:
        v = v.bitcast(dt)
    if len(shape) == 2:
        v = v.rearrange("p (a b) -> p a b", a=shape[0])
    elif len(shape) == 3:
        v = v.rearrange("p (a b c) -> p a b c", a=shape[0], b=shape[1])
    return v, at + n


def build(nc, A, O, K):
    ctx = ExitStack()
    with ctx:
        def sb(name, shape, dt=F32):
            return ctx.enter_context(nc.sbuf_tensor(name, shape, dt))

        def sem(name):
            return ctx.enter_context(nc.semaphore(name))

        mod_d = nc.dram_tensor("mod_rows", [NCOND, 6 * D], F32, kind="Internal").ap()
        h_d = nc.dram_tensor("ffn_in_rows", [T, D], F32, kind="Internal").ap()
        y_d = nc.dram_tensor("expert_out_rows", [T * TOPK, D], F32, kind="Internal").ap()

        x_sb = sb("x_sb", [P, NT, D])
        hT = sb("hT", [P, KC, T])
        cst = {k: sb("c_" + k, list(K[k].shape)) for k in CONSTS}
        ident, iota = cst["ident"], cst["iota"]
        ones = sb("ones", [P, P])
        epsc = sb("epsc", [P, 1])
        pchk = sb("pchk", [P, 1])
        stat = sb("stat", [P, 14, NT])
        hstat = sb("hstat", [P, 6, NT])
        cols = sb("cols", [P, NT, 4, H])
        wold_sb = sb("wold_sb", [P, H, NCH + NB])
        gnT = sb("gnT", [P, 2 * H])
        cwT = sb("cwT", [P, 2 * H, CW])
        cbT = sb("cbT", [P, 2 * H])
        bgate = sb("bgate", [H, 2])
        wgate = sb("wgate", [P, KC, 2 * H])
        GRN = ["li", "fx", "b", "u", "m", "mp"]
        grows = sb("grows", [H, len(GRN), T])
        GR = {n: grows[:, i, :] for i, n in enumerate(GRN)}
        mprev = sb("mprev", [H, NCH + 1])
        m_in = sb("m_in", [H, NB])
        woldr = sb("woldr", [H, NCH + NB])
        cvbuf = sb("cvbuf", [P, 2 * H * NB * (CW - 1)])
        n_in = sb("n_in", [NB * H, DH])
        n_col = sb("n_col", [P, (1 + NB) * H])
        n_out = sb("n_out", [(1 + NB) * H, DH])
        wtab = sb("wtab", [P, 4])
        idxg = sb("idxg", [P, 4], U32)
        idxs = sb("idxs", [P, 4], U32)
        NO = OVMAX + 4
        etab = sb("etab", [P, NO], I32)
        ntab = sb("ntab", [P, 1], I32)
        negoff = sb("negoff", [P, NO])
        ovf = sb("ovf", [P, 2, NE])
        ovs = sb("ovs", [P, 3, NO])

        NM = 34300
        mem = sb("mem", [P, NM])
        ring, at = carve(mem, 0, [2, KC * 512])
        at += 32
        stC, e_ = carve(mem, 0, [NB, H, DH + 1])
        stS, e_ = carve(mem, e_, [NB, H, DH])
        woA, wa_ = carve(mem, 0, [H, D])
        bcB, wb_ = carve(mem, NB * H * (DH + 1), [2, 2, D])
        assert wa_ <= NB * H * (DH + 1) and wb_ <= e_
        assert e_ <= at
        temps0 = at
        wi, at = carve(mem, at, [NCH, P])
        sT, at = carve(mem, at, [NCH, P])
        kwr, at = carve(mem, at, [NCH, P])
        wi_s, at = carve(mem, at, [NS], NS)
        sT_s, at = carve(mem, at, [NS], NS)
        kw_s, at = carve(mem, at, [P], NS)
        kw8, at = carve(mem, at, [NB, P], NS)
        q8f, at = carve(mem, at, [NB, NS + LB])
        q8d = q8f[:, :, 0:LB]
        q8 = q8f.rearrange("p b m -> p (b m)")[:, 0:NB * NS].rearrange("p (b m) -> p b m", b=NB)
        num_at = at
        num2, at = carve(mem, at, [2 * NT, DH + 1])
        num_end = at
        yn, at = carve(mem, at, [NT, DH])
        inter_t, at = carve(mem, at, [2, DH + 1])
        bnst, at = carve(mem, at, [NT, 6])
        bnag, at = carve(mem, at, [NT, 2])
        temps1 = at
        hrow, e_ = carve(mem, temps0, [2, D])
        junk, e_ = carve(mem, e_, [D])
        crow, e_ = carve(mem, e_, [D], NCOND)
        cTs, e_ = carve(mem, e_, [KC, 16])
        assert e_ <= temps1
        NCV = (CW - 1) * (1 + NB)
        rowst, e_ = carve(mem, temps0, [T])
        xc, e_ = carve(mem, e_, [2 * H, NCV])
        cv_out, e_ = carve(mem, e_, [D], NCV)
        assert e_ <= num_at
        yrow, e_ = carve(mem, temps0, [D])
        hrow2, e_ = carve(mem, e_, [2, D])
        junk2, e_mix = carve(mem, e_, [D])
        assert e_mix <= temps1
        v_at = at
        vv, at = carve(mem, at, [NT, 2 * H, DH + 1])
        g4, g4_end = carve(mem, v_at, [4, D], NCOND)
        gate_at = at
        gate, at = carve(mem, at, [2 * H, T])
        bcA, _ = carve(mem, gate_at, [2, 2, D])
        woB, e_ = carve(mem, v_at, [H, D])
        assert e_ <= gate_at
        qk_at = at
        qk, at = carve(mem, at, [2 * H, QW])
        bcC, e_ = carve(mem, qk_at + H * QW, [2, D])
        assert e_ <= at
        mod, _ = carve(mem, qk_at, [6, D], NCOND)
        rqk_at = at
        rqk, at = carve(mem, at, [2 * H, T])
        prC, at = carve(mem, at, [H, DH + 1])
        prS, at = carve(mem, at, [H, DH])
        acc, e_ = carve(mem, num_at, [2, T])
        assert e_ <= num_end
        cv_in, e_ = carve(mem, g4_end, [D], NB * (CW - 1))
        assert e_ <= gate_at
        rotT = acc[:, 0, :]
        assert at <= NM, at

        def yT(h):
            return qk[:, h, 0:T] if h < H else rqk[:, h - H, :]

        W, at = carve(mem, 0, [2, 3 * KC * FE])
        ycomb, _ = carve(mem, 0, [2, TOPK * D])
        at = e_mix
        hhT, at = carve(mem, at, [FJ * BLK])
        at = max(at, 3 * 2 * KC * FE)
        Pm, at = carve(mem, at, [2, NT * BLK], dt=BF16)
        xg, at = carve(mem, at, [2, D])
        xT, at = carve(mem, at, [2, KC * BLK])
        yo, at = carve(mem, max(at, 2 * TOPK * D), [2, D])
        bcG, at = carve(mem, at, [2, D])
        assert at <= qk_at
        gu_s, e_ = carve(mem, gate_at, [2, KC, FE])
        wr, e_ = carve(mem, e_, [KC, NE])
        assert e_ <= qk_at
        shout, at = carve(mem, qk_at, [NT, D])
        R, at = carve(mem, at, [NT, NE, 8], dt=BF16)
        Re, at = carve(mem, at, [2, NT * 8], dt=BF16)
        hh, at = carve(mem, at, [FE])
        sg, at = carve(mem, at, [FE])
        assert at <= rqk_at + H * T
        dn_s, at = carve(mem, rqk_at + H * T, [FJ, D])
        smat, at = carve(mem, at, [NT, NE])
        maskm, at = carve(mem, at, [NT, NE])
        pos, at = carve(mem, at, [NT, NE])
        rt, at = carve(mem, at, [6, NE])
        gs12, at = carve(mem, at, [2, 12])
        r8, at = carve(mem, at, [4, 8])
        brow, at = carve(mem, at, [NE])
        assert at <= NM, at
        ocmp, _ = carve(hT[:, :, :].rearrange("p c t -> p (c t)"), 0, [NO, NE])

        ps = [ctx.enter_context(nc.psum_tensor(f"bank{i}", [P, 512], F32)) for i in range(8)]

        names = """ld_id ld_const ld_x ld_cond ld_bg ld_small ld_w0 ld_w1 ld_wg sets ld_cv
            c_silu cT_t cT_ready nin_t mod_evac modA mod_st mod_ld1 rt_done h_ready hT_t hT_ready
            ring_used proj_mm proj_evac cv_pad conv_acc conv_silu st_cv xc_t cvo_ready st_out
            g_ax g_ln g_t g_exp cols_t cols_ready rot_done
            ld_stC ld_stS mixA wm wexp kwa stm stq q8_ready o1d o2 o2a nchunk so1 so2 so2a s_nc sdb sdu
            nrm_v nrm_s yn_ready yn_t ynT_ready n_cols n_cols_t n_out_ready ld_woA ld_woB st_C ld_bc1 y_mm y_ss y_s2 y_rt x1_done
            y_rt2 h2_ready h2T_t h2T_ready h2_st0 h2_st1 ld_bc2 ld_wr rl_mm rl_sig ld_ws ld_wsd ld_bcg ld_br
            msk_ready pos_mm pos_done tab_ready gu_mm gu_silu hh_ready hhT_t hhT_ready dn_mm dn_evac
            P_ready idx_mm idx_ready gat0 gat1 xgT_t xgT_a xgT_d egate egu egs ehh ehT_t ehT edn eout_a eout_d sct0 sct1
            ld_g0 ld_g1 ld_u0 ld_u1 ld_d0 ld_d1 sctr yp_mm yd0 yd1 yd_sum yl0 yl1 yl_sum yf_rt x2_done out_st dch ach pch pool_step""".split()
        S = {n: sem(n) for n in names}
        block = ctx.enter_context(nc.Block())
        w_in = A["w_in"][0].rearrange("(p c) n -> p c n", c=KC)
        w_ada = A["w_ada"][0].rearrange("(p c) n -> p c n", c=KC)
        MW = H * DH
        OG = 4 * MW
        BLOCKS = [("mv", 2 * MW), ("qk0", 0), ("qk1", MW), ("mo", 3 * MW), ("rq", OG + 2 * H),
                  ("rk", OG + 2 * H + MW), ("rv", OG + 2 * H + 2 * MW), ("rg", OG + 2 * H + 3 * MW)]
        NADA = 6 * D // 512
        NBLK = NADA + len(BLOCKS)
        UNITS = []
        for bi, (nm, _) in enumerate(BLOCKS):
            if nm in ("mv", "rv"):
                UNITS += [("tok", nm, bi, t) for t in range(NT)]
            else:
                UNITS += [("chan", nm, bi, c) for c in range(4)]
            if nm == "qk1":
                UNITS += [("gate", "g", bi, 0), ("gate", "g", bi, 1)]
        NU = len(UNITS)
        UEND = {}
        for u, x in enumerate(UNITS):
            UEND[x[1]] = u + 1
        UG = UEND["rv"]

        def unit_banks(u):
            b = 2 * (u % 2) + (4 if u >= UG else 0)
            return ps[b], ps[b + 1]

        def y_banks(t):
            return (1, 2) if t % 2 == 0 else (0, 3)

        UQ = UEND["mv"]
        TH = T // 2
        NST = 2 + 2 + 2

        def wview(j):
            gu = W[:, j, 0:2 * KC * FE].rearrange("p (m c f) -> p m c f", m=2, c=KC)
            dn = W[:, j, 2 * KC * FE:3 * KC * FE].rearrange("p (j d) -> p j d", j=FJ)
            return gu, dn

        def load_up(sp, w, src, s):
            sp.dma_start(w, src.rearrange("(p c) f -> p c f", c=KC)).then_inc(s, 16)

        def load_down(sp, dn, d, s):
            sp.dma_start(dn, d.rearrange("(j p) d -> p j d", p=P)).then_inc(s, 16)

        def one_expert(name, e):
            return A[name][0, bass.ds(e, 1)].rearrange("a d f -> (a d) f")

        def ladder(eng, body, load_table=True):
            for n in range(4):
                body(n, n, n + 2)
            with eng.Fori(1, NE // 4 - 1) as i:
                for j in range(4):
                    body(4 * i + j, j, 4 * i + j + 2)
            if load_table:
                eng.wait_ge(S["tab_ready"], 1)
            for n in range(NE - 4, NE):
                body(n, n % 4, n + 2)
            nov = eng.value_load(ntab[0:1, 0:1], min_val=0, max_val=OVMAX)
            with eng.Fori(0, OVMAX // 4) as i:
                with eng.If(4 * i < nov):
                    for j in range(4):
                        with eng.If(4 * i + j < nov):
                            body(4 * i + (NE + j), j, None, 4 * i + j)
            return nov

        def scount(n, j, s=None):
            if isinstance(n, int):
                return 16 * (n // 2 + 1)
            if s is None:
                return (n - j) * 8 + 16 * (j // 2 + 1)
            return (s - j) * 8 + 16 * (NE // 2 + j // 2 + 1)

        @block.sync
        def _(sp):
            def ring_load(n):
                if 2 <= n < NADA + 2:
                    sp.wait_ge(S["ring_used"], n - 1)
                elif n >= 2:
                    sp.wait_ge(S["proj_mm"], UEND[BLOCKS[n - NADA - 2][0]])
                src = w_ada[:, :, n * 512:(n + 1) * 512] if n < NADA else \
                    w_in[:, :, BLOCKS[n - NADA][1]:BLOCKS[n - NADA][1] + 512]
                dst = ring[:, n % 2, :].rearrange("p (c f) -> p c f", c=KC)
                sp.dma_start(dst, src).then_inc(S[f"ld_w{n % 2}"], 16)

            sp.dma_start(ident[:, :], K["ident"]).then_inc(S["ld_id"], 16)
            sp.dma_start(crow[0:1, :], A["c_prompt"]).then_inc(S["ld_cond"], 16)
            sp.dma_start(crow[1:NCOND, :], A["c_sample"]).then_inc(S["ld_cond"], 16)
            sp.dma_start(mod.rearrange("p a b -> p (a b)"), A["b_ada"][0].partition_broadcast(NCOND)).then_inc(S["ld_bg"], 16)
            ring_load(0)
            ring_load(1)
            for i, g in enumerate(["g_mix_pre", "g_mix_post", "g_ffn_pre", "g_ffn_post"]):
                sp.dma_start(g4[:, i, :], A[g][0].partition_broadcast(NCOND)).then_inc(S["ld_bg"], 16)
            sp.dma_start(cv_in, A["state_mlstm_conv"][0].rearrange("b w c -> (b w) c")).then_inc(S["ld_cv"], 16)

            for n in range(2, NADA + 2):
                ring_load(n)
                if 3 <= n < 3 + NT:
                    t = n - 3
                    src = A["x_prompt"][0, t * P:(t + 1) * P, :] if t < NCH else A["x_sample"].rearrange("b l d -> (b l) d")
                    sp.dma_start(x_sb[0:ROWS[t], t, :], src).then_inc(S["ld_x"], 16)
            for k in CONSTS[1:]:
                dst = cst[k][:, :] if len(K[k].shape) == 2 else cst[k][:, :, :]
                sp.dma_start(dst, K[k]).then_inc(S["ld_const"], 16)
            for n in range(NADA + 2, NBLK):
                ring_load(n)
            sp.wait_ge(S["proj_mm"], NU)
            for b in range(NB):
                sp.dma_start(stC[:, b, :, 0:DH], A["state_mlstm_C"][0, b].rearrange("h d e -> d h e")).then_inc(S["ld_stC"], 16)
            for b in range(NB):
                sp.dma_start(stS[:, b, :, :], A["state_ret_S"][0, b].rearrange("h d e -> d h e")).then_inc(S["ld_stS"], 16)
            wos = A["w_out"][0].rearrange("(c p) n -> p c n", p=P)
            sp.wait_ge(S["st_C"], 16 * (1 + NB))
            sp.wait_ge(S["n_cols"], 2)
            sp.dma_start(woA, wos[:, 0:H, :]).then_inc(S["ld_woA"], 16)
            sp.wait_ge(S["sdu"], 2 * NB * H)
            sp.dma_start(woB, wos[:, H:2 * H, :]).then_inc(S["ld_woB"], 16)
            sp.wait_ge(S["ynT_ready"], 4 * H)
            sp.dma_start(wr, A["w_router"][0].rearrange("(p c) n -> p c n", c=KC)).then_inc(S["ld_wr"], 16)
            load_up(sp, gu_s[:, 0, :, :], A["w_sh_gate"][0], S["ld_ws"])
            load_up(sp, gu_s[:, 1, :, :], A["w_sh_up"][0], S["ld_ws"])
            load_down(sp, dn_s, A["w_sh_down"][0], S["ld_wsd"])
            sp.wait_ge(S["st_out"], 16 * NST)
            sp.dma_start(brow, A["b_router"][0].partition_broadcast(P)).then_inc(S["ld_br"], 16)
            sp.wait_ge(S["h2T_t"], NT)
            sp.wait_ge(S["h2_st0"], 16 * ((NT + 1) // 2))
            sp.wait_ge(S["h2_st1"], 16 * (NT // 2))

            def body(n, j, ahead, s=None):
                later = not (isinstance(n, int) and n < 2)
                gu, dn = wview(j % 2)
                e = n if s is None else sp.value_load(etab[0:1, bass.ds(s, 1)], min_val=0, max_val=NE - 1)
                if later:
                    sp.wait_ge(S["egate"], n - 1)
                load_up(sp, gu[:, 0, :, :], one_expert("w_exp_gate", e), S[f"ld_g{j % 2}"])
                if later:
                    sp.wait_ge(S["egu"], n - 1)
                load_up(sp, gu[:, 1, :, :], one_expert("w_exp_up", e), S[f"ld_u{j % 2}"])
                if later:
                    sp.wait_ge(S["edn"], n - 1)
                load_down(sp, dn, one_expert("w_exp_down", e), S[f"ld_d{j % 2}"])

            ladder(sp, body)
            sp.wait_ge(S["sctr"], 1)
            yv = y_d.rearrange("(t k) d -> t (k d)", k=TOPK)
            for t in range(NT):
                if t >= 2:
                    sp.wait_ge(S["yp_mm"], t - 1)
                sp.dma_start(ycomb[0:ROWS[t], t % 2, 0:KPE * D], yv[t * P:t * P + ROWS[t], 0:KPE * D]).then_inc(S[f"yl{t % 2}"], 16)
                if t >= 2:
                    sp.wait_ge(S["yd_sum"], t - 1)
                sp.dma_start(ycomb[0:ROWS[t], t % 2, KPE * D:], yv[t * P:t * P + ROWS[t], KPE * D:]).then_inc(S[f"yd{t % 2}"], 16)
            for t in range(NT):
                sp.wait_ge(S["x2_done"], t + 1)
                dst = O[0][0, t * P:(t + 1) * P, :] if t < NCH else O[1].rearrange("b l d -> (b l) d")
                sp.dma_start(dst, x_sb[0:ROWS[t], t, :]).then_inc(S["out_st"], 16)
            sp.wait_ge(S["st_cv"], 32)
            sp.wait_ge(S["out_st"], 16 * NT)

        def spread(pool, dst, part, s):
            src = mod_d[:, part * D:(part + 1) * D]
            pool.dma_start(dst[:, 0, :], src[0].partition_broadcast(P)).then_inc(s, 16)
            pool.dma_start(dst[0:NS, 1, :],
                           src[1:NCOND].unsqueeze(1).to_broadcast([NB, LB, D])).then_inc(s, 16)

        SPREAD = 16 * 2

        @block.gpsimd
        def _(pool):
            pool.memset(ones[:, :], 1.0).then_inc(S["sets"], 1)
            pool.memset(epsc[:, :], EPS).then_inc(S["sets"], 1)
            pool.dma_start(n_in[:, :], A["state_mlstm_n"][0].rearrange("b h d -> (b h) d")).then_inc(S["ld_small"], 16)
            with nc.allow_non_contiguous_dma("a few short columns"):
                pool.dma_start(m_in[:, :], A["state_mlstm_m"][0].rearrange("b h -> h b")).then_inc(S["ld_small"], 16)
                pool.dma_start(gnT[:, 0:H], A["m_gn"][0].rearrange("(h p) -> p h", p=P)).then_inc(S["ld_small"], 16)
                pool.dma_start(gnT[:, H:2 * H], A["r_gn"][0].rearrange("(h p) -> p h", p=P)).then_inc(S["ld_small"], 16)
                for w in range(CW):
                    pool.dma_start(cwT[:, :, w], A["conv_w"][0, w].rearrange("(c p) -> p c", p=P)).then_inc(S["ld_small"], 16)
                pool.dma_start(cbT[:, :], A["conv_b"][0].rearrange("(c p) -> p c", p=P)).then_inc(S["ld_small"], 16)
                pool.dma_start(bgate[:, :], A["b_gates"][0].rearrange("(k h) -> h k", h=H)).then_inc(S["ld_small"], 16)
                pool.dma_start(wgate[:, :, :], w_in[:, :, OG:OG + 2 * H]).then_inc(S["ld_wg"], 16)
            pool.wait_ge(S["modA"], 1)
            pool.dma_start(mod_d[:, 0:2 * D], mod[:, 0:2, :].rearrange("p a b -> p (a b)")).then_inc(S["mod_st"], 16)
            pool.wait_ge(S["mod_st"], 16)
            spread(pool, bcA[:, 0], 1, S["mod_ld1"])
            spread(pool, bcA[:, 1], 0, S["mod_ld1"])
            pool.wait_ge(S["modA"], 4)
            pool.dma_start(mod_d[:, 2 * D:6 * D], mod[:, 2:6, :].rearrange("p a b -> p (a b)")).then_inc(S["mod_st"], 16)
            pool.wait_ge(S["cvo_ready"], 1)
            pool.dma_start(O[5][0, 0], cv_out[0:CW - 1, :]).then_inc(S["st_cv"], 16)
            pool.dma_start(O[10][0].rearrange("b w c -> (b w) c"), cv_out[CW - 1:NCV, :]).then_inc(S["st_cv"], 16)
            pool.wait_ge(S["g_exp"], 4)
            with nc.allow_non_contiguous_dma("one value per head and sequence"):
                pool.dma_start(O[4][0].rearrange("b h -> h b"), GR["fx"][:, SEQ - 1:SEQ]).then_inc(S["st_out"], 16)
                pool.dma_start(O[9][0].rearrange("b h -> h b"), GR["fx"][:, SEQ + LB - 1::LB]).then_inc(S["st_out"], 16)
            pool.wait_ge(S["sdu"], NB * H)
            pool.wait_ge(S["nchunk"], NCH * H)
            pool.dma_start(O[2][0, 0].rearrange("h d e -> d h e"), prC[:, :, 0:DH]).then_inc(S["st_C"], 16)
            for b in range(NB):
                pool.dma_start(O[7][0, b].rearrange("h d e -> d h e"), stC[:, b, :, 0:DH]).then_inc(S["st_C"], 16)
            pool.wait_ge(S["n_out_ready"], 1)
            pool.dma_start(O[3][0, 0], n_out[0:H, :]).then_inc(S["st_out"], 16)
            pool.dma_start(O[8][0].rearrange("b h d -> (b h) d"), n_out[H:(1 + NB) * H, :]).then_inc(S["st_out"], 16)
            pool.wait_ge(S["mod_st"], 32)
            spread(pool, bcC, 2, S["ld_bc1"])
            pool.wait_ge(S["sdu"], 2 * NB * H)
            pool.wait_ge(S["nchunk"], NCH * 2 * H)
            pool.dma_start(O[6][0, 0].rearrange("h d e -> d h e"), prS).then_inc(S["st_out"], 16)
            pool.dma_start(O[11][0].rearrange("b h d e -> d (b h) e"), stS.rearrange("p b h e -> p (b h) e")).then_inc(S["st_out"], 16)
            pool.wait_ge(S["st_out"], 16 * NST)
            for i, part in enumerate((4, 3)):
                spread(pool, bcB[:, i], part, S["ld_bc2"])
            for t in range(NT):
                pool.wait_ge(S["h2_ready"], t + 1)
                pool.dma_start(h_d[t * P:t * P + ROWS[t], :], hrow2[0:ROWS[t], t % 2, :]).then_inc(S[f"h2_st{t % 2}"], 16)
            pool.wait_ge(S["h2T_t"], NT)
            pool.memset(xg, 0.0).then_inc(S["pch"], 1)
            pool.wait_ge(S["pch"], 1)
            pool.wait_ge(S["h2_st0"], 16 * ((NT + 1) // 2))
            pool.wait_ge(S["h2_st1"], 16 * (NT // 2))

            def gather(j):
                pool.indirect_dma_start(xg[:, j % 2, :], None, h_d[:, :], bass.IndirectOffsetOnAxis(idxg[:, j:j + 1], 0),
                                        bounds_check=T - 1, oob_is_err=False).then_inc(S[f"gat{j % 2}"], 16)

            def body(n, j, ahead, s=None):
                pool.wait_ge(S["idx_ready"], n + 3)
                pool.wait_ge(S["xgT_t"], n + 1)
                pool.sem_inc(S["pool_step"], 1)
                gather((j + 2) % 4)
                pool.wait_ge(S["eout_a"], n + 1)
                pool.wait_ge(S["eout_d"], n + 1)
                pool.sem_inc(S["pool_step"], 1)
                pool.indirect_dma_start(y_d[:, :], bass.IndirectOffsetOnAxis(idxs[:, j:j + 1], 0), yo[:, j % 2, :], None,
                                        bounds_check=T * TOPK - 1, oob_is_err=False).then_inc(S[f"sct{j % 2}"], 16)
                if isinstance(n, int) and n == 3:
                    spread(pool, bcG, 5, S["ld_bcg"])

            def first(j):
                pool.wait_ge(S["idx_ready"], j + 1)
                gather(j)

            first(0)
            first(1)
            nov = ladder(pool, body)
            pool.wait_ge(S["sct0"], 16 * (NE // 2) + 16 * ((nov + 1) // 2))
            pool.wait_ge(S["sct1"], 16 * (NE // 2) + 16 * (nov // 2))
            pool.tensor_tensor(pchk[:, :], epsc[:, :], epsc[:, :], ALU.add).then_inc(S["sctr"], 1)

        @block.scalar
        def _(act):
            def step(ins):
                step.n += 1
                ins.then_inc(S["ach"], 1)
                act.wait_ge(S["ach"], step.n)
            step.n = 0
            a = act.activation
            act.wait_ge(S["ld_cond"], 32)
            a(crow, crow, ACT.Silu).then_inc(S["c_silu"], 1)
            act.wait_ge(S["ld_x"], 16 * NT)
            act.wait_ge(S["sets"], 2)
            for t in range(NT):
                n = ROWS[t]
                step(a(junk[0:n], x_sb[0:n, t, :], ACT.Square, accum_out=stat[0:n, 0, t:t + 1]))
            for t in range(NT):
                n = ROWS[t]
                a(stat[0:n, 1, t:t + 1], stat[0:n, 0, t:t + 1], ACT.Sqrt, bias=epsc[0:n, :], scale=1.0 / D).then_inc(S["rt_done"], 1)

            def evac_hT(t, s_t, s_ready):
                act.wait_ge(S[s_t], t + 1)
                for k in range(2):
                    n = ROWS[t]
                    src = ps[4 + 2 * (t % 2) + k][:, :].rearrange("p (c q) -> p c q", c=4)[:, :, 0:n]
                    a(hT[:, 4 * k:4 * k + 4, t * P:t * P + n], src, ACT.Copy).then_inc(S[s_ready], 1)

            evac_hT(0, "hT_t", "hT_ready")
            evac_hT(1, "hT_t", "hT_ready")
            def head_a(h):
                if h < H:
                    act.wait_ge(S["wm"], h + 1)
                    for c in range(NCH):
                        a(wi[:, c, :], wi[:, c, :], ACT.Exp, bias=cols[:, c, 0, h:h + 1], scale=-1.0)
                    a(wi_s, wi_s, ACT.Exp, bias=cols[0:NS, NCH, 0, h:h + 1], scale=-1.0).then_inc(S["wexp"], 1)
                act.wait_ge(S["mixA"], h + 1)
                if h >= 1:
                    act.wait_ge(S["s_nc"], h)
                for c in range(NCH):
                    col = cols[:, c, 3, h:h + 1] if h < H else cst["kw"][:, h - H:h - H + 1]
                    i = a(kwr[:, c, :], ps[2][:, c * P:(c + 1) * P], ACT.Copy, scale=col)
                i.then_inc(S["kwa"], 1)

            for u, (kind, nm, bi, c) in enumerate(UNITS):
                if u == 0:
                    act.wait_ge(S["modA"], 4)
                if u + 2 < NT:
                    evac_hT(u + 2, "hT_t", "hT_ready")
                if u == UG:
                    act.wait_ge(S["cols_ready"], 1)
                    act.wait_ge(S["st_cv"], 32)
                    head_a(0)
                if u == UQ:
                    act.wait_ge(S["mod_st"], 32)
                act.wait_ge(S["proj_mm"], u + 1)
                A0, A1 = unit_banks(u)
                if kind == "gate":
                    dst = GR["li" if c == 0 else "fx"]
                    act.wait_ge(S["ld_small"], 16 * 10)
                    a(dst[:, 0:TH], A0[0:H, 0:TH], ACT.Identity, bias=bgate[:, c:c + 1])
                    a(dst[:, TH:T], A1[0:H, 0:TH], ACT.Identity, bias=bgate[:, c:c + 1]).then_inc(S["proj_evac"], 1)
                elif kind == "tok":
                    h0 = 0 if nm == "mv" else H
                    n = ROWS[c]
                    a(vv[0:n, c, h0:h0 + H, 0:DH], A0[0:n, :].rearrange("p (h d) -> p h d", h=H), ACT.Copy).then_inc(S["proj_evac"], 1)
                elif nm[:2] == "qk":
                    ch = c + 4 * int(nm[2])
                    a(qk[:, ch, CW - 1:CW - 1 + TH], A0[:, 0:TH], ACT.Copy)
                    a(qk[:, ch, CW - 1 + TH:PADP], A1[:, 0:SEQ - TH], ACT.Copy)
                    a(qk[:, ch, PADP:QW].rearrange("p (b l) -> p b l", b=NB)[:, :, CW - 1:PADS],
                      A1[:, SEQ - TH:TH].rearrange("p (b l) -> p b l", b=NB), ACT.Copy).then_inc(S["proj_evac"], 1)
                else:
                    dst, f = {"mo": (gate[:, c, :], ACT.Sigmoid), "rg": (gate[:, H + c, :], ACT.Silu),
                              "rq": (rqk[:, c, :], ACT.Copy), "rk": (rqk[:, H + c, :], ACT.Copy)}[nm]
                    a(dst[:, 0:TH], A0[:, 0:TH], f)
                    a(dst[:, TH:T], A1[:, 0:TH], f).then_inc(S["proj_evac"], 1)
                if UQ < u <= UQ + 2 * H:
                    ch = u - UQ - 1
                    act.wait_ge(S["conv_acc"], ch + 1)
                    a(qk[:, ch, 0:T], acc[:, ch % 2, :], ACT.Silu).then_inc(S["conv_silu"], 1)
                if u == UEND["g"] + 1:
                    act.wait_ge(S["g_ax"], 1)
                    step(a(GR["u"], GR["u"], ACT.Exp, scale=-1.0))
                    a(GR["u"], GR["u"], ACT.Ln, bias=1.0).then_inc(S["g_ln"], 1)
                if u == UEND["mo"] + 1:
                    act.wait_ge(S["g_t"], 1)
                    a(woldr[:, 0:NCH], GR["li"][:, P - 1:SEQ:P], ACT.Exp)
                    a(woldr[:, NCH:NCH + NB], GR["li"][:, SEQ + LB - 1::LB], ACT.Exp).then_inc(S["g_exp"], 1)
                    a(rowst[32:32 + H, :], GR["li"], ACT.Exp).then_inc(S["g_exp"], 1)
                    a(rowst[64:64 + H, :], GR["fx"], ACT.Exp, scale=-1.0).then_inc(S["g_exp"], 1)
                    a(rowst[96:96 + H, :], GR["b"], ACT.Exp).then_inc(S["g_exp"], 1)
                if u == UEND["rk"]:
                    act.wait_ge(S["xc_t"], 1)
                    for k in range(2):
                        i = a(cv_out[:, k * 512:(k + 1) * 512], ps[6 + k][0:NCV, :], ACT.Copy)
                    i.then_inc(S["cvo_ready"], 1)
            def root(h):
                act.wait_ge(S["nrm_v"], h + 1)
                a(hstat[:, 2, :], hstat[:, 1, :], ACT.Sqrt, bias=epsc[:, :]).then_inc(S["nrm_s"], 1)

            def head_c(h):
                w = DH + 1 if h < H else DH
                for c in range(1, NCH):
                    act.wait_ge(S["o2"], h * (NCH - 1) + c)
                    act.wait_ge(S["nchunk"], h * NCH + c)
                    col = cols[:, c, 1, h:h + 1] if h < H else cst["inter"][:, h - H:h - H + 1]
                    a(inter_t[:, c % 2, 0:w], ps[6 + c % 2][:, 0:w], ACT.Copy, scale=col).then_inc(S["o2a"], 1)
                    if c == 1 and h >= 1:
                        root(h - 1)
                act.wait_ge(S["so2"], h + 1)
                act.wait_ge(S["nchunk"], h * NCH + NCH)
                col = cols[0:NS, NCH, 1, h:h + 1] if h < H else cst["inter_s"][:, h - H:h - H + 1]
                a(inter_t[0:NS, 0, 0:w], ps[6][0:NS, 0:w], ACT.Copy, scale=col).then_inc(S["so2a"], 1)

            for h in range(2 * H):
                head_c(h)
                if h + 1 < 2 * H:
                    head_a(h + 1)
            root(2 * H - 1)
            for t in range(NT):
                n = ROWS[t]
                act.wait_ge(S["y_mm"], t + 1)
                step(a(junk2[0:n, 0:512], ps[y_banks(t)[0]][0:n, :], ACT.Square, accum_out=stat[0:n, 2, t:t + 1]))
                a(junk2[0:n, 512:D], ps[y_banks(t)[1]][0:n, :], ACT.Square, accum_out=stat[0:n, 3, t:t + 1]).then_inc(S["y_ss"], 1)
                act.wait_ge(S["y_s2"], t + 1)
                a(stat[0:n, 5, t:t + 1], stat[0:n, 4, t:t + 1], ACT.Sqrt, bias=epsc[0:n, :], scale=1.0 / D).then_inc(S["y_rt"], 1)
                act.wait_ge(S["x1_done"], t + 1)
                step(a(junk2[0:n], x_sb[0:n, t, :], ACT.Square, accum_out=stat[0:n, 7, t:t + 1]))
                a(stat[0:n, 8, t:t + 1], stat[0:n, 7, t:t + 1], ACT.Sqrt, bias=epsc[0:n, :], scale=1.0 / D).then_inc(S["y_rt2"], 1)
                evac_hT(t, "h2T_t", "h2T_ready")
            act.wait_ge(S["rl_mm"], 1)
            act.wait_ge(S["st_out"], 16 * NST)
            a(smat[:, 0:NCH, :], ps[0][:, 0:NCH * NE].rearrange("p (t e) -> p t e", t=NCH), ACT.Sigmoid)
            a(smat[0:NS, NCH, :], ps[0][0:NS, NCH * NE:NT * NE], ACT.Sigmoid).then_inc(S["rl_sig"], 1)

            def sh_silu(t):
                n = ROWS[t]
                act.wait_ge(S["gu_mm"], t + 1)
                if t >= 1:
                    act.wait_ge(S["hh_ready"], t)
                a(sg[0:n], ps[3 - 2 * (t % 2)][0:n, 0:FE], ACT.Silu).then_inc(S["gu_silu"], 1)

            sh_silu(0)
            for t in range(NT):
                n = ROWS[t]
                if t + 1 < NT:
                    sh_silu(t + 1)
                act.wait_ge(S["hhT_t"], t + 1)
                hv = hhT.rearrange("p (j q) -> p j q", j=FJ)
                pv = ps[0][:, 0:FJ * P].rearrange("p (j q) -> p j q", j=FJ)
                a(hv[:, :, 0:n], pv[:, :, 0:n], ACT.Copy).then_inc(S["hhT_ready"], 1)
                act.wait_ge(S["dn_mm"], t + 1)
                a(shout[0:n, t, 0:512], ps[4][0:n, :], ACT.Copy)
                a(shout[0:n, t, 512:D], ps[5][0:n, :], ACT.Copy).then_inc(S["dn_evac"], 1)

            def xT_evac(n, j, s=None):
                act.wait_ge(S["xgT_t"], n + 1)
                a(xT[:, j % 2, 0:4 * BLK], ps[0][:, :], ACT.Copy).then_inc(S["xgT_a"], 1)

            def body(n, j, ahead, s=None):
                act.wait_ge(S["egate"], n + 1)
                a(sg, ps[2][:, 0:FE], ACT.Silu).then_inc(S["egs"], 1)
                for k in range(FJ):
                    act.wait_ge(S["ehT_t"], FJ * n + (k + 1))
                    a(hhT[:, k * BLK:(k + 1) * BLK], ps[3 - k][:, 0:BLK], ACT.Copy).then_inc(S["ehT"], 1)
                xT_evac(n + 1, j + 1)
                act.wait_ge(S["edn"], n + 1)
                if not (isinstance(n, int) and n < 2):
                    act.wait_ge(S[f"sct{j % 2}"], scount(n, j, s) - 16)
                a(yo[:, j % 2, 0:512], ps[4][:, :], ACT.Copy).then_inc(S["eout_a"], 1)

            xT_evac(0, 0)
            ladder(act, body)
            for t in range(NT):
                n = ROWS[t]
                act.wait_ge(S["yl_sum"], t + 1)
                step(a(yo[0:n, 1, :], yo[0:n, 0, :], ACT.Square, accum_out=stat[0:n, 10, t:t + 1]))
                a(stat[0:n, 11, t:t + 1], stat[0:n, 10, t:t + 1], ACT.Sqrt, bias=epsc[0:n, :], scale=1.0 / D).then_inc(S["yf_rt"], 1)

        @block.tensor
        def _(pe):
            mm, tr = pe.matmul, pe.transpose
            pe.wait_ge(S["ld_id"], 16)
            pe.wait_ge(S["c_silu"], 1)
            cv = crow.rearrange("p (q c) -> p c q", c=KC)
            for c in range(KC):
                i = tr(ps[7][:, 16 * c:16 * c + NCOND], cv[:, c, :], ident[0:NCOND, 0:NCOND])
            i.then_inc(S["cT_t"], 1)
            def ring_wait(n):
                pe.wait_ge(S[f"ld_w{n % 2}"], 16 * (n // 2 + 1))
                return ring[:, n % 2, :].rearrange("p (c f) -> p c f", c=KC)

            def rows_T(src, t, s_t):
                n = ROWS[t]
                for c in range(KC):
                    i = tr(ps[4 + 2 * (t % 2) + c // 4][:, (c % 4) * P:(c % 4) * P + n], src[0:n, t % 2, c * P:(c + 1) * P],
                           ident[0:n, 0:n])
                i.then_inc(S[s_t], 1)

            def h_T(t):
                pe.wait_ge(S["h_ready"], t + 1)
                if t >= 2:
                    pe.wait_ge(S["hT_ready"], 2 * (t - 1))
                rows_T(hrow, t, "hT_t")

            pe.wait_ge(S["cT_ready"], 1)
            for g in range(NADA):
                w = ring_wait(g)
                if g >= 2:
                    pe.wait_ge(S["mod_evac"], g - 1)
                for c in range(KC):
                    i = mm(ps[g % 2][0:NCOND, :], cTs[:, c, 0:NCOND], w[:, c, :], start=c == 0, stop=c == KC - 1)
                i.then_inc(S["ring_used"], 1)
                if g == 2:
                    pe.wait_ge(S["ld_small"], 160)
                    tr(ps[5][:, 0:NB * H], n_in[:, :], ident[0:NB * H, 0:NB * H]).then_inc(S["nin_t"], 1)
                    pe.wait_ge(S["ld_cv"], 16)
                    for c in range(2 * H):
                        i = tr(ps[6][:, 24 * c:24 * c + 24], cv_in[:, c * P:(c + 1) * P], ident[0:24, 0:24])
                    i.then_inc(S["nin_t"], 1)
                if g == 9:
                    pe.wait_ge(S["cv_pad"], 1)
                    h_T(0)
                    h_T(1)

            def QK(h):
                return (qk[:, h, 0:T], qk[:, H + h, 0:T]) if h < H else (rqk[:, h - H, :], rqk[:, h, :])

            def scores(h):
                q, k = QK(h)
                if h == H:
                    pe.wait_ge(S["rot_done"], 2 * H)
                for c in range(NCH):
                    mm(ps[1][:, c * P:(c + 1) * P], k[:, c * P:(c + 1) * P], q[:, c * P:(c + 1) * P], start=True, stop=True)

            def key_rows(h):
                _, k = QK(h)
                for c in range(NCH):
                    tr(ps[2][:, c * P:(c + 1) * P], k[:, c * P:(c + 1) * P], ident[:, :])

            def head_a(h):
                q, k = QK(h)
                if h >= 2:
                    pe.wait_ge(S["ynT_ready"], 2 * (h - 1))
                if h < H:
                    mm(ps[0][:, :], cst["sel"][:, h, :], GR["m"][:, 0:SEQ], start=True, stop=True)
                    mm(ps[3][0:NS, 0:NS], cst["sel"][:, h, 0:NS], GR["m"][:, SEQ:T], start=True, stop=True)
                mm(ps[3][0:NS, NS:2 * NS], k[:, SEQ:T], q[:, SEQ:T], start=True, stop=True)
                tr(ps[3][0:NS, P:2 * P], k[:, SEQ:T], ident[:, :]).then_inc(S["mixA"], 1)

            def chunks(h):
                q, k = QK(h)
                w = DH + 1 if h < H else DH
                if h >= 1:
                    pe.wait_ge(S["sdu"], h * NB)
                pe.wait_ge(S["stm"], h + 1)
                pe.wait_ge(S["kwa"], h + 1)
                for c in range(NCH):
                    o1 = ps[4 + c % 2]
                    if c >= 2:
                        pe.wait_ge(S["nchunk"], h * NCH + c - 1)
                    mm(o1[:, 0:w], sT[:, c, :], vv[:, c, h, 0:w], start=True, stop=True)
                    mm(o1[:, 256:256 + w], kwr[:, c, :], vv[:, c, h, 0:w], start=True, stop=True).then_inc(S["o1d"], 1)
                    if c >= 1:
                        pe.wait_ge(S["nchunk"], h * NCH + c)
                        st = prC[:, h, 0:w] if h < H else prS[:, h - H, :]
                        mm(ps[6 + c % 2][:, 0:w], q[:, c * P:(c + 1) * P], st, start=True, stop=True).then_inc(S["o2"], 1)
                    if h + 1 < 2 * H:
                        if c == 1:
                            scores(h + 1)
                        if c == 2:
                            key_rows(h + 1)

            def samples(h):
                w = DH + 1 if h < H else DH
                pe.wait_ge(S["q8_ready"], h + 1)
                if h == 0:
                    pe.wait_ge(S["ld_stC"], 16 * NB)
                    pe.wait_ge(S["n_cols"], 1)
                if h == H:
                    pe.wait_ge(S["ld_stS"], 16 * NB)
                pe.wait_ge(S["nchunk"], h * NCH + NCH)
                mm(ps[4][0:NS, 0:w], sT_s, vv[0:NS, NCH, h, 0:w], start=True, stop=True).then_inc(S["so1"], 1)
                for b in range(NB):
                    st = stC[:, b, h, 0:w] if h < H else stS[:, b, h - H, :]
                    i = mm(ps[6][0:NS, 0:w], q8[:, b, :], st, start=b == 0, stop=b == NB - 1)
                i.then_inc(S["so2"], 1)

            def deltas(h):
                w = DH + 1 if h < H else DH
                pe.wait_ge(S["s_nc"], h + 1)
                for b in range(NB):
                    if b >= 4:
                        pe.wait_ge(S["sdu"], h * NB + b - 3)
                    mm(ps[4 + b % 4][:, 0:w], kw8[:, b, :], vv[0:NS, NCH, h, 0:w], start=True, stop=True).then_inc(S["sdb"], 1)

            def out_T(h):
                pe.wait_ge(S["yn_ready"], h + 1)
                for t in range(NT):
                    n = ROWS[t]
                    bk, o = (ps[0], t * P) if t < NCH else (ps[3], 256)
                    i = tr(bk[:, o:o + n], yn[0:n, t, :], ident[0:n, 0:n])
                i.then_inc(S["yn_t"], 1)

            pe.wait_ge(S["mod_evac"], NADA)
            for u, (kind, nm, bi, c) in enumerate(UNITS):
                if u == UG:
                    pe.wait_ge(S["cols_ready"], 1)
                    pe.wait_ge(S["cvo_ready"], 1)
                    pe.wait_ge(S["proj_evac"], UG)
                    scores(0)
                    key_rows(0)
                    head_a(0)
                if u < NT:
                    if u + 2 < NT:
                        h_T(u + 2)
                    pe.wait_ge(S["hT_ready"], 2 * (u + 1))
                w = ring_wait(NADA + bi) if kind != "gate" else None
                A0, A1 = unit_banks(u)
                if u >= 2:
                    pe.wait_ge(S["proj_evac"], u - 1)
                if kind == "tok":
                    n = ROWS[c]
                    for k in range(KC):
                        i = mm(A0[0:n, :], hT[:, k, c * P:c * P + n], w[:, k, :], start=k == 0, stop=k == KC - 1)
                else:
                    if kind == "gate":
                        pe.wait_ge(S["ld_wg"], 16)
                    for k in range(KC):
                        st = w[:, k, c * P:(c + 1) * P] if kind == "chan" else wgate[:, k, c * H:(c + 1) * H]
                        m = P if kind == "chan" else H
                        mm(A0[0:m, 0:TH], st, hT[:, k, 0:TH], start=k == 0, stop=k == KC - 1)
                        i = mm(A1[0:m, 0:TH], st, hT[:, k, TH:T], start=k == 0, stop=k == KC - 1)
                i.then_inc(S["proj_mm"], 1)
                if u == UEND["rq"]:
                    pe.wait_ge(S["conv_acc"], 2 * H)
                    for c in range(2 * H):
                        i = tr(ps[6 + c // 4][0:NCV, (c % 4) * P:(c % 4 + 1) * P], xc[:, c, :], ident[:, :])
                    i.then_inc(S["xc_t"], 1)
                    pe.wait_ge(S["g_exp"], 4)
                    pe.wait_ge(S["ld_const"], 16 * (len(CONSTS) - 1))
                    for t in range(NT):
                        n = ROWS[t]
                        i = tr(ps[4 + t // NCH][0:n, (t % NCH) * P:(t % NCH + 1) * P], rowst[:, t * P:t * P + n], ident[:, :])
                    for h in range(H):
                        i = mm(ps[5][:, 256 + 16 * h:256 + 16 * h + NCH + NB], cst["sel"][:, h, :], woldr[:, :], start=True, stop=True)
                    i.then_inc(S["cols_t"], 1)
            pe.wait_ge(S["proj_evac"], NU)
            for h in range(2 * H):
                chunks(h)
                samples(h)
                pe.wait_ge(S["stq"], h + 1)
                if h >= 1:
                    out_T(h - 1)
                if h == H:
                    pe.wait_ge(S["n_cols"], 2)
                    tr(ps[7][0:(1 + NB) * H, 0:DH], n_col[:, :], ident[:, :]).then_inc(S["n_cols_t"], 1)
                    pe.wait_ge(S["n_out_ready"], 1)
                if h + 1 < 2 * H:
                    head_a(h + 1)
                deltas(h)
            def y_mm(t, heads=range(2 * H)):
                n = ROWS[t]
                if t >= 2:
                    pe.wait_ge(S["x1_done"], t - 1)
                for hf in range(2):
                    for k in heads:
                        i = mm(ps[y_banks(t)[hf]][0:n, :], yT(k)[:, t * P:t * P + n],
                               (woA if k < H else woB)[:, k % H, hf * 512:(hf + 1) * 512], start=k == 0, stop=k == 2 * H - 1)
                if heads[-1] == 2 * H - 1:
                    i.then_inc(S["y_mm"], 1)

            pe.wait_ge(S["ld_woA"], 16)
            y_mm(0, range(H))
            out_T(2 * H - 1)
            pe.wait_ge(S["ynT_ready"], 4 * H)
            pe.wait_ge(S["sdu"], 2 * H * NB)
            pe.wait_ge(S["ld_woB"], 16)
            y_mm(0, range(H, 2 * H))

            def router(t):
                n = ROWS[t]
                for k in range(KC):
                    i = mm(ps[0][0:n, t * NE:(t + 1) * NE], hT[:, k, t * P:t * P + n], wr[:, k, :], start=k == 0, stop=k == KC - 1)
                return i

            def shared_up(t):
                n = ROWS[t]
                if t == 0:
                    pe.wait_ge(S["ld_ws"], 32)
                if t == 1:
                    pe.wait_ge(S["x1_done"], NT)
                if t >= 2:
                    pe.wait_ge(S["hh_ready"], t - 1)
                for k in range(KC):
                    i = mm(ps[3 - 2 * (t % 2)][0:n, :].rearrange("p (m f) -> p m f", m=2), hT[:, k, t * P:t * P + n], gu_s[:, :, k, :],
                           start=k == 0, stop=k == KC - 1)
                i.then_inc(S["gu_mm"], 1)

            def shared_T(t):
                n = ROWS[t]
                pe.wait_ge(S["hh_ready"], t + 1)
                for jj in range(FJ):
                    i = tr(ps[0][:, jj * P:jj * P + n], hh[0:n, jj * P:(jj + 1) * P], ident[0:n, 0:n])
                i.then_inc(S["hhT_t"], 1)

            def shared_down(t):
                n = ROWS[t]
                pe.wait_ge(S["hhT_ready"], t + 1)
                if t == 0:
                    pe.wait_ge(S["ld_wsd"], 16)
                else:
                    pe.wait_ge(S["dn_evac"], t)
                for hf in range(2):
                    for jj in range(FJ):
                        i = mm(ps[4 + hf][0:n, :], hhT[:, jj * P:jj * P + n], dn_s[:, jj, hf * 512:(hf + 1) * 512],
                               start=jj == 0, stop=jj == FJ - 1)
                i.then_inc(S["dn_mm"], 1)

            def positions():
                pe.wait_ge(S["msk_ready"], NT)
                for t in range(NT):
                    n = ROWS[t]
                    o = ps[6][0:n, t * NE:(t + 1) * NE]
                    for tt in range(t):
                        mm(o, ones[:, 0:n], maskm[:, tt, :], start=tt == 0, stop=False)
                    mm(o, cst["tri"][0:n, 0:n], maskm[0:n, t, :], start=t == 0, stop=True)
                for t in range(NT):
                    n = ROWS[t]
                    i = mm(ps[6][:, NT * NE:(NT + 1) * NE], ones[0:n, :], maskm[0:n, t, :], start=t == 0, stop=t == NT - 1)
                i.then_inc(S["pos_mm"], 1)

            for t in range(NT):
                if t + 1 < NT:
                    y_mm(t + 1)
                else:
                    pe.wait_ge(S["h2T_ready"], 2 * (NT - 1))
                    pe.wait_ge(S["ld_wr"], 16)
                    pe.wait_ge(S["x1_done"], NT - 1)
                    for r in range(NT - 1):
                        router(r)
                    shared_up(0)
                pe.wait_ge(S["h2_ready"], t + 1)
                if t >= 2:
                    pe.wait_ge(S["h2T_ready"], 2 * (t - 1))
                rows_T(hrow2, t, "h2T_t")
            pe.wait_ge(S["h2T_ready"], 2 * NT)
            router(NT - 1).then_inc(S["rl_mm"], 1)
            shared_up(1)
            def find_idx(n, j, part=range(NT)):
                if part[0] == 0:
                    pe.wait_ge(S["P_ready"], n + 1)
                    if not (isinstance(n, int) and n == 0):
                        pe.wait_ge(S["idx_ready"], n)
                    else:
                        pe.wait_ge(S["pos_done"], 1)
                for tt in part:
                    k = ROWS[tt]
                    pm, at_ = Pm[0:k, j % 2, tt * BLK:(tt + 1) * BLK], tt * 8
                    mm(ps[6][:, 0:3], pm, Re[0:k, j % 2, at_:at_ + 3], start=tt == 0, stop=False)
                    mm(ps[6][:, 0:3], pm, Re[0:k, j % 2, at_ + 3:at_ + 6], start=False, stop=False)
                    i = mm(ps[6][:, 1:2], pm, Re[0:k, j % 2, at_ + 6:at_ + 7], start=False, stop=tt == NT - 1)
                if part[-1] == NT - 1:
                    i.then_inc(S["idx_mm"], 1)

            def x_T(n, j, s=None):
                jj = j % 2
                pe.wait_ge(S[f"gat{jj}"], scount(n, j, s))
                if not (isinstance(n, int) and n == 0):
                    pe.wait_ge(S["xgT_a"], n)
                    pe.wait_ge(S["xgT_d"], n)
                for c in range(KC):
                    i = tr(ps[c // 4][:, (c % 4) * BLK:(c % 4 + 1) * BLK], xg[:, jj, c * P:(c + 1) * P], ident[:, :])
                i.then_inc(S["xgT_t"], 1)

            def body(n, j, ahead, s=None):
                jj = j % 2
                gu, dn = wview(jj)
                pe.wait_ge(S["xgT_a"], n + 1)
                pe.wait_ge(S["xgT_d"], n + 1)
                pe.wait_ge(S[f"ld_g{jj}"], scount(n, j, s))
                pe.wait_ge(S[f"ld_u{jj}"], scount(n, j, s))
                if not (isinstance(n, int) and n == 0):
                    pe.wait_ge(S["ehh"], FJ * n)
                for m, (bank, done) in enumerate(((ps[2], "egate"), (ps[7], "egu"))):
                    for c in range(KC):
                        i = mm(bank[:, 0:FE], xT[:, jj, c * BLK:(c + 1) * BLK], gu[:, m, c, :], start=c == 0, stop=c == KC - 1)
                    i.then_inc(S[done], 1)
                x_T(n + 1, j + 1, s if s is None else s + 1)
                find_idx(n + 2, j + 2, range(1))
                for k in range(FJ):
                    pe.wait_ge(S["ehh"], FJ * n + (k + 1))
                    tr(ps[3 - k][:, 0:BLK], hh[:, k * P:(k + 1) * P], ident[:, :]).then_inc(S["ehT_t"], 1)
                find_idx(n + 2, j + 2, range(1, NT))
                pe.wait_ge(S[f"ld_d{jj}"], scount(n, j, s))
                if isinstance(n, int) and n == 0:
                    pe.wait_ge(S["dn_evac"], NT)
                else:
                    pe.wait_ge(S["eout_a"], n)
                    pe.wait_ge(S["eout_d"], n)
                for k in range(FJ):
                    pe.wait_ge(S["ehT"], FJ * n + (k + 1))
                    for hf in range(2):
                        i = mm(ps[4 + hf][:, :], hhT[:, k * BLK:(k + 1) * BLK], dn[:, k, hf * 512:(hf + 1) * 512],
                               start=k == 0, stop=k == FJ - 1)
                i.then_inc(S["edn"], 1)

            for t in range(NT):
                shared_T(t)
                if t == NT - 3:
                    positions()
                if t + 2 < NT:
                    shared_up(t + 2)
                if t == NT - 2:
                    find_idx(0, 0)
                    find_idx(1, 1)
                if t == NT - 1:
                    pe.wait_ge(S["hhT_ready"], NT)
                    x_T(0, 0)
                shared_down(t)
            ladder(pe, body)
            for t in range(NT):
                n = ROWS[t]
                pe.wait_ge(S[f"yl{t % 2}"], 16 * (t // 2 + 1))
                if t >= 2:
                    pe.wait_ge(S["yl_sum"], t - 1)
                for hf in range(2):
                    parts = [shout[0:n, t, hf * 512:(hf + 1) * 512]] + \
                        [ycomb[0:n, t % 2, k * D + hf * 512:k * D + (hf + 1) * 512] for k in range(KPE)]
                    for k, y in enumerate(parts):
                        i = mm(ps[2 * (t % 2) + hf][0:n, :], ident[0:n, 0:n], y, start=k == 0, stop=k == KPE)
                i.then_inc(S["yp_mm"], 1)

        @block.vector
        def _(dve):
            def step(ins):
                step.n += 1
                ins.then_inc(S["dch"], 1)
                dve.wait_ge(S["dch"], step.n)
            step.n = 0
            tt_, ts, stt, cp = dve.tensor_tensor, dve.tensor_scalar, dve.scalar_tensor_tensor, dve.tensor_copy
            dve.wait_ge(S["cT_t"], 1)
            cp(cTs[:, :, 0:NCOND], ps[7][:, 0:16 * KC].rearrange("p (c n) -> p c n", c=KC)[:, :, 0:NCOND]).then_inc(S["cT_ready"], 1)
            dve.memset(cols[:, :, :, :], 1.0)
            dve.wait_ge(S["ld_bg"], 16 * 5)
            def by_chunk(rows):
                return rows.rearrange("p (c q) -> p q c", c=KC)

            def h_row(t):
                n, o = ROWS[t], int(t == NCH)
                if t >= 1:
                    dve.wait_ge(S["h_ready"], t)
                step(stt(junk[0:n], x_sb[0:n, t, :], stat[0:n, 2, t:t + 1], bcA[0:n, 0, o, :], ALU.mult, ALU.mult))
                if t >= 2:
                    dve.wait_ge(S["hT_t"], t - 1)
                tt_(by_chunk(hrow[0:n, t % 2, :]), junk[0:n].rearrange("p (q c) -> p q c", c=KC),
                    bcA[0:n, 1, o, :].rearrange("p (q c) -> p q c", c=KC), ALU.add).then_inc(S["h_ready"], 1)

            MODF = mod.rearrange("p a b -> p (a b)")
            for g in range(NADA):
                dve.wait_ge(S["ring_used"], g + 1)
                sl = MODF[:, g * 512:(g + 1) * 512]
                tt_(sl, sl, ps[g % 2][0:NCOND, :], ALU.add).then_inc(S["mod_evac"], 1)
                if g == 2:
                    dve.wait_ge(S["nin_t"], 2)
                    cp(n_col[:, 0:NB * H], ps[5][:, 0:NB * H])
                    cp(cvbuf[:, :], ps[6][:, 0:2 * H * 24]).then_inc(S["cv_pad"], 1)
                if g == 8:
                    dve.wait_ge(S["mod_ld1"], 2 * SPREAD)
                    dve.wait_ge(S["rt_done"], NT)
                    step(dve.reciprocal(stat[:, 2, 0:NCH], stat[:, 1, 0:NCH]))
                    step(dve.reciprocal(stat[0:NS, 2, NCH:NT], stat[0:NS, 1, NCH:NT]))
                    h_row(0)
                    h_row(1)
                if g == 10:
                    h_row(2)
                    h_row(3)
                if g == 3:
                    dve.wait_ge(S["mod_evac"], g + 1)
                    stt(mod[:, 1, :], mod[:, 1, :], 1.0, g4[:, 0, :], ALU.add, ALU.mult).then_inc(S["modA"], 1)
            dve.wait_ge(S["mod_evac"], NADA)
            tt_(mod[:, 2, :], mod[:, 2, :], g4[:, 1, :], ALU.mult).then_inc(S["modA"], 1)
            stt(mod[:, 4, :], mod[:, 4, :], 1.0, g4[:, 2, :], ALU.add, ALU.mult).then_inc(S["modA"], 1)
            tt_(mod[:, 5, :], mod[:, 5, :], g4[:, 3, :], ALU.mult).then_inc(S["modA"], 1)

            h_row(4)
            dve.wait_ge(S["mod_st"], 32)
            dve.wait_ge(S["h_ready"], NT)
            step(dve.memset(qk[:, :, 0:CW - 1], 0.0))
            for b in range(NB):
                i = cp(qk[:, :, PADP + b * PADS:PADP + b * PADS + CW - 1],
                       cvbuf[:, :].rearrange("p (c b w) -> p c b w", c=2 * H, b=NB)[:, :, b, :])
            step(i)
            step(dve.memset(vv[:, :, :, DH:DH + 1], 1.0))
            for ch in range(2 * H):
                dve.wait_ge(S["proj_evac"], UQ + ch + 1)
                last = QW - NB * PADS
                step(cp(xc[:, ch, 0:CW - 1], qk[:, ch, SEQ:PADP]))
                step(cp(xc[:, ch, CW - 1:NCV].rearrange("p (b w) -> p b w", b=NB),
                        qk[:, ch, PADP:QW].rearrange("p (b l) -> p b l", b=NB)[:, :, LB:PADS]))
                if ch >= 2:
                    dve.wait_ge(S["conv_silu"], ch - 1)
                ap, as_ = acc[:, ch % 2, 0:SEQ], acc[:, ch % 2, SEQ:T].rearrange("p (b l) -> p b l", b=NB)
                qs = qk[:, ch, PADP:QW].rearrange("p (b l) -> p b l", b=NB)
                for w in range(CW):
                    tap = cwT[:, ch, w:w + 1]
                    xp, xs = qk[:, ch, w:w + SEQ], qs[:, :, w:w + LB]
                    if w == 0:
                        ts(ap, xp, tap, cbT[:, ch:ch + 1], ALU.mult, ALU.add)
                        step(ts(as_, xs, tap, cbT[:, ch:ch + 1], ALU.mult, ALU.add))
                    else:
                        stt(ap, xp, tap, ap, ALU.mult, ALU.add)
                        i = stt(as_, xs, tap, as_, ALU.mult, ALU.add)
                        if w < CW - 1:
                            step(i)
                i.then_inc(S["conv_acc"], 1)
            dve.wait_ge(S["ld_const"], 16 * (len(CONSTS) - 1))
            dve.wait_ge(S["proj_evac"], UEND["g"])
            stt(GR["u"], GR["fx"], -1.0, GR["fx"], ALU.mult, ALU.max).then_inc(S["g_ax"], 1)
            dve.wait_ge(S["g_ln"], 1)
            step(ts(GR["fx"], GR["fx"], 0.0, None, ALU.min))
            step(tt_(GR["u"], GR["fx"], GR["u"], ALU.subtract))
            step(dve.tensor_tensor_scan(GR["b"], cst["seg"][:, :], GR["u"], 0.0, ALU.mult, ALU.add))
            step(tt_(GR["u"], GR["li"], GR["b"], ALU.subtract))
            step(dve.memset(mprev[:, :], 0.0))
            for c in range(NCH):
                cs = slice(c * P, (c + 1) * P)
                step(dve.tensor_tensor_scan(GR["m"][:, cs], GR["u"][:, cs], GR["u"][:, cs], mprev[:, c:c + 1], ALU.max, ALU.max))
                step(tt_(mprev[:, c + 1:c + 2], GR["m"][:, c * P + P - 1:c * P + P], GR["b"][:, c * P + P - 1:c * P + P], ALU.add))
            step(cp(GR["mp"][:, SEQ:T], GR["u"][:, SEQ:T]))
            st0 = GR["mp"][:, SEQ::LB]
            dve.wait_ge(S["ld_small"], 160)
            step(tt_(st0, st0, m_in[:, :], ALU.max))
            step(dve.tensor_tensor_scan(GR["m"][:, SEQ:T], cst["segneg"][:, 0:NS], GR["mp"][:, SEQ:T], 0.0, ALU.add, ALU.max))
            step(cp(GR["mp"][:, 0:SEQ].rearrange("p (c l) -> p c l", c=NCH), mprev[:, 0:NCH].unsqueeze(2).to_broadcast([H, NCH, P])))
            step(cp(GR["mp"][:, SEQ:T].rearrange("p (b l) -> p b l", b=NB), m_in[:, :].unsqueeze(2).to_broadcast([H, NB, LB])))
            step(tt_(GR["fx"], GR["b"], GR["m"], ALU.add))
            step(tt_(GR["li"], GR["mp"], GR["m"], ALU.subtract))
            step(tt_(GR["b"][:, 0:SEQ].rearrange("p (c l) -> p c l", c=NCH), GR["u"][:, 0:SEQ].rearrange("p (c l) -> p c l", c=NCH),
                     GR["m"][:, P - 1:SEQ:P].unsqueeze(2).to_broadcast([H, NCH, P]), ALU.subtract))
            step(tt_(GR["b"][:, SEQ:T].rearrange("p (b l) -> p b l", b=NB), GR["u"][:, SEQ:T].rearrange("p (b l) -> p b l", b=NB),
                     GR["m"][:, SEQ + LB - 1::LB].unsqueeze(2).to_broadcast([H, NB, LB]), ALU.subtract))
            dve.wait_ge(S["hT_t"], NT)
            step(dve.memset(rowst, 0.0))
            step(cp(rowst[0:H, :], GR["u"]))
            dve.memset(q8f, 0.0).then_inc(S["g_t"], 1)
            step(dve.memset(bnag, 1.0))
            dve.wait_ge(S["conv_silu"], 2 * H)
            for i8 in range(2 * H):
                if i8 == H:
                    dve.wait_ge(S["cols_t"], 1)
                    for t in range(NT):
                        n = ROWS[t]
                        src = ps[4 + t // NCH][0:n, (t % NCH) * P:(t % NCH + 1) * P].rearrange("p (k r) -> p k r", k=4)[:, :, 0:H]
                        i = cp(cols[0:n, t, :, :], src)
                    step(i)
                    step(cp(wold_sb[:, :, :], ps[5][:, 256:256 + 16 * H].rearrange("p (h n) -> p h n", h=H)[:, :, 0:NCH + NB]))
                    step(ts(cols[:, 0:NCH, 3, :], cols[:, 0:NCH, 3, :], KSCALE, None, ALU.mult))
                    ts(cols[0:NS, NCH, 3, :], cols[0:NS, NCH, 3, :], KSCALE, None, ALU.mult).then_inc(S["cols_ready"], 1)
                dve.wait_ge(S["proj_evac"], UEND["rq" if i8 < H else "rk"] - H + i8 % H + 1)
                x = rqk[:, i8, :]
                if i8 >= 1:
                    dve.wait_ge(S["rot_done"], i8)
                HF = P // 2
                tt_(rotT[0:HF], x[HF:P], cst["sin"][HF:P, :], ALU.mult)
                step(tt_(rotT[HF:P], x[0:HF], cst["sin"][0:HF, :], ALU.mult))
                step(tt_(x, x, cst["cos"][:, :], ALU.mult))
                tt_(x, x, rotT, ALU.add).then_inc(S["rot_done"], 1)
            def norm_cols():
                dve.wait_ge(S["ld_stC"], 16 * NB)
                cp(stC[:, :, :, DH], n_col[:, 0:NB * H].rearrange("p (b h) -> p b h", b=NB)).then_inc(S["n_cols"], 1)

            def masks(h):
                dve.wait_ge(S["mixA"], h + 1)
                if h < H:
                    tt_(wi, ps[0][:, :].rearrange("p (c l) -> p c l", c=NCH),
                        cst["causal"][:, :].unsqueeze(1).to_broadcast([P, NCH, P]), ALU.add)
                    tt_(wi_s, ps[3][0:NS, 0:NS], cst["causal_s"][:, :], ALU.add).then_inc(S["wm"], 1)

            def scores(h):
                S1 = ps[1][:, :].rearrange("p (c l) -> p c l", c=NCH)
                if h < H:
                    dve.wait_ge(S["wexp"], h + 1)
                    stt(sT, S1, KSCALE, wi, ALU.mult, ALU.mult)
                    stt(sT_s, ps[3][0:NS, NS:2 * NS], KSCALE, wi_s, ALU.mult, ALU.mult).then_inc(S["stm"], 1)
                else:
                    tt_(sT, S1, cst["decay"][:, h - H, :].unsqueeze(1).to_broadcast([P, NCH, P]), ALU.mult)
                    tt_(sT_s, ps[3][0:NS, NS:2 * NS], cst["decay_s"][:, h - H, :], ALU.mult).then_inc(S["stm"], 1)

            def sample_queries(h):
                q = qk[:, h, 0:T] if h < H else rqk[:, h - H, :]
                cp(q8d, q[:, SEQ:T].rearrange("p (b l) -> p b l", b=NB)).then_inc(S["q8_ready"], 1)

            def sample_keys(h):
                col = cols[0:NS, NCH, 3, h:h + 1] if h < H else cst["kw_s"][:, h - H:h - H + 1]
                step(ts(kw_s, ps[3][0:NS, P:2 * P], col, None, ALU.mult))
                tt_(kw8, kw_s.unsqueeze(1).to_broadcast([NS, NB, P]), cst["bmask"][:, :].unsqueeze(2).to_broadcast([NS, NB, P]),
                    ALU.mult).then_inc(S["stq"], 1)

            def chunk(h, c):
                num, w = num2[:, (h % 2) * NT:(h % 2 + 1) * NT, :], DH + 1 if h < H else DH
                o1 = ps[4 + c % 2]
                st = prC[:, h, 0:w] if h < H else prS[:, h - H, :]
                dve.wait_ge(S["o1d"], h * NCH + c + 1)
                if c == 0:
                    cp(st, o1[:, 256:256 + w])
                    cp(num[:, c, 0:w], o1[:, 0:w]).then_inc(S["nchunk"], 1)
                else:
                    dve.wait_ge(S["o2a"], h * (NCH - 1) + c)
                    tt_(num[:, c, 0:w], o1[:, 0:w], inter_t[:, c % 2, 0:w], ALU.add)
                    dec = wold_sb[:, h, c:c + 1] if h < H else cst["gL"][:, h - H:h - H + 1]
                    stt(st, st, dec, o1[:, 256:256 + w], ALU.mult, ALU.add).then_inc(S["nchunk"], 1)

            def samples(h):
                num, w = num2[:, (h % 2) * NT:(h % 2 + 1) * NT, :], DH + 1 if h < H else DH
                dve.wait_ge(S["so1"], h + 1)
                dve.wait_ge(S["so2a"], h + 1)
                tt_(num[0:NS, NCH, 0:w], ps[4][0:NS, 0:w], inter_t[0:NS, 0, 0:w], ALU.add).then_inc(S["s_nc"], 1)

            def deltas(h):
                w = DH + 1 if h < H else DH
                for b in range(NB):
                    dve.wait_ge(S["sdb"], h * NB + b + 1)
                    st = stC[:, b, h, 0:w] if h < H else stS[:, b, h - H, :]
                    dec = wold_sb[:, h, NCH + b:NCH + b + 1] if h < H else cst["gL"][:, H + h - H:H + h - H + 1]
                    stt(st, st, dec, ps[4 + b % 4][:, 0:w], ALU.mult, ALU.add).then_inc(S["sdu"], 1)

            def norm_a(h):
                num = num2[:, (h % 2) * NT:(h % 2 + 1) * NT, :]
                dve.wait_ge(S["s_nc"], h + 1)
                dve.wait_ge(S["nchunk"], (h + 1) * NCH)
                for t in range(NT):
                    n = ROWS[t]
                    i = dve.bn_stats(bnst[0:n, t, :], num[0:n, t, 0:DH])
                step(i)
                for t in range(NT):
                    n = ROWS[t]
                    i = dve.bn_aggr(bnag[0:n, t, :], bnst[0:n, t, :])
                step(i)
                if h < H:
                    step(stt(hstat[:, 0, :], num[:, :, DH], -1.0, num[:, :, DH], ALU.mult, ALU.max))
                    step(tt_(hstat[:, 0, :], hstat[:, 0, :], cols[:, :, 2, h], ALU.max))
                    step(dve.reciprocal(hstat[:, 3, :], hstat[:, 0, :]))
                    step(tt_(hstat[:, 4, :], hstat[:, 3, :], hstat[:, 3, :], ALU.mult))
                    tt_(hstat[:, 1, :], bnag[:, :, 1], hstat[:, 4, :], ALU.mult).then_inc(S["nrm_v"], 1)
                else:
                    cp(hstat[:, 1, :], bnag[:, :, 1]).then_inc(S["nrm_v"], 1)

            def norm_b(h):
                num = num2[:, (h % 2) * NT:(h % 2 + 1) * NT, :]
                dve.wait_ge(S["nrm_s"], h + 1)
                step(dve.reciprocal(hstat[:, 5, :], hstat[:, 2, :]))
                if h < H:
                    step(tt_(hstat[:, 5, :], hstat[:, 5, :], hstat[:, 3, :], ALU.mult))
                for t in range(NT):
                    n = ROWS[t]
                    i = ts(yn[0:n, t, :], num[0:n, t, 0:DH], bnag[0:n, t, 0:1], hstat[0:n, 5, t:t + 1], ALU.subtract, ALU.mult)
                i.then_inc(S["yn_ready"], 1)

            def out_T(h):
                dve.wait_ge(S["yn_t"], h + 1)
                y = yT(h)
                g = gnT[:, h:h + 1]
                stt(y[:, 0:SEQ], ps[0][:, :], g, gate[:, h, 0:SEQ], ALU.mult, ALU.mult).then_inc(S["ynT_ready"], 1)
                stt(y[:, SEQ:T], ps[3][:, 256:256 + NS], g, gate[:, h, SEQ:T], ALU.mult, ALU.mult).then_inc(S["ynT_ready"], 1)

            dve.wait_ge(S["rot_done"], 2 * H)
            step(dve.memset(num2, 0.0))
            dve.wait_ge(S["xc_t"], 1)
            dve.wait_ge(S["st_cv"], 32)
            masks(0)
            scores(0)
            dve.wait_ge(S["proj_evac"], NU)
            for h in range(2 * H):
                chunk(h, 0)
                if h >= 1:
                    norm_a(h - 1)
                chunk(h, 1)
                if h >= 1:
                    norm_b(h - 1)
                chunk(h, 2)
                sample_queries(h)
                for c in range(3, NCH):
                    chunk(h, c)
                sample_keys(h)
                if h == 0:
                    norm_cols()
                samples(h)
                if h >= 1:
                    out_T(h - 1)
                if h == H:
                    dve.wait_ge(S["n_cols_t"], 1)
                    cp(n_out[:, :], ps[7][0:(1 + NB) * H, 0:DH]).then_inc(S["n_out_ready"], 1)
                if h + 1 < 2 * H:
                    masks(h + 1)
                deltas(h)
                if h == H - 1:
                    dve.wait_ge(S["sdu"], NB * H)
                    dve.wait_ge(S["nchunk"], NCH * H)
                    cp(n_col[:, 0:H], prC[:, :, DH])
                    cp(n_col[:, H:].rearrange("p (b h) -> p b h", b=NB), stC[:, :, :, DH]).then_inc(S["n_cols"], 1)
                if h + 1 < 2 * H:
                    scores(h + 1)
            norm_a(2 * H - 1)
            norm_b(2 * H - 1)
            out_T(2 * H - 1)
            dve.wait_ge(S["ld_bc1"], SPREAD)
            for t in range(NT):
                n, o = ROWS[t], int(t == NCH)
                dve.wait_ge(S["y_ss"], t + 1)
                tt_(stat[0:n, 4, t:t + 1], stat[0:n, 2, t:t + 1], stat[0:n, 3, t:t + 1], ALU.add).then_inc(S["y_s2"], 1)
                dve.wait_ge(S["y_rt"], t + 1)
                if t >= 1:
                    dve.wait_ge(S["h2_ready"], t)
                step(dve.reciprocal(stat[0:n, 6, t:t + 1], stat[0:n, 5, t:t + 1]))
                for k in range(2):
                    i = stt(yrow[0:n, k * 512:(k + 1) * 512], ps[y_banks(t)[k]][0:n, :], stat[0:n, 6, t:t + 1],
                            bcC[0:n, o, k * 512:(k + 1) * 512], ALU.mult, ALU.mult)
                step(i)
                tt_(x_sb[0:n, t, :], x_sb[0:n, t, :], yrow[0:n], ALU.add).then_inc(S["x1_done"], 1)
                dve.wait_ge(S["y_rt2"], t + 1)
                step(dve.reciprocal(stat[0:n, 9, t:t + 1], stat[0:n, 8, t:t + 1]))
                dve.wait_ge(S["ld_bc2"], 2 * SPREAD)
                step(stt(yrow[0:n], x_sb[0:n, t, :], stat[0:n, 9, t:t + 1], bcB[0:n, 0, o, :], ALU.mult, ALU.mult))
                if t >= 2:
                    dve.wait_ge(S["h2T_t"], t - 1)
                    dve.wait_ge(S[f"h2_st{t % 2}"], 16 * (t // 2))
                tt_(by_chunk(hrow2[0:n, t % 2, :]), yrow[0:n].rearrange("p (q c) -> p q c", c=KC),
                    bcB[0:n, 1, o, :].rearrange("p (q c) -> p q c", c=KC), ALU.add).then_inc(S["h2_ready"], 1)
            dve.wait_ge(S["ld_br"], 16)
            step(dve.memset(gs12, -MARK))
            step(dve.memset(r8, -MARK))
            tok = cst["tokcol"][:, :].unsqueeze(2).to_broadcast([P, NT, NE])
            step(dve.memset(R[:, :, :, :], 0.0))
            step(cp(R[:, :, :, 0], tok))
            ts(R[:, :, :, 2], R[:, :, :, 0], float(TOPK), None, ALU.mult)
            step(tt_(R[:, :, :, 3], tok, R[:, :, :, 0], ALU.subtract))
            def shared_mul(t):
                n = ROWS[t]
                dve.wait_ge(S["gu_silu"], t + 1)
                if t >= 1:
                    dve.wait_ge(S["hhT_t"], t)
                tt_(hh[0:n], sg[0:n], ps[3 - 2 * (t % 2)][0:n, FE:2 * FE], ALU.mult).then_inc(S["hh_ready"], 1)

            def route(t):
                n = ROWS[t]
                dve.wait_ge(S["rl_sig"], 1)
                s_, sbias, srt, sel_, cum = smat[0:n, t, :], rt[0:n, 0, :], rt[0:n, 1, :], rt[0:n, 2, :], rt[0:n, 3, :]
                step(tt_(sbias, s_, brow[0:n], ALU.add))
                for g in range(NG):
                    i = dve.max(srt[:, g * GSZ:(g + 1) * GSZ], sbias[:, g * GSZ:(g + 1) * GSZ])
                step(i)
                top = srt.rearrange("p (g k) -> p g k", g=NG)
                gs = gs12[0:n, 0, :]
                step(tt_(gs[:, 0:NG], top[:, :, 0], top[:, :, 1], ALU.add))
                step(dve.max(r8[0:n, 0, :], gs[:, 0:NG]))
                step(cp(r8[0:n, 1, 0:4], r8[0:n, 0, 0:4]))
                step(dve.match_replace(gs12[0:n, 1, :], r8[0:n, 1, :], gs, MARK))
                step(ts(r8[0:n, 2, :], gs12[0:n, 1, 0:NG], MARK, None, ALU.is_equal))
                step(ts(r8[0:n, 3, :], r8[0:n, 2, :], BIG, -BIG, ALU.mult, ALU.add))
                step(tt_(sel_.rearrange("p (g k) -> p g k", g=NG), sbias.rearrange("p (g k) -> p g k", g=NG),
                         r8[0:n, 3, :].unsqueeze(2).to_broadcast([n, NG, GSZ]), ALU.add))
                step(dve.max(r8[0:n, 0, :], sel_))
                step(dve.match_replace(cum, r8[0:n, 0, :], sel_, MARK))
                M = maskm[0:n, t, :]
                ts(M, cum, MARK, None, ALU.is_equal).then_inc(S["msk_ready"], 1)
                dve.wait_ge(S["msk_ready"], t + 1)
                step(tt_(sel_, s_, M, ALU.mult))
                step(dve.tensor_reduce(stat[0:n, 12, t:t + 1], sel_, AX.X, ALU.add))
                step(dve.reciprocal(stat[0:n, 13, t:t + 1], stat[0:n, 12, t:t + 1]))
                step(ts(rt[0:n, 4, :], sel_, stat[0:n, 13, t:t + 1], ROUTED, ALU.mult, ALU.mult))
                w_, w1, w2, w3 = rt[0:n, 4, :], R[0:n, t, :, 1], R[0:n, t, :, 4], R[0:n, t, :, 6]
                step(cp(w1, w_))
                step(tt_(w_, w_, w1, ALU.subtract))
                step(cp(w2, w_))
                tt_(w3, w_, w2, ALU.subtract)
                step(dve.tensor_tensor_scan(cum, ones[0:n, 0:NE], M, 0.0, ALU.mult, ALU.add))
                step(ts(cum, cum, -1.0, 1.0, ALU.mult, ALU.add))
                step(stt(R[0:n, t, :, 5], R[0:n, t, :, 3], float(TOPK), cum, ALU.mult, ALU.add))

            for t in range(NT - 2):
                route(t)
                shared_mul(t)
            route(NT - 2)
            route(NT - 1)
            shared_mul(NT - 2)
            dve.wait_ge(S["pos_mm"], 1)
            PV = ps[6][:, 0:(NT + 1) * NE].rearrange("p (t e) -> p t e", t=NT + 1)
            step(stt(pos[:, 0:NCH, :], PV[:, 0:NCH, :], FAR, maskm[:, 0:NCH, :], ALU.add, ALU.mult))
            step(stt(pos[0:NS, NCH, :], PV[0:NS, NCH, :], FAR, maskm[0:NS, NCH, :], ALU.add, ALU.mult))
            step(ts(pos[:, 0:NCH, :], pos[:, 0:NCH, :], -FAR, None, ALU.add))
            step(ts(pos[0:NS, NCH, :], pos[0:NS, NCH, :], -FAR, None, ALU.add))
            cp(ovf[:, 0, :], PV[:, NT, :]).then_inc(S["pos_done"], 1)
            dve.wait_ge(S["pos_done"], 1)

            def table(part):
                cnt, ob = ovf[:, 0, :], ovf[:, 1, :]
                if part == 1:
                    step(dve.tensor_reduce(ovs[:, 0, :], ocmp, AX.X, ALU.add))
                    step(tt_(ocmp, ocmp, ob.unsqueeze(1).to_broadcast([P, NO, NE]), ALU.mult))
                    return
                if part == 2:
                    step(dve.tensor_reduce(ovs[:, 1, :], ocmp, AX.X, ALU.add))
                    step(ts(ovs[:, 2, :], ovs[:, 0, :], float(NE), -FAR, ALU.is_ge, ALU.mult))
                    step(tt_(ovs[:, 1, :], ovs[:, 1, :], iota[:, 0:NO], ALU.subtract))
                    step(ts(ovs[:, 1, :], ovs[:, 1, :], float(BLK), -float(BLK), ALU.mult, ALU.add))
                    step(tt_(negoff[:, :], ovs[:, 1, :], ovs[:, 2, :], ALU.add))
                    ts(etab[:, :], ovs[:, 0, :], float(NE - 1), None, ALU.min).then_inc(S["tab_ready"], 1)
                    return
                step(ts(ob, cnt, float(BLK), None, ALU.is_gt))
                for m in range(2, DEEP):
                    step(stt(ob, cnt, float(BLK * m), ob, ALU.is_gt, ALU.add))
                step(dve.tensor_tensor_scan(cnt, ones[:, 0:NE], ob, 0.0, ALU.mult, ALU.add))
                step(cp(ntab[:, :], cnt[:, NE - 1:NE]))
                s_ = iota[:, 0:NO]
                step(tt_(ocmp, s_.unsqueeze(2).to_broadcast([P, NO, NE]), cnt.unsqueeze(1).to_broadcast([P, NO, NE]), ALU.is_ge))

            def place(n, j, e, off):
                if not (isinstance(n, int) and n < 2):
                    dve.wait_ge(S["idx_mm"], n - 1)
                re_ = Re[:, j % 2, :].rearrange("p (t k) -> p t k", t=NT)
                cp(re_, R[:, :, e, :] if isinstance(e, int) else R[:, :, bass.ds(e, 1), :].rearrange("p t a k -> p t (a k)"))
                for tt in range(NT):
                    k = ROWS[tt]
                    p = pos[0:k, tt, e:e + 1] if isinstance(e, int) else pos[0:k, tt, bass.ds(e, 1)]
                    i = ts(Pm[0:k, j % 2, tt * BLK:(tt + 1) * BLK], iota[0:k, 0:BLK], p,
                           off if isinstance(off, float) else off[0:k], ALU.subtract, ALU.is_equal)
                i.then_inc(S["P_ready"], 1)

            def idx_out(n, j, s=None):
                dve.wait_ge(S["idx_mm"], n + 1)
                q = j % 4
                if not (isinstance(n, int) and n < 4):
                    dve.wait_ge(S[f"sct{j % 2}"], icount(n, j, s))
                ts(idxg[:, q:q + 1], ps[6][:, 0:1], -1.0, float(OOB), ALU.mult, ALU.add)
                cp(wtab[:, q:q + 1], ps[6][:, 1:2])
                ts(idxs[:, q:q + 1], ps[6][:, 2:3], -1.0, float(TOPK * OOB), ALU.mult, ALU.add).then_inc(S["idx_ready"], 1)

            def icount(n, j, s):
                if isinstance(n, int):
                    return 16 * ((n - 4) // 2 + 1)
                if s is None:
                    return (n - j) * 8 + 16 * (j // 2 - 1)
                return (s - j) * 8 + 16 * (NE // 2 + j // 2 - 1)

            def body(n, j, ahead, s=None):
                if s is not None:
                    e = dve.value_load(etab[0:1, bass.ds(s + 2, 1)], min_val=0, max_val=NE - 1)
                    off = negoff[:, bass.ds(s + 2, 1)]
                elif isinstance(ahead, int) and ahead >= NE:
                    a_ = ahead - NE
                    e = dve.value_load(etab[0:1, a_:a_ + 1], min_val=0, max_val=NE - 1)
                    off = negoff[:, a_:a_ + 1]
                else:
                    e, off = ahead, 0.0
                place(n + 2, j, e, off)
                dve.wait_ge(S["egs"], n + 1)
                dve.wait_ge(S["egu"], n + 1)
                if not (isinstance(n, int) and n == 0):
                    dve.wait_ge(S["ehT_t"], FJ * n)
                for k in range(FJ):
                    cs = slice(k * P, (k + 1) * P)
                    stt(hh[:, cs], sg[:, cs], wtab[:, j:j + 1], ps[7][:, k * P:(k + 1) * P],
                        ALU.mult, ALU.mult).then_inc(S["ehh"], 1)
                dve.wait_ge(S["xgT_t"], n + 2)
                cp(xT[:, (j + 1) % 2, 4 * BLK:8 * BLK], ps[1][:, :]).then_inc(S["xgT_d"], 1)
                idx_out(n + 2, j + 2, s if s is None else s + 2)
                if isinstance(n, int) and 1 <= n <= 3:
                    table(n - 1)
                dve.wait_ge(S["edn"], n + 1)
                if not (isinstance(n, int) and n < 2):
                    dve.wait_ge(S[f"sct{j % 2}"], scount(n, j, s) - 16)
                cp(yo[:, j % 2, 512:D], ps[5][:, :]).then_inc(S["eout_d"], 1)

            for n in range(2):
                place(n, n, n, 0.0)
            shared_mul(NT - 1)
            for n in range(2):
                idx_out(n, n)
            dve.wait_ge(S["xgT_t"], 1)
            cp(xT[:, 0, 4 * BLK:8 * BLK], ps[1][:, :]).then_inc(S["xgT_d"], 1)
            dve.wait_ge(S["xgT_d"], 1)
            ladder(dve, body)
            dve.wait_ge(S["ld_bcg"], SPREAD)
            for t in range(NT):
                n, o = ROWS[t], int(t == NCH)
                dve.wait_ge(S[f"yd{t % 2}"], 16 * (t // 2 + 1))
                yc = ycomb[0:n, t % 2, KPE * D:].rearrange("p (k d) -> p d k", k=TOPK - KPE)
                if t >= 1:
                    dve.wait_ge(S["x2_done"], t)
                else:
                    dve.wait_ge(S["sctr"], 1)
                dve.tensor_reduce(yo[0:n, 0, :], yc, AX.X, ALU.add).then_inc(S["yd_sum"], 1)
                dve.wait_ge(S["yd_sum"], t + 1)
                dve.wait_ge(S["yp_mm"], t + 1)
                for hf in range(2):
                    half = yo[0:n, 0, hf * 512:(hf + 1) * 512]
                    i = tt_(half, half, ps[2 * (t % 2) + hf][0:n, :], ALU.add)
                i.then_inc(S["yl_sum"], 1)
                dve.wait_ge(S["yf_rt"], t + 1)
                step(dve.reciprocal(stat[0:n, 12, t:t + 1], stat[0:n, 11, t:t + 1]))
                step(stt(yo[0:n, 0, :], yo[0:n, 0, :], stat[0:n, 12, t:t + 1], bcG[0:n, o, :], ALU.mult, ALU.mult))
                tt_(x_sb[0:n, t, :], x_sb[0:n, t, :], yo[0:n, 0, :], ALU.add).then_inc(S["x2_done"], 1)


def shape_constants():
    import numpy as np
    f = np.float32
    i = np.arange(P)
    k = {"ident": np.eye(P, dtype=f), "iota": np.tile(i.astype(f), (P, 1)), "tri": (i[:, None] < i[None, :]).astype(f)}
    k["causal"] = np.where(i[None, :] >= i[:, None], 0.0, BIG).astype(f)
    s = np.arange(NS)
    same = (s[:, None] // LB == s[None, :] // LB) & (s[None, :] >= s[:, None])
    k["causal_s"] = np.where(same, 0.0, BIG).astype(f)
    lg = np.log1p(-np.exp2(-5.0 - np.arange(H, dtype=f))).astype(f)
    rel = (i[None, :] - i[:, None]).astype(f)
    k["decay"] = np.stack([np.where(rel >= 0, np.exp(np.maximum(rel, 0) * g), 0.0) * KSCALE for g in lg], 1).astype(f)
    rel = (s[None, :] - s[:, None]).astype(f)
    k["decay_s"] = np.stack([np.where(same, np.exp(np.maximum(rel, 0) * g), 0.0) * KSCALE for g in lg], 1).astype(f)
    half = DH // 2
    fr = (f(10000.0) ** (-np.arange(half, dtype=f) / f(half))).astype(f)
    pos = np.concatenate([np.arange(SEQ), 4096 + np.tile(np.arange(LB), NB)]).astype(f)
    ang = (pos[None, :] * fr[:, None]).astype(f).astype(np.float64)
    k["cos"] = np.concatenate([np.cos(ang), np.cos(ang)]).astype(f)
    k["sin"] = np.concatenate([np.sin(ang), -np.sin(ang)]).astype(f)
    sel = np.zeros((H, H, P), f)
    for h in range(H):
        sel[h, h] = 1.0
    k["sel"] = sel
    k["bmask"] = (s[:, None] // LB == np.arange(NB)[None, :]).astype(f)
    k["inter"] = np.exp((i[:, None] + 1.0) * lg[None, :]).astype(f)
    k["inter_s"] = np.exp((s[:, None] % LB + 1.0) * lg[None, :]).astype(f)
    k["kw"] = (np.exp((P - 1.0 - i)[:, None] * lg[None, :]) * KSCALE).astype(f)
    k["kw_s"] = (np.exp((LB - 1.0 - s % LB)[:, None] * lg[None, :]) * KSCALE).astype(f)
    seg = np.ones((H, T), f)
    seg[:, 0:SEQ:P] = 0.0
    seg[:, SEQ::LB] = 0.0
    k["seg"] = seg
    sn = np.zeros((H, NS), f)
    sn[:, ::LB] = -BIG
    k["segneg"] = sn
    tok = (np.arange(NT)[None, :] * P + i[:, None]).astype(f)
    k["tokcol"] = (OOB - tok).astype(f)
    k["gL"] = np.tile(np.concatenate([np.exp(P * lg), np.exp(LB * lg)])[None, :], (P, 1)).astype(f)
    return {n: np.ascontiguousarray(v) for n, v in k.items()}


_OUTS = [(1, SEQ, D), (NB, LB, D), (1, 1, H, DH, DH), (1, 1, H, DH), (1, 1, H), (1, 1, CW - 1, D), (1, 1, H, DH, DH),
         (1, NB, H, DH, DH), (1, NB, H, DH), (1, NB, H), (1, NB, CW - 1, D), (1, NB, H, DH, DH)]


def kernel(**inputs):
    import numpy as np
    import concourse.bacc as bacc
    from concourse.bass_utils import run_bass_kernel_spmd

    nc = bacc.Bacc("TRN2", target_bir_lowering=False, num_devices=1)
    arrays, args, consts = {}, {}, {}
    for name, v in inputs.items():
        v = np.ascontiguousarray(v)
        arrays["in_" + name] = v
        args[name] = nc.dram_tensor("in_" + name, v.shape, mybir.dt.from_np(v.dtype), kind="ExternalInput").ap()
    for name, v in shape_constants().items():
        arrays["k_" + name] = v
        consts[name] = nc.dram_tensor("k_" + name, v.shape, F32, kind="ExternalInput").ap()
    outs = [nc.dram_tensor(f"out_{i}", s, F32, kind="ExternalOutput").ap() for i, s in enumerate(_OUTS)]
    build(nc, args, outs, consts)
    r = run_bass_kernel_spmd(nc, [arrays], core_ids=[0])
    return tuple(r.results[0][f"out_{i}"] for i in range(len(_OUTS)))
```
